# Optimizing a Trainium2 kernel written in Bass

```python
import math
import jax, jax.numpy as jnp
from jax import lax
import numpy as np

'''One inference step of a 1-layer hybrid decoder trunk (Hymba-style parallel head groups).

Layer (pre-RMSNorm, plain residual adds):
  h = rmsnorm(x); one combined input projection -> [q | k | v | u]
    mixer A (8 heads x 64): LongNet dilated sliding-window causal attention, branches
      (window, dilation) = (128,1), (512,4), (2048,16); keys at distances 0, d, 2d, .. <= window,
      gathered by stride; T5 relative-position bias (32 log buckets per head, one table shared by
      all layers); branch outputs merged with weights proportional to their softmax denominators.
    mixer B (4 channel groups x 128): causal multi-scale pooling, trailing mean over 2/4/8/16
      positions (cumulative-sum form) minus the token, per-group linear map, per-channel scale.
  x += W_out [A | B]
  x += cross-attention (4 heads x 256) into 256 memory tokens (keys/values from rmsnorm(mem))
  x += top-4-of-32 clamped-SwiGLU MoE (softmax router with bias over the selected logits)
final RMSNorm.

Inputs: x_prompt (BATCH, SEQ, D_MODEL); x_sample (DEC_BATCH, DEC_SEQ, D_MODEL);
  cache_k_win, cache_v_win (DEPTH, DEC_BATCH, min(WIN_MAX, PAST_LEN), A_HEADS, A_HEAD_DIM),
    rows in chronological order, the last row being position PAST_LEN-1;
  state_pool (DEPTH, DEC_BATCH, POOL_STATE, B_WIDTH): last 15 pooling-mixer input rows;
  cache_mem_k, cache_mem_v (DEPTH, DEC_BATCH, N_MEM, X_HEADS, X_HEAD_DIM);
  mem_prompt (BATCH, N_MEM, D_MODEL); then the weights.
Returns (y_prompt, y_sample, k_win_prompt, v_win_prompt, pool_prompt, mem_k_prompt, mem_v_prompt,
         k_win_sample, v_win_sample, pool_sample):
  y_prompt (BATCH, SEQ, D_MODEL); y_sample (DEC_BATCH, DEC_SEQ, D_MODEL);
  k_win_prompt, v_win_prompt (DEPTH, BATCH, min(WIN_MAX, SEQ), A_HEADS, A_HEAD_DIM);
  pool_prompt (DEPTH, BATCH, POOL_STATE, B_WIDTH);
  mem_k_prompt, mem_v_prompt (DEPTH, BATCH, N_MEM, X_HEADS, X_HEAD_DIM);
  k_win_sample, v_win_sample (DEPTH, DEC_BATCH, min(WIN_MAX, PAST_LEN), A_HEADS, A_HEAD_DIM);
  pool_sample (DEPTH, DEC_BATCH, POOL_STATE, B_WIDTH).
'''

D_MODEL = 1024
BATCH = 1
SEQ = 256
DEPTH = 1
DEC_BATCH = 8
DEC_SEQ = 4
PAST_LEN = 2048
PAGE_SIZE = 128

A_HEADS = 8
A_HEAD_DIM = 64
A_WIDTH = A_HEADS * A_HEAD_DIM
DILATED = ((128, 1), (512, 4), (2048, 16))
WIN_MAX = max(w for w, _ in DILATED)
QB = 128
POOL_WINDOWS = (2, 4, 8, 16)
POOL_GROUPS = len(POOL_WINDOWS)
B_WIDTH = D_MODEL - A_WIDTH
POOL_GROUP_DIM = B_WIDTH // POOL_GROUPS
POOL_STATE = max(POOL_WINDOWS) - 1
MIX_IN = 3 * A_WIDTH + B_WIDTH
MIX_OUT = A_WIDTH + B_WIDTH
N_MEM = 256
X_HEADS = 4
X_HEAD_DIM = D_MODEL // X_HEADS
X_WIDTH = X_HEADS * X_HEAD_DIM
N_EXPERTS = 32
TOP_K = 4
D_FF = D_MODEL
SWIGLU_LIMIT = 7.0
SWIGLU_ALPHA = 1.702
MOE_BLOCK = 128
N_BUCKETS = 32
REL_MAX_DIST = WIN_MAX
RMS_EPS = 1e-6
NEG = -1e30

kernel_name = 'hybrid_dilated_pool_moe_decode_step'

def _rmsnorm(x, g):
    xf = x.astype(jnp.float32)
    y = xf * lax.rsqrt(jnp.mean(xf * xf, axis=-1, keepdims=True) + RMS_EPS)
    return (y * g.astype(jnp.float32)).astype(x.dtype)

def _t5_bucket(n):
    max_exact = N_BUCKETS // 2
    nf = jnp.maximum(n, 1).astype(jnp.float32)
    large = max_exact + (jnp.log(nf / max_exact) / math.log(REL_MAX_DIST / max_exact)
                         * (N_BUCKETS - max_exact)).astype(jnp.int32)
    return jnp.where(n < max_exact, n, jnp.minimum(large, N_BUCKETS - 1))

def _split_mix_proj(h, w_in):
    B, S, _ = h.shape
    p = h @ w_in
    q = p[..., :A_WIDTH].reshape(B, S, A_HEADS, A_HEAD_DIM) * (A_HEAD_DIM ** -0.5)
    k = p[..., A_WIDTH:2 * A_WIDTH].reshape(B, S, A_HEADS, A_HEAD_DIM)
    v = p[..., 2 * A_WIDTH:3 * A_WIDTH].reshape(B, S, A_HEADS, A_HEAD_DIM)
    u = p[..., 3 * A_WIDTH:]
    return q, k, v, u

def _dilated_branch_prompt(q, k, v, window, dil, rel_bias):
    B, S, H, Dh = q.shape
    steps = window // dil
    L = S // dil
    nb = -(-L // QB)
    Lp = nb * QB
    N = B * dil

    def to_sub(a):
        a = a.reshape(B, L, dil, H, Dh).transpose(0, 2, 1, 3, 4).reshape(N, L, H, Dh)
        return jnp.pad(a, ((0, 0), (0, Lp - L), (0, 0), (0, 0)))

    def band(a):
        a = jnp.pad(a, ((0, 0), (QB, 0), (0, 0), (0, 0))).reshape(N, nb + 1, QB, H, Dh)
        return jnp.concatenate([a[:, :-1], a[:, 1:]], axis=2)

    qb = to_sub(q).reshape(N, nb, QB, H, Dh)
    kb = band(to_sub(k))
    vb = band(to_sub(v))
    qi = jnp.arange(QB)[:, None]
    ki = jnp.arange(2 * QB)[None, :]
    j = qi + QB - ki
    in_band = (j >= 0) & (j <= steps)
    bias = rel_bias[_t5_bucket(jnp.clip(j, 0, steps) * dil)].transpose(2, 0, 1)
    u_k = jnp.arange(nb)[:, None] * QB - QB + ki
    mask = in_band[None] & (u_k >= 0)[:, None, :]
    logits = jnp.einsum('nbqhd,nbkhd->nbhqk', qb, kb, preferred_element_type=jnp.float32)
    logits = logits + bias.astype(jnp.float32)[None, None]
    logits = jnp.where(mask[None, :, None], logits, NEG)
    lse = jax.nn.logsumexp(logits, axis=-1)
    p = jnp.exp(logits - lse[..., None])
    o = jnp.einsum('nbhqk,nbkhd->nbqhd', p.astype(v.dtype), vb)
    o = o.reshape(N, Lp, H, Dh)[:, :L].reshape(B, dil, L, H, Dh).transpose(0, 2, 1, 3, 4).reshape(B, S, H, Dh)
    lse = lse.transpose(0, 1, 3, 2).reshape(N, Lp, H)[:, :L].reshape(B, dil, L, H).transpose(0, 2, 1, 3).reshape(B, S, H)
    return o, lse

def _dilated_branch_sample(q, k_all, v_all, window, dil, rel_bias):
    T = q.shape[1]
    n_hist = k_all.shape[1] - T
    steps = window // dil
    s = jnp.arange(steps + 1)
    idx = (n_hist + jnp.arange(T))[:, None] - s[None, :] * dil
    valid = idx >= 0
    idx_c = jnp.maximum(idx, 0)
    kg = k_all[:, idx_c]
    vg = v_all[:, idx_c]
    bias = rel_bias[_t5_bucket(s * dil)].T.astype(jnp.float32)
    logits = jnp.einsum('bthd,btjhd->bhtj', q, kg, preferred_element_type=jnp.float32) + bias[None, :, None, :]
    logits = jnp.where(valid[None, None], logits, NEG)
    lse = jax.nn.logsumexp(logits, axis=-1)
    p = jnp.exp(logits - lse[..., None])
    o = jnp.einsum('bhtj,btjhd->bthd', p.astype(v_all.dtype), vg)
    return o, lse.transpose(0, 2, 1)

def _merge_branches(branches, dtype):
    outs = jnp.stack([o for o, _ in branches], 0).astype(jnp.float32)
    wts = jax.nn.softmax(jnp.stack([l for _, l in branches], 0), axis=0)
    return jnp.einsum('rbsh,rbshd->bshd', wts, outs).astype(dtype)

def _pool_mix(u_ext, n_prev, w_pool, pool_scale):
    B = u_ext.shape[0]
    S = u_ext.shape[1] - n_prev
    u_new = u_ext[:, n_prev:].astype(jnp.float32)
    cs = jnp.cumsum(jnp.pad(u_ext.astype(jnp.float32), ((0, 0), (1, 0), (0, 0))), axis=1)
    end = n_prev + jnp.arange(S) + 1
    outs = []
    for g, w in enumerate(POOL_WINDOWS):
        sl = slice(g * POOL_GROUP_DIM, (g + 1) * POOL_GROUP_DIM)
        lo = jnp.maximum(end - w, 0)
        cnt = jnp.minimum(end, w).astype(jnp.float32)[:, None]
        mean = (cs[:, end, sl] - cs[:, lo, sl]) / cnt
        outs.append(mean - u_new[..., sl])
    d = jnp.stack(outs, axis=2).astype(u_ext.dtype)
    y = jnp.einsum('bsgc,gce->bsge', d, w_pool) * pool_scale.reshape(POOL_GROUPS, POOL_GROUP_DIM)
    return y.reshape(B, S, B_WIDTH)

def _mix_out(o_a, o_b, w_out):
    B, S = o_b.shape[:2]
    return jnp.concatenate([o_a.reshape(B, S, A_WIDTH), o_b.astype(o_a.dtype)], axis=-1) @ w_out

def _mem_kv(mem, g_mem, w_xk, w_xv):
    B, M, _ = mem.shape
    m = _rmsnorm(mem, g_mem)
    return (m @ w_xk).reshape(B, M, X_HEADS, X_HEAD_DIM), (m @ w_xv).reshape(B, M, X_HEADS, X_HEAD_DIM)

def _cross_attn(h, mk, mv, w_xq, w_xo):
    B, S, _ = h.shape
    q = (h @ w_xq).reshape(B, S, X_HEADS, X_HEAD_DIM) * (X_HEAD_DIM ** -0.5)
    logits = jnp.einsum('bshd,bmhd->bhsm', q, mk, preferred_element_type=jnp.float32)
    p = jax.nn.softmax(logits, axis=-1)
    o = jnp.einsum('bhsm,bmhd->bshd', p.astype(mv.dtype), mv)
    return o.reshape(B, S, X_WIDTH) @ w_xo

def _moe(h, w_router, b_router, w_gate_up, b_gate_up, w_down, b_down):
    B, S, D = h.shape
    T = B * S
    x2 = h.reshape(T, D)
    logits = (x2 @ w_router + b_router).astype(jnp.float32)
    top_v, top_i = lax.top_k(logits, TOP_K)
    gates = jax.nn.softmax(top_v, axis=-1)
    e_flat = top_i.reshape(-1).astype(jnp.int32)
    tok_flat = jnp.broadcast_to(jnp.arange(T, dtype=jnp.int32)[:, None], (T, TOP_K)).reshape(-1)
    order = jnp.argsort(e_flat)
    e_s = e_flat[order]
    tok_s = tok_flat[order]
    g_s = gates.reshape(-1)[order]
    counts = jnp.bincount(e_flat, length=N_EXPERTS)
    padded = (counts + MOE_BLOCK - 1) // MOE_BLOCK * MOE_BLOCK
    ends = jnp.cumsum(padded)
    pstart = ends - padded
    start = jnp.cumsum(counts) - counts
    n_slots = T * TOP_K
    ppos = pstart[e_s] + jnp.arange(n_slots) - start[e_s]
    n_blocks = (n_slots + N_EXPERTS * (MOE_BLOCK - 1) + MOE_BLOCK - 1) // MOE_BLOCK
    slot_tok = jnp.full((n_blocks * MOE_BLOCK,), T, jnp.int32).at[ppos].set(tok_s)
    block_e = jnp.minimum(jnp.searchsorted(ends, jnp.arange(n_blocks) * MOE_BLOCK, side='right'), N_EXPERTS - 1)
    x_pad = jnp.concatenate([x2, jnp.zeros((1, D), x2.dtype)], axis=0)

    def expert_block(args):
        tok_b, e = args
        xb = x_pad[tok_b]
        hu = xb @ w_gate_up[e] + b_gate_up[e]
        g = jnp.minimum(hu[:, :D_FF], SWIGLU_LIMIT)
        u = jnp.clip(hu[:, D_FF:], -SWIGLU_LIMIT, SWIGLU_LIMIT)
        a = g * jax.nn.sigmoid(SWIGLU_ALPHA * g) * (u + 1)
        return a @ w_down[e] + b_down[e]

    out = lax.map(expert_block, (slot_tok.reshape(n_blocks, MOE_BLOCK), block_e))
    y_s = out.reshape(-1, D)[ppos] * g_s[:, None].astype(out.dtype)
    return jax.ops.segment_sum(y_s, tok_s, num_segments=T).reshape(B, S, D)

def setup_inputs(seed: int = 0) -> dict:
    key = jax.random.key(seed)
    ks = iter(jax.random.split(key, 32))

    def nrm(shape, scale=1.0):
        return jax.random.normal(next(ks), shape, jnp.float32) * scale

    def gain(shape):
        return 1.0 + nrm(shape, 0.05)

    lb = min(WIN_MAX, PAST_LEN)
    return {
        'x_prompt': nrm((BATCH, SEQ, D_MODEL)),
        'x_sample': nrm((DEC_BATCH, DEC_SEQ, D_MODEL)),
        'cache_k_win': nrm((DEPTH, DEC_BATCH, lb, A_HEADS, A_HEAD_DIM)),
        'cache_v_win': nrm((DEPTH, DEC_BATCH, lb, A_HEADS, A_HEAD_DIM)),
        'state_pool': nrm((DEPTH, DEC_BATCH, POOL_STATE, B_WIDTH)),
        'cache_mem_k': nrm((DEPTH, DEC_BATCH, N_MEM, X_HEADS, X_HEAD_DIM)),
        'cache_mem_v': nrm((DEPTH, DEC_BATCH, N_MEM, X_HEADS, X_HEAD_DIM)),
        'mem_prompt': nrm((BATCH, N_MEM, D_MODEL)),
        'rel_bias': nrm((N_BUCKETS, A_HEADS), 0.5),
        'g_mix': gain((DEPTH, D_MODEL)),
        'w_in': nrm((DEPTH, D_MODEL, MIX_IN), D_MODEL ** -0.5),
        'w_pool': nrm((DEPTH, POOL_GROUPS, POOL_GROUP_DIM, POOL_GROUP_DIM), POOL_GROUP_DIM ** -0.5),
        'pool_scale': gain((DEPTH, B_WIDTH)),
        'w_out': nrm((DEPTH, MIX_OUT, D_MODEL), MIX_OUT ** -0.5),
        'g_mem': gain((DEPTH, D_MODEL)),
        'g_x': gain((DEPTH, D_MODEL)),
        'w_xq': nrm((DEPTH, D_MODEL, X_WIDTH), D_MODEL ** -0.5),
        'w_xk': nrm((DEPTH, D_MODEL, X_WIDTH), D_MODEL ** -0.5),
        'w_xv': nrm((DEPTH, D_MODEL, X_WIDTH), D_MODEL ** -0.5),
        'w_xo': nrm((DEPTH, X_WIDTH, D_MODEL), X_WIDTH ** -0.5),
        'g_ff': gain((DEPTH, D_MODEL)),
        'w_router': nrm((DEPTH, D_MODEL, N_EXPERTS), D_MODEL ** -0.5),
        'b_router': nrm((DEPTH, N_EXPERTS), 0.01),
        'w_gate_up': nrm((DEPTH, N_EXPERTS, D_MODEL, 2 * D_FF), D_MODEL ** -0.5),
        'b_gate_up': nrm((DEPTH, N_EXPERTS, 2 * D_FF), 0.01),
        'w_down': nrm((DEPTH, N_EXPERTS, D_FF, D_MODEL), D_FF ** -0.5),
        'b_down': nrm((DEPTH, N_EXPERTS, D_MODEL), 0.01),
        'g_final': gain((D_MODEL,)),
    }

def reference(x_prompt, x_sample, cache_k_win, cache_v_win, state_pool, cache_mem_k, cache_mem_v, mem_prompt,
              rel_bias, g_mix, w_in, w_pool, pool_scale, w_out, g_mem, g_x, w_xq, w_xk, w_xv, w_xo, g_ff,
              w_router, b_router, w_gate_up, b_gate_up, w_down, b_down, g_final):
    xp, xs = x_prompt, x_sample
    kw_p, vw_p, pool_p, mk_p, mv_p = [], [], [], [], []
    kw_s, vw_s, pool_s = [], [], []
    for l in range(DEPTH):
        moe_w = (w_router[l], b_router[l], w_gate_up[l], b_gate_up[l], w_down[l], b_down[l])
        q, k, v, u = _split_mix_proj(_rmsnorm(xp, g_mix[l]), w_in[l])
        o_a = _merge_branches([_dilated_branch_prompt(q, k, v, w, d, rel_bias) for (w, d) in DILATED], xp.dtype)
        o_b = _pool_mix(u, 0, w_pool[l], pool_scale[l])
        xp = xp + _mix_out(o_a, o_b, w_out[l])
        mk, mv = _mem_kv(mem_prompt, g_mem[l], w_xk[l], w_xv[l])
        xp = xp + _cross_attn(_rmsnorm(xp, g_x[l]), mk, mv, w_xq[l], w_xo[l])
        xp = xp + _moe(_rmsnorm(xp, g_ff[l]), *moe_w)
        n_keep = min(WIN_MAX, k.shape[1])
        kw_p.append(k[:, k.shape[1] - n_keep:])
        vw_p.append(v[:, v.shape[1] - n_keep:])
        pool_p.append(u[:, u.shape[1] - POOL_STATE:])
        mk_p.append(mk)
        mv_p.append(mv)
        q, k, v, u = _split_mix_proj(_rmsnorm(xs, g_mix[l]), w_in[l])
        k_all = jnp.concatenate([cache_k_win[l].astype(k.dtype), k], axis=1)
        v_all = jnp.concatenate([cache_v_win[l].astype(v.dtype), v], axis=1)
        o_a = _merge_branches([_dilated_branch_sample(q, k_all, v_all, w, d, rel_bias) for (w, d) in DILATED], xs.dtype)
        u_all = jnp.concatenate([state_pool[l].astype(u.dtype), u], axis=1)
        o_b = _pool_mix(u_all, POOL_STATE, w_pool[l], pool_scale[l])
        xs = xs + _mix_out(o_a, o_b, w_out[l])
        xs = xs + _cross_attn(_rmsnorm(xs, g_x[l]), cache_mem_k[l], cache_mem_v[l], w_xq[l], w_xo[l])
        xs = xs + _moe(_rmsnorm(xs, g_ff[l]), *moe_w)
        n_new = k.shape[1]
        kw_s.append(k_all[:, n_new:])
        vw_s.append(v_all[:, n_new:])
        pool_s.append(u_all[:, n_new:])
    y_prompt = _rmsnorm(xp, g_final)
    y_sample = _rmsnorm(xs, g_final)
    k_win_prompt = jnp.stack(kw_p)
    v_win_prompt = jnp.stack(vw_p)
    pool_prompt = jnp.stack(pool_p)
    mem_k_prompt = jnp.stack(mk_p)
    mem_v_prompt = jnp.stack(mv_p)
    k_win_sample = jnp.stack(kw_s)
    v_win_sample = jnp.stack(vw_s)
    pool_sample = jnp.stack(pool_s)
    return (y_prompt, y_sample, k_win_prompt, v_win_prompt, pool_prompt, mem_k_prompt, mem_v_prompt, k_win_sample, v_win_sample, pool_sample)


_drawn_inputs = setup_inputs


def setup_inputs(seed=0):
    import zlib

    import numpy as np

    out = dict(_drawn_inputs(seed))
    spreads = {}
    factors = {'g_x': 3.142, 'b_gate_up': 8.0, 'b_down': 8.0}
    for name, (base, spread) in spreads.items():
        noise = np.random.default_rng([zlib.crc32(name.encode()), seed]).standard_normal(out[name].shape)
        drawn = base * np.exp(spread * noise) if base else spread * noise
        out[name] = __import__('jax').numpy.asarray(drawn.astype(out[name].dtype))
    for name, factor in factors.items():
        out[name] = (out[name] * factor).astype(out[name].dtype)
    return out
```

```python
import math
from contextlib import ExitStack

import concourse.bass as bass
import numpy as np
from concourse import mybir

P = 128
D = 1024
KC = D // P
SEQ, DEC_B, DEC_T = 256, 8, 4
NS = DEC_B * DEC_T
T = SEQ + NS
TOK = [(0, P), (P, P), (SEQ, NS)]
PAST = 2048
HEADS, HD = 8, 64
AW = HEADS * HD
NMEM, XH, XHD = 256, 4, 256
POOLW = (2, 4, 8, 16)
STATE = max(POOLW) - 1
EXPERTS, TOPK = 32, 4
CAP = 64
ROUNDS = -(-T // CAP)
STEPS = EXPERTS * ROUNDS
NTAB = STEPS + 2
FAR = float(2 ** 20)
NEG = -1e30
EPS = 1e-6
BUCKETS = 32
TOEP = 384


def buckets(dist):
    half = BUCKETS // 2
    n = np.maximum(dist, 1).astype(np.float32)
    large = half + (np.log(n / np.float32(half)) / np.float32(math.log(PAST / half))
                    * np.float32(BUCKETS - half)).astype(np.int32)
    return np.where(dist < half, dist, np.minimum(large, BUCKETS - 1))


def bias_rows(dist, add):
    d = np.asarray(dist)
    out = np.zeros((BUCKETS + 1, d.size), np.float32)
    out[buckets(np.clip(d, 0, PAST)), np.arange(d.size)] = 1.0
    out[BUCKETS] = add
    return out


def constants():
    dist = 255 - np.arange(TOEP)
    count = (dist <= 128).astype(int) + (dist % 4 == 0) + (dist % 16 == 0)
    ok = (dist >= 0) & (count > 0)
    toep = bias_rows(dist, np.where(ok, np.log(np.maximum(count, 1)), NEG))
    p = np.arange(P)
    window = [bias_rows(512 - 4 * p, 0.0), bias_rows(2048 - 16 * p, 0.0)]
    window += [bias_rows(128 + t - p, np.where(p >= t, 0.0, NEG)) for t in range(DEC_T)]
    key_t = np.arange(NS) % DEC_T
    fresh = [bias_rows(t - key_t, 0.0) for t in range(DEC_T)]
    kb, kt = np.arange(NS)[:, None] // DEC_T, np.arange(NS)[:, None] % DEC_T
    qb, qt = np.arange(NS)[None, :] // DEC_T, np.arange(NS)[None, :] % DEC_T
    fresh_mask = np.where((kb == qb) & (kt <= qt), np.where(kt == qt, math.log(3.0), 0.0), NEG)
    first = np.array([[1.0 / min(i + 1, w) for i in range(16)] for w in POOLW])
    n = np.arange(NTAB)
    return {
        "c_bias": np.concatenate([toep] + window + fresh, 1).astype(np.float32),
        "c_fresh": fresh_mask.astype(np.float32),
        "c_first": np.tile(first.reshape(1, 64), (P, 1)).astype(np.float32),
        "c_ident": np.eye(P, dtype=np.float32),
        "c_before": (p[:, None] < p[None, :]).astype(np.float32),
        "c_iota": np.tile(np.arange(CAP, dtype=np.float32), (P, 1)),
        "c_expert": (np.arange(96)[:, None] % 32 == n[None, :] % 32).astype(np.float32),
    }


def build(nc, i, o):
    f32, bf16, u32, i32 = mybir.dt.float32, mybir.dt.bfloat16, mybir.dt.uint32, mybir.dt.int32
    ALU, ACT, AX = mybir.AluOpType, mybir.ActivationFunctionType, mybir.AxisListType
    ds = bass.ds
    ctx = ExitStack()
    with ctx:
        def sb(name, shape, dt=f32):
            return ctx.enter_context(nc.sbuf_tensor(name, shape, dt))

        def sem(name):
            return ctx.enter_context(nc.semaphore(name))

        toep_dram = nc.dram_tensor("toep_dram", (P, HEADS, TOEP), f32, kind="Internal").ap()
        y_dram = nc.dram_tensor("y_dram", (STEPS * CAP, D), f32, kind="Internal").ap()

        wide = sb("wide", [P, KC, 2 * D])
        slim = sb("slim", [P, KC, D])
        x = sb("x", [P, 3, D])
        hn = sb("hn", [P, 3, D])
        ta = sb("ta", [P, KC, T])
        tb = sb("tb", [P, KC, T])
        mkT = sb("mkT", [P, KC, NMEM])
        mv = sb("mv", [P, 2, D])
        att = sb("att", [P, 10112])
        scr = sb("scr", [P, 2048])
        ident = sb("ident", [P, P])
        iota = sb("iota", [P, CAP])
        ones = sb("ones", [P, P])
        gcol = sb("gcol", [P, 4, KC])
        small = sb("small", [P, 512])
        eps = sb("eps", [P, 1])
        idx = sb("idx", [P, 3, 8], u32)
        rows = sb("rows", [P, 3, TOPK], u32)
        most = sb("most", [1, 1], i32)

        wf = wide[:, :, :].rearrange("p k n -> p (k n)")
        kwin = [wf[:, 4608 * s:4608 * s + 4608].rearrange("p (s n) -> p s n", n=AW) for s in range(2)]
        vwin = wf[:, 9216:13824].rearrange("p (s n) -> p s n", n=AW)
        prod = wf[:, 13824:15360].rearrange("p (s n) -> p s n", n=AW)
        cmem = [wf[:, 2048 * s:2048 * s + 2048].rearrange("p (m n) -> p m n", n=D) for s in range(8)]
        qn = att[:, 0:1536].rearrange("p (t n) -> p t n", n=AW)
        kn = att[:, 1536:3072].rearrange("p (t n) -> p t n", n=AW)
        vn = att[:, 3072:4608].rearrange("p (t n) -> p t n", n=AW)
        qkvn = att[:, 0:4608].rearrange("p (c t n) -> p c t n", c=3, n=AW)
        toep_sb = att[:, 0:3072].rearrange("p (h n) -> p h n", n=TOEP)
        qT = att[:, 4608:5760].rearrange("p (c n) -> p c n", n=T)
        kT = att[:, 5760:6912].rearrange("p (c n) -> p c n", n=T)
        UP = STATE + SEQ
        uP = att[:, 6912:6912 + 4 * UP].rearrange("p (g n) -> p g n", n=UP)
        bias = att[:, 8000:10048].rearrange("p (h n) -> p h n", n=SEQ)
        mvf = mv[:, :, :].rearrange("p t n -> p (t n)")
        dT = mvf[:, 0:1152].rearrange("p (g n) -> p g n", n=T)
        US = STATE + DEC_T
        uS = mvf[:, 1152:1152 + 4 * DEC_B * US].rearrange("p (g b n) -> p g b n", b=DEC_B, n=US)
        unew = mvf[:, 1760:1888].rearrange("p (g n) -> p g n", n=NS)
        mkTf = mkT[:, :, :].rearrange("p k n -> p (k n)")
        cb = mkTf[0:33, 0:TOEP + 10 * P]
        rb = mkTf[0:33, 1300:1308]
        wr = mkTf[:, 0:256].rearrange("p (k n) -> p k n", n=EXPERTS)
        before = mkTf[:, 256:384]
        rbrep = scr[0:33, 0:1024].rearrange("p (h n) -> p h n", n=P)
        state = scr[0:DEC_B * STATE, 1024:1536]
        wpool = scr[:, 1536:2048].rearrange("p (g n) -> p g n", n=P)
        sum_p = [scr[:, 0:UP], scr[:, UP:2 * UP]]
        sum_s = [scr[:, 600 + 152 * s:600 + 152 * s + 152].rearrange("p (b n) -> p b n", n=US) for s in range(2)]
        lg = [scr[:, 512 * s:512 * s + 512].rearrange("p (h n) -> p h n", n=NMEM) for s in range(2)]
        pT = [scr[:, 1024 + 512 * s:1536 + 512 * s].rearrange("p (c n) -> p c n", n=P) for s in range(2)]
        S_ = [small[:, 128 * s:128 * s + 96].rearrange("p (k t h) -> p k t h", k=3, t=DEC_T) for s in range(2)]
        bs = att[:, 10048:10048 + 64]
        bsw = sb("bsw", [P, 3, DEC_T, HEADS])
        bfr = sb("bfr", [NS, DEC_B, DEC_T, HEADS])
        pp = sb("pp", [P, 4, DEC_T, HEADS])
        pr = sb("pr", [P, 4, DEC_T, HEADS])
        fmask = sb("fmask", [NS, NS])
        cfirst = bs.rearrange("p (g n) -> p g n", n=16)
        pscale = sb("pscale", [P, 4])
        mx = small[:, 256:288]
        gm = small[:, 288:320]
        zs = small[:, 320:352]
        zz = small[:, 352:384]
        stat = small[:, 384:512]

        ktm = [att[:, 2048 * s:2048 * s + 2048].rearrange("p (k n) -> p k n", n=NMEM) for s in range(2)]
        sx = att[:, 4608:4864].rearrange("p (b m c) -> p b m c", m=2, c=16)
        px = att[:, 4864:5120].rearrange("p (b m c) -> p b m c", m=2, c=16)
        mxx, gmx = att[:, 5120:5248], att[:, 5248:5376]
        zsx, zzx = att[:, 5376:5504], att[:, 5504:5632]
        logit = att[:, 4096:4192].rearrange("p (t n) -> p t n", n=EXPERTS)
        top = att[:, 4192:4216].rearrange("p (t n) -> p t n", n=8)
        idxf = att[:, 4216:4240].rearrange("p (t n) -> p t n", n=8)
        gate = sb("gate", [P, 3, TOPK])
        hot = att[:, 4240:4624].rearrange("p (t k n) -> p t k n", k=TOPK, n=EXPERTS)
        msk = att[:, 4624:4720].rearrange("p (t n) -> p t n", n=EXPERTS)
        gmat = att[:, 4720:4816].rearrange("p (t n) -> p t n", n=EXPERTS)
        posn = att[:, 4816:4912].rearrange("p (t n) -> p t n", n=EXPERTS)
        prodr = att[:, 4912:5296].rearrange("p (t k n) -> p t k n", k=TOPK, n=EXPERTS)
        slot = att[:, 5296:5308].rearrange("p (t n) -> p t n", n=TOPK)
        jump = att[:, 5308:5320].rearrange("p (t n) -> p t n", n=TOPK)
        rowf = att[:, 5320:5332].rearrange("p (t n) -> p t n", n=TOPK)
        gT = att[0:EXPERTS, 5336:5336 + T]
        brow = att[0:1, 5632:5664]
        cntf = att[0:1, 5664:5665]
        table = att[:, 5760:5760 + 3 * NTAB].rearrange("p (t n) -> p t n", n=NTAB)
        expert1 = att[0:96, 6260:6260 + NTAB]
        parts = att[0:96, 6912:7936].bitcast(bf16)
        braw = att[0:96, 8000:10048]
        bdn = scr[0:EXPERTS, 0:D]
        xe = att[:, 0:512].rearrange("p (k n) -> p k n", n=CAP)
        gc, uc, gu, sg = (att[:, 512 * s:512 * s + 512] for s in (1, 2, 3, 4))
        aT = att[:, 2560:3072].rearrange("p (j h n) -> p j h n", j=4, h=2)
        ye = att[:, 3072:3584]
        onehot = att[:, 3584:3776].rearrange("p (t n) -> p t n", n=CAP)
        pick = att[0:96, 3776:3808].bitcast(bf16)
        yk = [wf[:, D * s:D * s + D] for s in range(12)]
        gfin = wf[:, 12 * D:13 * D]
        xout = [wf[:, (13 + t) * D:(14 + t) * D] for t in range(3)]

        bank = [ctx.enter_context(nc.psum_tensor(f"bank{b}", [P, 512], f32)) for b in range(8)]

        jobs = []

        def add(*name):
            jobs.append(name)

        add("bias_w"), add("bias_f")
        for h in range(HEADS):
            add("toep", h)
        for t in range(3):
            for h in range(2):
                add("tr1", t, h)
        for t in range(3):
            for c in range(3):
                add("qkv", t, c)
        for c in range(4):
            add("u", c)
        for t in range(3):
            add("trq", t), add("trk", t)
        add("fresh", 0), add("fresh", 1)
        add("state"), add("utp"), add("uts")
        for g in range(4):
            add("pool", g)
        UNITS = [(hp, qt) for hp in range(4) for qt in range(2)]
        add("s", 0, 0), add("s", 0, 1)
        for u in range(8):
            if u + 1 < 8:
                add("s", u + 1, 0), add("s", u + 1, 1)
            add("pt", u), add("o", u)
        FILL = {0: [("trm", 0, 0), ("trm", 0, 1), ("trm", 1, 0), ("trm", 1, 1)],
                1: [("mk", 0, 0), ("mk", 0, 1)], 2: [("mk", 1, 0), ("mk", 1, 1)],
                3: [("trmk", 0, 0), ("trmk", 0, 1), ("trmk", 1, 0), ("trmk", 1, 1)],
                4: [("mv", 0, 0), ("mv", 0, 1)], 5: [("mv", 1, 0), ("mv", 1, 1)]}
        for b in range(DEC_B):
            for t in range(DEC_T):
                add("qb", b, t)
            if b:
                add("pv", b - 1)
            for f in FILL.get(b, []):
                add(*f)
        add("pv", DEC_B - 1)
        for t in range(3):
            add("out", t, 0), add("out", t, 1)
        for t in range(3):
            add("tr2", t, 0), add("tr2", t, 1)
        for c in range(8):
            add("xq", c)
        for b in range(DEC_B):
            for m in range(2):
                add("trck", b, m, 0), add("trck", b, m, 1)
            if b:
                add("sx", b - 1)
        add("sx", DEC_B - 1)
        XUNITS = [(hp, qt) for hp in range(2) for qt in range(2)]
        add("xs", 0)
        for u in range(4):
            if u + 1 < 4:
                add("xs", u + 1)
            add("xpt", u), add("xo_", u)
        add("pvx")
        for t in range(3):
            add("xo", t, 0), add("xo", t, 1)
        for t in range(3):
            add("tr3", t, 0), add("tr3", t, 1)
        for t in range(3):
            add("route", t)
        for t in range(3):
            add("pos", t)
        add("count"), add("trg")
        for t in range(3):
            add("bd", t, 0), add("bd", t, 1)
        number = {name: n for n, name in enumerate(jobs)}
        assert len(number) == len(jobs)

        bank_full = [sem(f"bank_full{b}") for b in range(8)]
        bank_free = [sem(f"bank_free{b}") for b in range(8)]

        def place(name):
            n = number[name]
            return n % 8, n // 8

        def take(pe, *name):
            b, use = place(name)
            if use:
                pe.wait_ge(bank_free[b], use)
            return bank[b], bank_full[b]

        def product(eng, *name):
            b, use = place(name)
            eng.wait_ge(bank_full[b], use + 1)
            return bank[b], bank_free[b]

        def read_out(eng, *name):
            b, use = place(name)
            eng.wait_ge(bank_free[b], use + 1)

        loaded = {}

        def load(eng, name, out, in_):
            eng.dma_start(out, in_).then_inc(loaded[name], 16)

        for n in ("x0", "x1", "x2", "rel", "cbias", "cfresh", "cfirst", "ident", "before", "iota", "gcol", "wr",
                  "state", "wpool", "pscale", "toep", "mem", "expert", "braw0", "braw1", "braw2", "brow", "bdn",
                  "gfin"):
            loaded[n] = sem(f"loaded_{n}")
        wide_in = [sem(f"wide_in{k}") for k in range(KC)]
        slim_in = [sem(f"slim_in{k}") for k in range(KC)]
        wide_used = sem("wide_used")
        slim_used = sem("slim_used")
        k_in = [sem("k_in0"), sem("k_in1")]
        v_in = sem("v_in")
        ck_in = [sem(f"ck_in{s}") for s in range(4)]
        cv_in = [sem(f"cv_in{s}") for s in range(8)]
        toep_out = sem("toep_out")
        consts = sem("consts")
        squares = sem("squares")
        normed = sem("normed")
        rb_rep = sem("rb_rep")
        fresh_in = sem("fresh_in")
        pooled = sem("pooled")
        summed = sem("summed")
        expd = sem("expd")
        scaled = sem("scaled")
        pt_in = sem("pt_in")
        scored = sem("scored")
        gmax = sem("gmax")
        shifted = sem("shifted")
        sexp = sem("sexp")
        zpart = sem("zpart")
        zall = sem("zall")
        prob = sem("prob")
        xscored, xgmax, xshift, xexp, xzpart, xzall, xprob = (sem(n) for n in (
            "xscored", "xgmax", "xshift", "xexp", "xzpart", "xzall", "xprob"))
        parts_in = sem("parts_in")
        gexp = sem("gexp")
        gz = sem("gz")
        toph = sem("toph")
        hots = sem("hots")
        gmats = sem("gmats")
        tables = sem("tables")
        most_in = sem("most_in")
        stored = {n: sem(f"stored_{n}") for n in ("copies", "kv", "pool", "mk", "mv", "y")}
        dve_done = sem("dve_done")
        act_done = sem("act_done")
        pool_done = sem("pool_done")
        onehot_in, pick_in, xe_in, xg_full, gc_in, uc_in, gu_in, sg_in, a_in, at_full, at_in, y_read, y_stored = (
            sem(n) for n in ("onehot_in", "pick_in", "xe_in", "xg_full", "gc_in", "uc_in", "gu_in", "sg_in", "a_in", "at_full",
                             "at_in", "y_read", "y_stored"))
        gathered = [sem(f"gathered{n}") for n in range(3)]
        xsum = sem("xsum")
        fin = sem("fin")
        bank_g, bank_u, bank_t, bank_x, bank_y = bank[0], bank[1], bank[2], bank[3], bank[4]
        LAST = [place(n) for n in [("bd", t, h) for t in range(3) for h in range(2)]]

        def swap(ap):
            return ap.rearrange("p a b -> p b a")

        w_in = i["w_in"][0].rearrange("(k p) n -> k p n", p=P)

        def wch(name):
            return i[name][0].rearrange("(k p) n -> k p n", p=P)

        SLIM = ["w_xk", "w_xv", "w_out", "w_xq", "w_xo"]
        SLIM_LAST = [("mk", 1, 1), ("mv", 1, 1), ("out", 2, 1), ("xq", 7), None]

        block = ctx.enter_context(nc.Block())

        @block.sync
        def _(sp):
            load(sp, "ident", ident[:, :], i["c_ident"])
            for t, (t0, n) in enumerate(TOK):
                src = i["x_prompt"][0, t0:t0 + n, :] if t < 2 else i["x_sample"].rearrange("b t d -> (b t) d")
                load(sp, f"x{t}", x[0:n, t, :], src)
            load(sp, "rel", rb[0:BUCKETS, :], i["rel_bias"])
            load(sp, "cbias", cb[:, 0:TOEP + 6 * P + 4 * NS], i["c_bias"])
            load(sp, "cfresh", fmask[:, :], i["c_fresh"])
            load(sp, "gcol", gcol[:, :, :], i["g_all"])
            for k in range(KC):
                sp.dma_start(wide[:, k, :], w_in[k]).then_inc(wide_in[k], 16)
            load(sp, "cfirst", bs, i["c_first"])
            load(sp, "state", state, i["state_pool"][0].rearrange("b s d -> (b s) d"))
            load(sp, "wpool", wpool, i["w_pool"][0].rearrange("g c e -> c g e"))
            load(sp, "pscale", pscale[:, :], i["pool_scale_col"])
            load(sp, "iota", iota[:, :], i["c_iota"])

            def slim_round(r):
                if r:
                    b, use = place(SLIM_LAST[r - 1])
                    sp.wait_ge(bank_full[b], use + 1)
                src = wch(SLIM[r])
                for k in range(KC):
                    sp.dma_start(slim[:, k, :], src[k]).then_inc(slim_in[k], 16)

            slim_round(0)
            sp.wait_ge(toep_out, 16)
            skew = bass.AP(toep_dram.tensor, P - 1, [[HEADS * TOEP - 1, P], [TOEP, HEADS], [1, SEQ]])
            load(sp, "toep", bias, skew)
            b, use = place(("tr1", 2, 1))
            sp.wait_ge(bank_full[b], use + 1)
            load(sp, "mem", hn[:, 0:2, :], i["mem_prompt"][0].rearrange("(t p) d -> p t d", p=P))

            def window(dst, cache, b, s):
                src = cache[0, b]
                sp.dma_start(dst[:, 0:4, :], src[PAST - 512:PAST].rearrange("(p t) h d -> p t (h d)", p=P)).then_inc(s, 16)
                sp.dma_start(dst[:, 4:8, :], src.rearrange("(p t) h d -> p t (h d)", p=P)[:, 0:4, :]).then_inc(s, 16)
                sp.dma_start(dst[:, 8, :], src[PAST - P:PAST].rearrange("p h d -> p (h d)")).then_inc(s, 16)

            b, use = place(("u", 3))
            sp.wait_ge(bank_full[b], use + 1)
            window(kwin[0], i["cache_k_win"], 0, k_in[0])
            window(vwin, i["cache_v_win"], 0, v_in)
            window(kwin[1], i["cache_k_win"], 1, k_in[1])
            for b in range(1, DEC_B):
                if b + 1 < DEC_B:
                    sp.wait_ge(scored, b)
                    window(kwin[(b + 1) % 2], i["cache_k_win"], b + 1, k_in[(b + 1) % 2])
                bb, use = place(("pv", b - 1))
                sp.wait_ge(bank_full[bb], use + 1)
                window(vwin, i["cache_v_win"], b, v_in)
                if b == 3:
                    slim_round(1)
                if b == 6:
                    slim_round(2)
            bb, use = place(("pv", DEC_B - 1))
            sp.wait_ge(bank_full[bb], use + 1)
            sp.wait_ge(scored, DEC_B)

            def cache_mem(dst, name, b, s):
                sp.dma_start(dst, i[name][0, b].rearrange("(m p) h d -> p m (h d)", p=P)).then_inc(s, 16)

            for b in range(4):
                cache_mem(cmem[b], "cache_mem_k", b, ck_in[b])
            for b in range(4):
                cache_mem(cmem[4 + b], "cache_mem_v", b, cv_in[b])
            slim_round(3)
            for b in range(4, DEC_B):
                bb, use = place(("trck", b - 4, 1, 1))
                sp.wait_ge(bank_full[bb], use + 1)
                cache_mem(cmem[b - 4], "cache_mem_k", b, ck_in[b - 4])
            for b in range(4, DEC_B):
                bb, use = place(("trck", b, 1, 1))
                sp.wait_ge(bank_full[bb], use + 1)
                cache_mem(cmem[b - 4], "cache_mem_v", b, cv_in[b])
            slim_round(4)
            for s in range(3):
                load(sp, f"braw{s}", braw[32 * s:32 * s + 32, :], i["b_gate_up"][0])
            read_out(sp, "xpt", 3)
            b, use = place(("xo_", 3))
            sp.wait_ge(bank_full[b], use + 1)
            load(sp, "bdn", bdn, i["b_down"][0])
            load(sp, "before", before, i["c_before"])
            load(sp, "wr", wr, i["w_router"][0].rearrange("(k p) n -> p k n", p=P))
            sp.wait_ge(xprob, 1)
            b, use = place(("pvx",))
            sp.wait_ge(bank_full[b], use + 1)
            load(sp, "brow", brow, i["b_router"])
            load(sp, "expert", expert1, i["c_expert"])

            def step(e, n):
                for k in range(KC):
                    sp.wait_ge(wide_used, 8 * n + k + 1)
                    sp.dma_start(wide[:, k, :], i["w_gate_up"][0, ds(e, 1), k * P:(k + 1) * P, :]
                                 .rearrange("e p n -> p (e n)")).then_inc(wide_in[k], 16)
                for k in range(KC):
                    sp.wait_ge(slim_used, 8 * n + k + 1)
                    sp.dma_start(slim[:, k, :], i["w_down"][0, ds(e, 1), k * P:(k + 1) * P, :]
                                 .rearrange("e p n -> p (e n)")).then_inc(slim_in[k], 16)

            with sp.Fori(0, EXPERTS) as e:
                step(e, e)
            sp.wait_ge(most_in, 1)
            crowd = sp.value_load(most[0:1, 0:1], min_val=0, max_val=T)
            with sp.If(crowd > CAP):
                with sp.Fori(1, ROUNDS) as j:
                    with sp.Fori(0, EXPERTS) as e:
                        step(e, j * EXPERTS + e)
            sp.wait_ge(wide_used, 8 * EXPERTS + 8)
            with sp.If(crowd > CAP):
                sp.wait_ge(wide_used, 8 * STEPS + 8)
            load(sp, "gfin", gfin, i["g_final_rows"])
            for t in range(3):
                n = TOK[t][1]
                sp.wait_ge(fin, t + 1)
                dst = o["y_prompt"][0, TOK[t][0]:TOK[t][0] + n, :] if t < 2 else o["y_sample"].rearrange("b t d -> (b t) d")
                sp.dma_start(dst, xout[t][0:n, :]).then_inc(stored["y"], 16)
            sp.wait_ge(stored["y"], 48)

        @block.gpsimd
        def _(pool):
            step = [0]

            def link(ins):
                step[0] += 1
                ins.then_inc(pool_done, 1)
                pool.wait_ge(pool_done, step[0])

            KEEP = PAST - DEC_T
            copies = []
            for b in range(DEC_B):
                for src, dst in (("cache_k_win", "k_win_sample"), ("cache_v_win", "v_win_sample")):
                    copies.append((o[dst][0, b, 0:KEEP].rearrange("s h d -> (s h d)").rearrange("(a n) -> a n", a=64),
                                   i[src][0, b, DEC_T:PAST].rearrange("s h d -> (s h d)").rearrange("(a n) -> a n", a=64)))

            def copy(n):
                for _ in range(n):
                    d, s = copies.pop(0)
                    pool.dma_start(d, s).then_inc(stored["copies"], 16)

            nc.gpsimd.memset(ones[:, :], 1.0).then_inc(consts, 1)
            pool.dma_start(o["pool_sample"][0, :, 0:STATE - DEC_T, :], i["state_pool"][0, :, DEC_T:STATE, :]).then_inc(stored["copies"], 16)
            read_out(pool, "toep", HEADS - 1)
            read_out(pool, "toep", HEADS - 2)
            pool.dma_start(toep_dram, toep_sb).then_inc(toep_out, 16)
            copy(4)
            for c, (kp, ks) in ((1, ("k_win_prompt", "k_win_sample")), (2, ("v_win_prompt", "v_win_sample"))):
                for t in range(3):
                    read_out(pool, "qkv", t, c)
                pool.dma_start(o[kp][0, 0].rearrange("(t p) h d -> p t (h d)", p=P), qkvn[:, c, 0:2, :]).then_inc(stored["kv"], 16)
                pool.dma_start(o[ks][0, :, KEEP:PAST].rearrange("b t h d -> b t (h d)"),
                               qkvn[0:NS, c, 2, :]).then_inc(stored["kv"], 16)
            read_out(pool, "utp")
            pool.dma_start(o["pool_prompt"][0, 0], hn[0:STATE, 2, 0:512]).then_inc(stored["pool"], 16)
            read_out(pool, "uts")
            pool.dma_start(o["pool_sample"][0, :, STATE - DEC_T:STATE, :], hn[0:NS, 2, 512:1024]).then_inc(stored["pool"], 16)
            copy(2)
            for b in range(DEC_B):
                pool.wait_ge(scored, b + 1)
                nc.gpsimd.partition_all_reduce(gm, mx, P, bass.bass_isa.ReduceOp.max).then_inc(gmax, 1)
                pool.wait_ge(zpart, b + 1)
                nc.gpsimd.partition_all_reduce(zz, zs, P, bass.bass_isa.ReduceOp.add).then_inc(zall, 1)
                if b in (3, 4):
                    if b == 3:
                        for t in range(2):
                            for h in range(2):
                                read_out(pool, "mk", t, h)
                        pool.dma_start(o["mem_k_prompt"][0, 0].rearrange("(t p) h d -> p t (h d)", p=P),
                                       hn[:, 0:2, :]).then_inc(stored["mk"], 16)
                if b % 2:
                    copy(1)
            for t in range(2):
                for h in range(2):
                    read_out(pool, "mv", t, h)
            pool.dma_start(o["mem_v_prompt"][0, 0].rearrange("(t p) h d -> p t (h d)", p=P), mv[:, :, :]).then_inc(stored["mv"], 16)
            copy(3)
            pool.wait_ge(xscored, 1)
            nc.gpsimd.partition_all_reduce(gmx, mxx, P, bass.bass_isa.ReduceOp.max).then_inc(xgmax, 1)
            pool.wait_ge(xzpart, 1)
            nc.gpsimd.partition_all_reduce(zzx, zsx, P, bass.bass_isa.ReduceOp.add).then_inc(xzall, 1)
            copy(len(copies))
            for s in range(3):
                pool.wait_ge(loaded[f"braw{s}"], 16)
            link(nc.gpsimd.tensor_copy(parts, braw))
            for s in (1, 2):
                link(nc.gpsimd.tensor_tensor(braw[32 * s:32 * s + 32, :], braw[32 * s:32 * s + 32, :],
                                             parts[32 * s:32 * s + 32, :], ALU.subtract))
            for s in (1, 2):
                link(nc.gpsimd.tensor_copy(parts[32 * s:32 * s + 32, :], braw[32 * s:32 * s + 32, :]))
            link(nc.gpsimd.tensor_tensor(braw[64:96, :], braw[64:96, :], parts[64:96, :], ALU.subtract))
            nc.gpsimd.tensor_copy(parts[64:96, :], braw[64:96, :]).then_inc(parts_in, 1)
            pool.wait_ge(most_in, 1)
            crowd = pool.value_load(most[0:1, 0:1], min_val=0, max_val=T)
            pool.wait_ge(y_stored, 32 * EXPERTS + 1)
            pool.wait_ge(wide_used, 8 * EXPERTS + 8)

            def gather(given):
                for t in range(3):
                    n = TOK[t][1]
                    for k in range(TOPK):
                        pool.indirect_dma_start(yk[4 * t + k][0:n, :], None, given,
                                                bass.IndirectOffsetOnAxis(ap=rows[0:n, t, k:k + 1], axis=0)).then_inc(gathered[t], 16)

            pool.wait_ge(tables, 1)
            with pool.If(crowd > CAP):
                pool.wait_ge(y_stored, 32 * STEPS + 1)
                pool.wait_ge(wide_used, 8 * STEPS + 8)
                gather(y_dram)
            with pool.Else():
                gather(y_dram[0:EXPERTS * CAP, :])
            pool.wait_ge(stored["copies"], 16 * (2 * DEC_B + 1))
            pool.wait_ge(stored["kv"], 64)
            pool.wait_ge(stored["pool"], 32)
            pool.wait_ge(stored["mk"], 16)
            pool.wait_ge(stored["mv"], 16)

        @block.scalar
        def _(act):
            A = nc.scalar.activation
            step = [0]

            def link(ins):
                step[0] += 1
                ins.then_inc(act_done, 1)
                act.wait_ge(act_done, step[0])

            def root(col, n, src, junk, wait_eps=False):
                link(A(junk, src, ACT.Square, accum_out=stat[0:n, col:col + 1]))
                A(stat[0:n, col:col + 1], stat[0:n, col:col + 1], ACT.Sqrt, bias=eps[0:n, :], scale=1.0 / D).then_inc(squares, 1)

            act.wait_ge(consts, 2)
            for t, (t0, n) in enumerate(TOK):
                act.wait_ge(loaded[f"x{t}"], 16)
                root(t, n, x[0:n, t, :], hn[0:n, t, :])
            for h in range(HEADS):
                ps, s = product(act, "toep", h)
                A(toep_sb[:, h, :], ps[:, 0:TOEP], ACT.Copy).then_inc(s, 1)
            act.wait_ge(toep_out, 16)
            for t, (t0, n) in enumerate(TOK):
                for c in range(3):
                    ps, s = product(act, "qkv", t, c)
                    A(qkvn[0:n, c, t, :], ps[0:n, :], ACT.Copy, scale=HD ** -0.5 if c == 0 else 1.0).then_inc(s, 1)
            for c in range(4):
                ps, s = product(act, "u", c)
                A(uP[:, c, STATE:UP], ps[:, 0:SEQ], ACT.Copy)
                link(A(unew[:, c, :], ps[:, SEQ:T], ACT.Copy))
                A(uS[:, c, :, STATE:US], ps[:, SEQ:T].rearrange("p (b t) -> p b t", t=DEC_T), ACT.Copy).then_inc(s, 1)
            for t, (t0, n) in enumerate(TOK):
                for name, dst in (("trq", qT), ("trk", kT)):
                    ps, s = product(act, name, t)
                    A(dst[:, :, t0:t0 + n], ps[:, :].rearrange("p (c n) -> p c n", n=P)[:, :, 0:n], ACT.Copy).then_inc(s, 1)
            ps, s = product(act, "state")
            A(uS[:, :, :, 0:STATE], ps[:, 0:480].rearrange("p (g b n) -> p g b n", g=4, n=STATE), ACT.Copy).then_inc(s, 1)
            ps, s = product(act, "utp")
            A(hn[0:STATE, 2, 0:512], ps[0:STATE, :], ACT.Copy).then_inc(s, 1)
            ps, s = product(act, "uts")
            A(hn[0:NS, 2, 512:1024], ps[0:NS, :], ACT.Copy).then_inc(s, 1)
            act.wait_ge(loaded["pscale"], 16)
            for g in range(4):
                ps, s = product(act, "pool", g)
                A(tb[:, 4 + g, :], ps[:, 0:T], ACT.Copy, scale=pscale[:, g:g + 1]).then_inc(s, 1)
            for u, (hp, qt) in enumerate(UNITS):
                nk = P * (qt + 1)
                act.wait_ge(summed, 2 * u + 2)
                for h in range(2):
                    A(lg[u % 2][:, h, 0:nk], lg[u % 2][:, h, 0:nk], ACT.Exp, bias=stat[:, 8 + 4 * (u % 2) + h:9 + 4 * (u % 2) + h],
                      accum_out=stat[:, 10 + 4 * (u % 2) + h:11 + 4 * (u % 2) + h]).then_inc(expd, 1)
                ps, s = product(act, "pt", u)
                w = 2 * nk
                A(pT[u % 2].rearrange("p c n -> p (c n)")[:, 0:w], ps[:, 0:w], ACT.Copy).then_inc(s, 1)
                ps, s = product(act, "o", u)
                A(tb[:, hp, P * qt:P * qt + P], ps[:, 0:P], ACT.Copy).then_inc(s, 1)
            act.wait_ge(loaded["mem"], 16)
            for t in range(2):
                root(3 + t, P, hn[:, t, :], mkTf[:, 0:D] if t == 0 else mkTf[:, D:2 * D])

            def fill(name):
                kind, t, h = name
                ps, s = product(act, *name)
                if kind == "trm":
                    for c in range(4):
                        ins = A(ta[:, 4 * h + c, P * t:P * t + P], ps[:, P * c:P * c + P], ACT.Copy,
                                scale=gcol[:, 1, 4 * h + c:4 * h + c + 1])
                    ins.then_inc(s, 1)
                elif kind == "mk":
                    A(hn[:, t, 512 * h:512 * h + 512], ps[:, :], ACT.Copy).then_inc(s, 1)
                elif kind == "trmk":
                    A(mkT[:, 4 * h:4 * h + 4, P * t:P * t + P], ps[:, :].rearrange("p (c n) -> p c n", n=P), ACT.Copy).then_inc(s, 1)
                else:
                    A(mv[:, t, 512 * h:512 * h + 512], ps[:, :], ACT.Copy).then_inc(s, 1)

            def sample_exp(b):
                act.wait_ge(shifted, b + 1)
                A(pr[:, :, :, :], pp[:, :, :, :], ACT.Exp).then_inc(sexp, 1)

            def sample_out(b):
                ps, s = product(act, "pv", b)
                v = ps[:, 0:32].rearrange("p (c t h) -> p c t h", t=DEC_T, h=2)
                c0 = SEQ + DEC_T * b
                link(A(tb[0:64, 0:4, c0:c0 + DEC_T], v[0:64, :, :, 0], ACT.Copy))
                A(tb[64:128, 0:4, c0:c0 + DEC_T], v[64:128, :, :, 1], ACT.Copy).then_inc(s, 1)

            for b in range(DEC_B):
                if b:
                    sample_exp(b - 1)
                    sample_out(b - 1)
                for f in FILL.get(b, []):
                    fill(f)
            sample_exp(DEC_B - 1)
            sample_out(DEC_B - 1)
            act.wait_ge(stored["mk"], 16)
            act.wait_ge(stored["pool"], 32)
            for t, (t0, n) in enumerate(TOK):
                read_out(act, "out", t, 0)
                read_out(act, "out", t, 1)
                root(5 + t, n, x[0:n, t, :], hn[0:n, t, :])
            for c in range(8):
                ps, s = product(act, "xq", c)
                A(tb[:, c, :], ps[:, 0:T], ACT.Copy, scale=XHD ** -0.5).then_inc(s, 1)
            act.wait_ge(stored["kv"], 64)
            for b in range(DEC_B):
                for m in range(2):
                    ps, s = product(act, "trck", b, m, 0)
                    A(ktm[b % 2][:, 0:4, P * m:P * m + P], ps[:, :].rearrange("p (c n) -> p c n", n=P), ACT.Copy).then_inc(s, 1)
            act.wait_ge(xshift, 1)
            A(px, sx, ACT.Exp).then_inc(xexp, 1)
            for u, (hp, qt) in enumerate(XUNITS):
                act.wait_ge(summed, 17 + u)
                ps, _ = product(act, "xs", u)
                for h in range(2):
                    ins = A(lg[u % 2][:, h, :], ps[:, 256 * h:256 * h + 256], ACT.Exp, bias=stat[:, 8 + 4 * (u % 2) + h:9 + 4 * (u % 2) + h],
                            accum_out=stat[:, 10 + 4 * (u % 2) + h:11 + 4 * (u % 2) + h])
                    if h == 0:
                        ins.then_inc(expd, 1)
                    else:
                        b_, _u = place(("xs", u))
                        ins.then_inc(bank_free[b_], 1)
                ps, s = product(act, "xpt", u)
                A(pT[u % 2].rearrange("p c n -> p (c n)"), ps[:, :], ACT.Copy).then_inc(s, 1)
                ps, s = product(act, "xo_", u)
                A(ta[:, 4 * hp:4 * hp + 4, P * qt:P * qt + P], ps[:, :].rearrange("p (c n) -> p c n", n=P), ACT.Copy).then_inc(s, 1)
            ps, s = product(act, "pvx")
            A(ta[:, :, SEQ:T], ps[:, 0:256].rearrange("p (c n) -> p c n", n=NS), ACT.Copy).then_inc(s, 1)
            for t, (t0, n) in enumerate(TOK):
                read_out(act, "xo", t, 0)
                read_out(act, "xo", t, 1)
                root(16 + t, n, x[0:n, t, :], hn[0:n, t, :])
            act.wait_ge(toph, 1)
            for t, (t0, n) in enumerate(TOK):
                A(gate[0:n, t, :], top[0:n, t, 0:4], ACT.Exp, bias=stat[0:n, 20 + t:21 + t], accum_out=stat[0:n, 24 + t:25 + t]).then_inc(gexp, 1)
            ps, s = product(act, "trg")
            A(gT, ps[0:EXPERTS, 0:T], ACT.Copy).then_inc(s, 1)
            act.wait_ge(most_in, 1)
            crowd = act.value_load(most[0:1, 0:1], min_val=0, max_val=T)
            for name in [("bd", t, h) for t in range(3) for h in range(2)]:
                read_out(act, *name)
            act.sem_inc(y_read, 1)
            act.sem_inc(y_stored, 1)

            def step_(n):
                act.wait_ge(gc_in, n + 1)
                A(sg, gc, ACT.Sigmoid, scale=1.702).then_inc(sg_in, 1)
                act.wait_ge(at_full, n + 1)
                A(aT.rearrange("p j h n -> p (j h n)"), bank_t[:, :], ACT.Copy).then_inc(at_in, 1)
                act.wait_ge(slim_used, 8 * n + 16)
                act.wait_ge(y_stored, 32 * n + 1)
                A(ye, bank_y[:, :], ACT.Copy).then_inc(y_read, 1)
                act.wait_ge(y_read, n + 2)
                for h in range(2):
                    act.dma_start(y_dram[ds(n * CAP, CAP), 512 * h:512 * h + 512], ye[64 * h:64 * h + 64, :]).then_inc(y_stored, 16)

            with act.Fori(0, EXPERTS) as n:
                step_(n)
            with act.If(crowd > CAP):
                with act.Fori(1, ROUNDS) as j:
                    with act.Fori(0, EXPERTS) as e:
                        step_(j * EXPERTS + e)
            for t, (t0, n) in enumerate(TOK):
                act.wait_ge(xsum, t + 1)
                root(32 + t, n, x[0:n, t, :], hn[0:n, t, :])

        @block.vector
        def _(dve):
            V = nc.vector
            step = [0]

            def link(ins):
                step[0] += 1
                ins.then_inc(dve_done, 1)
                dve.wait_ge(dve_done, step[0])

            def norm(col, n, src, dst, count):
                dve.wait_ge(squares, count)
                link(V.reciprocal(stat[0:n, col:col + 1], stat[0:n, col:col + 1]))
                V.tensor_scalar(dst, src, stat[0:n, col:col + 1], None, ALU.mult).then_inc(normed, 1)

            def gained(name, dst, g):
                for t, (t0, n) in enumerate(TOK):
                    for h in range(2):
                        ps, s = product(dve, name, t, h)
                        V.tensor_tensor(dst[:, 4 * h:4 * h + 4, t0:t0 + n], ps[:, :].rearrange("p (c n) -> p c n", n=P)[:, :, 0:n],
                                        gcol[:, g, 4 * h:4 * h + 4].unsqueeze(2).broadcast_to([P, 4, n]), ALU.mult).then_inc(s, 1)

            V.memset(eps[:, :], EPS).then_inc(consts, 1)
            V.memset(uP[:, :, 0:STATE], 0.0)
            V.memset(pp[:, 3, :, :], NEG)
            link(V.memset(rb[32:33, :], 1.0))
            dve.wait_ge(loaded["rel"], 16)
            V.tensor_copy(rbrep, rb.unsqueeze(2).broadcast_to([33, HEADS, P])).then_inc(rb_rep, 1)
            for t, (t0, n) in enumerate(TOK):
                norm(t, n, x[0:n, t, :], hn[0:n, t, :], t + 1)
            ps, s = product(dve, "bias_w")
            V.tensor_copy(bsw[:, :, :, :].rearrange("p k t h -> p (k t h)"), ps[:, 0:96]).then_inc(s, 1)
            ps, s = product(dve, "bias_f")
            dve.wait_ge(loaded["cfresh"], 16)
            for b in range(DEC_B):
                ins = V.tensor_tensor(bfr[:, b, :, :], ps[0:NS, 0:32].rearrange("p (t h) -> p t h", h=HEADS),
                                      fmask[:, 4 * b:4 * b + 4].unsqueeze(2).broadcast_to([NS, DEC_T, HEADS]), ALU.add)
            ins.then_inc(s, 1)
            dve.wait_ge(loaded["gcol"], 16)
            gained("tr1", ta, 0)
            for h in range(2):
                ps, s = product(dve, "fresh", h)
                dst = bfr[:, :, :, :].rearrange("p b t (c h) -> p h c (b t)", h=2)[:, h]
                V.tensor_tensor(dst, dst, ps[0:NS, 0:128].rearrange("p (c q) -> p c q", q=NS), ALU.add).then_inc(s, 1)
            dve.wait_ge(loaded["cfirst"], 16)
            for c in range(4):
                read_out(dve, "u", c)
            read_out(dve, "state")
            for g, w in enumerate(POOLW):
                sp_, ss_ = uP[:, g, :], uS[:, g]
                m, turn = 1, 0
                while m < w:
                    dp, dss = sum_p[turn], sum_s[turn]
                    V.tensor_tensor(dp[:, 2 * m - 1:UP], sp_[:, 2 * m - 1:UP], sp_[:, m - 1:UP - m], ALU.add)
                    link(V.tensor_tensor(dss[:, :, 2 * m - 1:US], ss_[:, :, 2 * m - 1:US], ss_[:, :, m - 1:US - m], ALU.add))
                    sp_, ss_ = dp, dss
                    m, turn = 2 * m, 1 - turn
                V.scalar_tensor_tensor(out=dT[:, g, 0:SEQ], in0=sp_[:, STATE:UP], scalar=1.0 / w, in1=uP[:, g, STATE:UP],
                                       op0=ALU.mult, op1=ALU.subtract)
                V.scalar_tensor_tensor(out=dT[:, g, SEQ:T].rearrange("p (b t) -> p b t", t=DEC_T), in0=ss_[:, :, STATE:US], scalar=1.0 / w,
                                       in1=uS[:, g, :, STATE:US], op0=ALU.mult, op1=ALU.subtract)
                link(V.tensor_tensor(stat[:, 48:64], sp_[:, STATE:STATE + 16], cfirst[:, g, :], ALU.mult))
                link(V.tensor_tensor(dT[:, g, 0:16], stat[:, 48:64], uP[:, g, STATE:STATE + 16], ALU.subtract))
                dve.sem_inc(pooled, 1)
            dve.wait_ge(loaded["toep"], 16)

            def logits(u):
                hp, qt = UNITS[u]
                nk = P * (qt + 1)
                if u >= 2:
                    b_, use = place(("pt", u - 2))
                    dve.wait_ge(bank_full[b_], use + 1)
                for h in range(2):
                    ps, s = product(dve, "s", u, h)
                    V.tensor_tensor(lg[u % 2][:, h, 0:nk], ps[:, 0:nk], bias[:, 2 * hp + h, SEQ - nk:SEQ], ALU.add).then_inc(s, 1)
                for h in range(2):
                    read_out(dve, "s", u, h)
                    c = 8 + 4 * (u % 2) + h
                    V.tensor_reduce(stat[:, c:c + 1], lg[u % 2][:, h, 0:nk], AX.X, ALU.max, negate=True).then_inc(summed, 1)

            def share(u, n, nk):
                c = 10 + 4 * (u % 2)
                link(V.reciprocal(stat[:, c:c + 2], stat[:, c:c + 2]))
                V.tensor_tensor(lg[u % 2][:, :, 0:nk], lg[u % 2][:, :, 0:nk],
                                stat[:, c:c + 2].unsqueeze(2).broadcast_to([P, 2, nk]), ALU.mult).then_inc(scaled, 1)

            for g in range(4):
                b_, use = place(("pool", g))
                dve.wait_ge(bank_full[b_], use + 1)
            logits(0)
            for u in range(8):
                if u + 1 < 8:
                    logits(u + 1)
                dve.wait_ge(expd, 2 * u + 2)
                share(u, u + 1, P * (UNITS[u][1] + 1))
            for t in range(2):
                norm(3 + t, P, hn[:, t, :], hn[:, t, :], 4 + t)

            def shift(b):
                dve.wait_ge(gmax, b + 1)
                s = S_[b % 2]
                V.tensor_tensor(pp[:, 0:3, :, :].rearrange("p k t h -> p k (t h)"), s.rearrange("p k t h -> p k (t h)"),
                                gm.unsqueeze(1).broadcast_to([P, 3, 32]), ALU.subtract)
                link(V.tensor_tensor(pp[0:NS, 3, :, :].rearrange("p t h -> p (t h)"), bfr[:, b, :, :].rearrange("p t h -> p (t h)"),
                                     gm[0:NS, :], ALU.subtract))
                dve.sem_inc(shifted, 1)

            def sums(b):
                dve.wait_ge(sexp, b + 1)
                V.tensor_reduce(zs, pr[:, :, :, :].rearrange("p k t h -> p (t h) k"), AX.X, ALU.add).then_inc(zpart, 1)

            def shares(b):
                dve.wait_ge(zall, b + 1)
                link(V.reciprocal(zz, zz))
                V.tensor_tensor(pr[:, :, :, :].rearrange("p k t h -> p k (t h)"), pr[:, :, :, :].rearrange("p k t h -> p k (t h)"),
                                zz.unsqueeze(1).broadcast_to([P, 4, 32]), ALU.mult).then_inc(prob, 1)

            for b in range(DEC_B):
                dve.wait_ge(k_in[b % 2], 48 * (b // 2 + 1))
                kw = kwin[b % 2]
                for t in range(DEC_T):
                    ps, s = product(dve, "qb", b, t)
                    pair = kw[:, 0:8, :].rearrange("p (k s) n -> p k s n", k=2)[:, :, t, :]
                    V.tensor_tensor(prod[:, 0:2, :], pair, ps[:, :].unsqueeze(1).broadcast_to([P, 2, AW]), ALU.mult)
                    V.tensor_tensor(prod[:, 2, :], kw[:, 8, :], ps[:, :], ALU.mult).then_inc(s, 1)
                    read_out(dve, "qb", b, t)
                    link(V.tensor_reduce(S_[b % 2][:, :, t, :], prod.rearrange("p k (h d) -> p k h d", d=HD), AX.X, ALU.add))
                    if b and t < 3:
                        (shift, sums, shares)[t](b - 1)
                s = S_[b % 2]
                link(V.tensor_tensor(s, s, bsw[:, :, :, :], ALU.add))
                link(V.tensor_reduce(mx, s.rearrange("p k t h -> p (t h) k"), AX.X, ALU.max))
                V.tensor_tensor(mx[0:NS, :], mx[0:NS, :], bfr[:, b, :, :].rearrange("p t h -> p (t h)"), ALU.max).then_inc(scored, 1)
            shift(DEC_B - 1), sums(DEC_B - 1), shares(DEC_B - 1)

            def residual(name):
                for t, (t0, n) in enumerate(TOK):
                    for h in range(2):
                        ps, s = product(dve, name, t, h)
                        dst = x[0:n, t, 512 * h:512 * h + 512]
                        V.tensor_tensor(dst, dst, ps[0:n, :], ALU.add).then_inc(s, 1)

            residual("out")
            for t, (t0, n) in enumerate(TOK):
                norm(5 + t, n, x[0:n, t, :], hn[0:n, t, :], 6 + t)
            gained("tr2", ta, 2)
            def take_scores(b):
                ps, s = product(dve, "sx", b)
                V.tensor_copy(sx[:, b].rearrange("p m c -> p (m c)"), ps[:, 0:32]).then_inc(s, 1)

            dve.wait_ge(stored["kv"], 64)
            for b in range(DEC_B):
                for m in range(2):
                    ps, s = product(dve, "trck", b, m, 1)
                    V.tensor_copy(ktm[b % 2][:, 4:8, P * m:P * m + P], ps[:, :].rearrange("p (c n) -> p c n", n=P)).then_inc(s, 1)
                if b:
                    take_scores(b - 1)
            take_scores(DEC_B - 1)
            for b in range(DEC_B):
                read_out(dve, "sx", b)
            flat = sx
            link(V.tensor_reduce(mxx.rearrange("p (b c) -> p b c", c=16), flat.rearrange("p b m c -> p b c m"), AX.X, ALU.max))
            dve.sem_inc(xscored, 1)
            dve.wait_ge(xgmax, 1)
            link(V.tensor_tensor(sx, flat, gmx.rearrange("p (b c) -> p b c", c=16).unsqueeze(2).broadcast_to([P, 8, 2, 16]), ALU.subtract))
            dve.sem_inc(xshift, 1)
            dve.wait_ge(xexp, 1)
            V.tensor_reduce(zsx.rearrange("p (b c) -> p b c", c=16), px.rearrange("p b m c -> p b c m"), AX.X, ALU.add).then_inc(xzpart, 1)
            dve.wait_ge(xzall, 1)
            link(V.reciprocal(zzx, zzx))
            V.tensor_tensor(px, px, zzx.rearrange("p (b c) -> p b c", c=16).unsqueeze(2).broadcast_to([P, 8, 2, 16]), ALU.mult).then_inc(xprob, 1)
            def xmax(u):
                if u >= 2:
                    b_, use = place(("xpt", u - 2))
                    dve.wait_ge(bank_full[b_], use + 1)
                ps, _ = product(dve, "xs", u)
                c = 8 + 4 * (u % 2)
                V.tensor_reduce(stat[:, c:c + 2], ps[:, :].rearrange("p (h n) -> p h n", n=NMEM), AX.X, ALU.max, negate=True).then_inc(summed, 1)

            xmax(0)
            for u in range(4):
                if u + 1 < 4:
                    xmax(u + 1)
                read_out(dve, "xs", u)
                dve.wait_ge(expd, 17 + u)
                share(u, 9 + u, NMEM)
            residual("xo")
            for t, (t0, n) in enumerate(TOK):
                norm(16 + t, n, x[0:n, t, :], hn[0:n, t, :], 9 + t)
            gained("tr3", tb, 3)
            for t, (t0, n) in enumerate(TOK):
                ps, s = product(dve, "route", t)
                V.tensor_copy(logit[0:n, t, :], ps[0:n, 0:EXPERTS]).then_inc(s, 1)
                read_out(dve, "route", t)
                link(V.max(top[0:n, t, :], logit[0:n, t, :]))
                V.max_index(idx[0:n, t, :], top[0:n, t, :], logit[0:n, t, :])
                link(V.tensor_scalar(stat[0:n, 20 + t:21 + t], top[0:n, t, 0:1], -1.0, None, ALU.mult))
            dve.sem_inc(toph, 1)
            dve.wait_ge(loaded["iota"], 16)
            for t, (t0, n) in enumerate(TOK):
                link(V.tensor_copy(idxf[0:n, t, :], idx[0:n, t, :]))
                for k in range(TOPK):
                    ins = V.tensor_scalar(hot[0:n, t, k, :], iota[0:n, 0:EXPERTS], idxf[0:n, t, k:k + 1], None, ALU.is_equal)
                link(ins)
                V.tensor_reduce(msk[0:n, t, :], hot[0:n, t].rearrange("p k e -> p e k"), AX.X, ALU.add).then_inc(hots, 1)
            dve.wait_ge(gexp, 3)
            for t, (t0, n) in enumerate(TOK):
                link(V.reciprocal(stat[0:n, 24 + t:25 + t], stat[0:n, 24 + t:25 + t]))
                link(V.tensor_scalar(gate[0:n, t, :], gate[0:n, t, :], stat[0:n, 24 + t:25 + t], None, ALU.mult))
                link(V.tensor_tensor(prodr[0:n, t], hot[0:n, t], gate[0:n, t, :].unsqueeze(2).broadcast_to([n, TOPK, EXPERTS]), ALU.mult))
                V.tensor_reduce(gmat[0:n, t, :], prodr[0:n, t].rearrange("p k e -> p e k"), AX.X, ALU.add).then_inc(gmats, 1)
            for t, (t0, n) in enumerate(TOK):
                ps, s = product(dve, "pos", t)
                V.tensor_copy(posn[0:n, t, :], ps[0:n, 0:EXPERTS]).then_inc(s, 1)
                read_out(dve, "pos", t)
                link(V.scalar_tensor_tensor(out=table[0:n, t, 0:EXPERTS], in0=posn[0:n, t, :], scalar=FAR, in1=msk[0:n, t, :],
                                            op0=ALU.add, op1=ALU.mult))
                link(V.tensor_scalar(table[0:n, t, 0:EXPERTS], table[0:n, t, 0:EXPERTS], -FAR, None, ALU.add))
                for j in range(1, ROUNDS):
                    V.tensor_scalar(table[0:n, t, EXPERTS * j:EXPERTS * j + EXPERTS], table[0:n, t, 0:EXPERTS], -float(CAP * j), None, ALU.add)
                ins = V.memset(table[0:n, t, STEPS:NTAB], -FAR)
                link(ins)
            for t, (t0, n) in enumerate(TOK):
                ins = V.tensor_scalar(onehot[0:n, t, :], iota[0:n, 0:CAP], table[0:n, t, 0:1], None, ALU.is_equal)
            link(ins)
            dve.sem_inc(onehot_in, 1)
            ps, s = product(dve, "count")
            link(V.tensor_reduce(cntf, ps[0:1, 0:EXPERTS], AX.X, ALU.max))
            link(V.tensor_copy(most[:, :], cntf))
            dve.sem_inc(s, 1)
            dve.sem_inc(most_in, 1)
            crowd = dve.value_load(most[0:1, 0:1], min_val=0, max_val=T)
            residual("bd")
            dve.wait_ge(loaded["expert"], 16)
            V.tensor_scalar(pick, ones[0:96, 0:CAP], expert1[:, 0:1], None, ALU.mult).then_inc(pick_in, 1)

            def evac_xe():
                V.tensor_tensor(xe, bank_x[:, :].rearrange("p (k n) -> p k n", n=CAP),
                                gcol[:, 3, :].unsqueeze(2).broadcast_to([P, KC, CAP]), ALU.mult).then_inc(xe_in, 1)

            dve.wait_ge(xg_full, 1)
            evac_xe()
            for t, (t0, n) in enumerate(TOK):
                ins = V.tensor_scalar(onehot[0:n, t, :], iota[0:n, 0:CAP], table[0:n, t, 1:2], None, ALU.is_equal)
            ins.then_inc(onehot_in, 1)
            for t, (t0, n) in enumerate(TOK):
                link(V.tensor_tensor(prodr[0:n, t], hot[0:n, t], posn[0:n, t, :].unsqueeze(1).broadcast_to([n, TOPK, EXPERTS]), ALU.mult))
                link(V.tensor_reduce(slot[0:n, t, :], prodr[0:n, t], AX.X, ALU.add))
                link(V.scalar_tensor_tensor(out=rowf[0:n, t, :], in0=idxf[0:n, t, 0:TOPK], scalar=float(CAP), in1=slot[0:n, t, :],
                                            op0=ALU.mult, op1=ALU.add))
                for j in range(1, ROUNDS):
                    link(V.tensor_scalar(jump[0:n, t, :], slot[0:n, t, :], float(CAP * j), float((EXPERTS - 1) * CAP), ALU.is_ge, ALU.mult))
                    link(V.tensor_tensor(rowf[0:n, t, :], rowf[0:n, t, :], jump[0:n, t, :], ALU.add))
                link(V.tensor_copy(rows[0:n, t, :], rowf[0:n, t, :]))
            dve.sem_inc(tables, 1)

            def step_(n):
                dve.wait_ge(wide_used, 8 * n + 16)
                V.tensor_scalar(gc, bank_g[:, :], 7.0, None, ALU.min).then_inc(gc_in, 1)
                V.tensor_scalar(uc, bank_u[:, :], 7.0, -7.0, ALU.min, ALU.max).then_inc(uc_in, 1)
                dve.wait_ge(gc_in, n + 1)
                dve.wait_ge(uc_in, n + 1)
                V.scalar_tensor_tensor(out=gu, in0=uc, scalar=1.0, in1=gc, op0=ALU.add, op1=ALU.mult).then_inc(gu_in, 1)
                dve.wait_ge(gu_in, n + 1)
                dve.wait_ge(sg_in, n + 1)
                V.tensor_tensor(gu, gu, sg, ALU.mult).then_inc(a_in, 1)
                V.tensor_scalar(pick, ones[0:96, 0:CAP], expert1[:, ds(n + 1, 1)], None, ALU.mult).then_inc(pick_in, 1)
                dve.wait_ge(xg_full, n + 2)
                evac_xe()
                for t, (t0, m) in enumerate(TOK):
                    ins = V.tensor_scalar(onehot[0:m, t, :], iota[0:m, 0:CAP], table[0:m, t, ds(n + 2, 1)], None, ALU.is_equal)
                ins.then_inc(onehot_in, 1)

            with dve.Fori(0, EXPERTS) as n:
                step_(n)
            with dve.If(crowd > CAP):
                with dve.Fori(1, ROUNDS) as j:
                    with dve.Fori(0, EXPERTS) as e:
                        step_(j * EXPERTS + e)
            def last_norm(t):
                n = TOK[t][1]
                dve.wait_ge(squares, 12 + t)
                link(V.reciprocal(stat[0:n, 32 + t:33 + t], stat[0:n, 32 + t:33 + t]))
                V.scalar_tensor_tensor(out=xout[t][0:n, :], in0=x[0:n, t, :], scalar=stat[0:n, 32 + t:33 + t], in1=gfin[0:n, :],
                                       op0=ALU.mult, op1=ALU.mult).then_inc(fin, 1)

            for t, (t0, n) in enumerate(TOK):
                dve.wait_ge(gathered[t], 64)
                for k in range(TOPK):
                    ins = V.scalar_tensor_tensor(out=x[0:n, t, :], in0=yk[4 * t + k][0:n, :], scalar=gate[0:n, t, k:k + 1],
                                                 in1=x[0:n, t, :], op0=ALU.mult, op1=ALU.add)
                    if k < TOPK - 1:
                        link(ins)
                ins.then_inc(xsum, 1)
                if t == 0:
                    dve.wait_ge(loaded["gfin"], 16)
                else:
                    last_norm(t - 1)
            last_norm(2)

        @block.tensor
        def _(pe):
            M = nc.tensor.matmul
            TR = nc.tensor.transpose

            pe.wait_ge(loaded["cbias"], 16)
            pe.wait_ge(rb_rep, 1)
            cw = [cb[:, TOEP + P * s:TOEP + P * s + P] for s in range(6)]
            ps, s = take(pe, "bias_w")
            for kind in range(3):
                for t in range(DEC_T):
                    c = 32 * kind + 8 * t
                    ins = M(ps[:, c:c + 8], cw[kind if kind < 2 else 2 + t], rb, start=True, stop=True)
            ins.then_inc(s, 1)
            ps, s = take(pe, "bias_f")
            for t in range(DEC_T):
                c = TOEP + 6 * P + NS * t
                ins = M(ps[0:NS, 8 * t:8 * t + 8], cb[:, c:c + NS], rb, start=True, stop=True)
            ins.then_inc(s, 1)
            for h in range(HEADS):
                ps, s = take(pe, "toep", h)
                M(ps[:, 0:TOEP], rbrep[:, h, :], cb[:, 0:TOEP], start=True, stop=True).then_inc(s, 1)

            def transposes(name, count):
                for t, (t0, n) in enumerate(TOK):
                    pe.wait_ge(normed, count + t)
                    for h in range(2):
                        ps, s = take(pe, name, t, h)
                        for c in range(4):
                            ins = TR(ps[:, P * c:P * c + n], hn[0:n, t, 512 * h + P * c:512 * h + P * c + P], ident[0:n, 0:n])
                        ins.then_inc(s, 1)

            pe.wait_ge(loaded["ident"], 16)
            transposes("tr1", 1)
            for t, (t0, n) in enumerate(TOK):
                read_out(pe, "tr1", t, 0), read_out(pe, "tr1", t, 1)
                tk = [take(pe, "qkv", t, c) for c in range(3)]
                for k in range(KC):
                    if t == 0:
                        pe.wait_ge(wide_in[k], 16)
                    for c in range(3):
                        ins = M(tk[c][0][0:n, :], ta[:, k, t0:t0 + n], wide[:, k, 512 * c:512 * c + 512], start=k == 0, stop=k == KC - 1)
                        if k == KC - 1:
                            ins.then_inc(tk[c][1], 1)
            for c in range(4):
                ps, s = take(pe, "u", c)
                for k in range(KC):
                    ins = M(ps[:, 0:T], wide[:, k, 1536 + P * c:1536 + P * c + P], ta[:, k, :], start=k == 0, stop=k == KC - 1)
                ins.then_inc(s, 1)
            for t, (t0, n) in enumerate(TOK):
                for ci, name, src in ((0, "trq", qn), (1, "trk", kn)):
                    read_out(pe, "qkv", t, ci)
                    ps, s = take(pe, name, t)
                    for c in range(4):
                        ins = TR(ps[:, P * c:P * c + n], src[0:n, t, P * c:P * c + P], ident[0:n, 0:n])
                    ins.then_inc(s, 1)
            for h in range(2):
                read_out(pe, "trq", 2), read_out(pe, "trk", 2)
                ps, s = take(pe, "fresh", h)
                for c in range(4):
                    ins = M(ps[0:NS, NS * c:NS * c + NS], kT[64 * h:64 * h + 64, c, SEQ:T], qT[64 * h:64 * h + 64, c, SEQ:T], start=True, stop=True)
                ins.then_inc(s, 1)
            pe.wait_ge(loaded["state"], 16)
            ps, s = take(pe, "state")
            ns = DEC_B * STATE
            for c in range(4):
                ins = TR(ps[:, ns * c:ns * c + ns], state[:, P * c:P * c + P], ident[0:ns, 0:ns])
            ins.then_inc(s, 1)
            for c in range(4):
                read_out(pe, "u", c)
            ps, s = take(pe, "utp")
            for c in range(4):
                ins = TR(ps[0:STATE, P * c:P * c + P], uP[:, c, UP - STATE:UP], ident[:, :])
            ins.then_inc(s, 1)
            ps, s = take(pe, "uts")
            for c in range(4):
                ins = TR(ps[0:NS, P * c:P * c + P], unew[:, c, :], ident[:, :])
            ins.then_inc(s, 1)
            pe.wait_ge(loaded["wpool"], 16)
            for g in range(4):
                pe.wait_ge(pooled, g + 1)
                ps, s = take(pe, "pool", g)
                M(ps[:, 0:T], wpool[:, g, :], dT[:, g, :], start=True, stop=True).then_inc(s, 1)

            def scores(u):
                hp, qt = UNITS[u]
                nk = P * (qt + 1)
                for h in range(2):
                    ps, s = take(pe, "s", u, h)
                    r = slice(64 * h, 64 * h + 64)
                    M(ps[:, 0:nk], qT[r, hp, P * qt:P * qt + P], kT[r, hp, 0:nk], start=True, stop=True).then_inc(s, 1)

            for t in range(2):
                read_out(pe, "trq", t), read_out(pe, "trk", t)
            scores(0)
            for u, (hp, qt) in enumerate(UNITS):
                if u + 1 < 8:
                    scores(u + 1)
                pe.wait_ge(scaled, u + 1)
                ps, s = take(pe, "pt", u)
                for h in range(2):
                    for c in range(qt + 1):
                        z = P * ((qt + 1) * h + c)
                        ins = TR(ps[:, z:z + P], lg[u % 2][:, h, P * c:P * c + P], ident[:, :])
                ins.then_inc(s, 1)
                read_out(pe, "pt", u)
                ps, s = take(pe, "o", u)
                for h in range(2):
                    for c in range(qt + 1):
                        hd = 64 * (2 * hp + h)
                        ins = M(ps[64 * h:64 * h + 64, 0:P], vn[:, c, hd:hd + 64], pT[u % 2][:, (qt + 1) * h + c, :], start=c == 0, stop=c == qt)
                ins.then_inc(s, 1)

            def rows_times(name, t, left, n, t0, halves=2):
                tk = [take(pe, name, t, h) for h in range(2)]
                for k in range(KC):
                    if t == 0:
                        pe.wait_ge(slim_in[k], 16 * round_[0])
                    for h in range(2):
                        ins = M(tk[h][0][0:n, :], left[:, k, t0:t0 + n], slim[:, k, 512 * h:512 * h + 512], start=k == 0, stop=k == KC - 1)
                        if k == KC - 1:
                            ins.then_inc(tk[h][1], 1)
                return ins

            round_ = [1]

            def fill(name):
                kind, t, h = name
                if kind == "trm":
                    pe.wait_ge(normed, 4 + t)
                    ps, s = take(pe, *name)
                    for c in range(4):
                        ins = TR(ps[:, P * c:P * c + P], hn[:, t, 512 * h + P * c:512 * h + P * c + P], ident[:, :])
                    ins.then_inc(s, 1)
                elif kind in ("mk", "mv"):
                    if h == 0:
                        round_[0] = 1 if kind == "mk" else 2
                        read_out(pe, "trm", t, 0), read_out(pe, "trm", t, 1)
                        rows_times(kind, t, ta, P, P * t)
                else:
                    read_out(pe, "mk", t, h)
                    ps, s = take(pe, *name)
                    for c in range(4):
                        ins = TR(ps[:, P * c:P * c + P], hn[:, t, 512 * h + P * c:512 * h + P * c + P], ident[:, :])
                    ins.then_inc(s, 1)

            def values(b):
                pe.wait_ge(prob, b + 1)
                pe.wait_ge(v_in, 48 * (b + 1))
                ps, s = take(pe, "pv", b)
                for c in range(4):
                    dst = ps[:, 8 * c:8 * c + 8]
                    cc = slice(P * c, P * c + P)
                    M(dst, vwin[:, 8, cc], pr[:, 2, :, 2 * c:2 * c + 2], start=True, stop=False)
                    M(dst, vn[0:NS, 2, cc], pr[0:NS, 3, :, 2 * c:2 * c + 2], start=False, stop=False)
                    for kind in range(2):
                        for t in range(DEC_T):
                            ins = M(dst[:, 2 * t:2 * t + 2], vwin[:, 4 * kind + t, cc], pr[:, kind, t, 2 * c:2 * c + 2],
                                    start=False, stop=kind == 1 and t == DEC_T - 1)
                ins.then_inc(s, 1)

            for b in range(DEC_B):
                for t in range(DEC_T):
                    ps, s = take(pe, "qb", b, t)
                    r = DEC_T * b + t
                    M(ps[:, :], ident[0:NS, r:r + 1].broadcast_to([NS, P]), qn[0:NS, 2, :], start=True, stop=True).then_inc(s, 1)
                if b:
                    values(b - 1)
                for f in FILL.get(b, []):
                    fill(f)
            values(DEC_B - 1)
            read_out(pe, "pv", DEC_B - 1)
            round_[0] = 3
            for t, (t0, n) in enumerate(TOK):
                rows_times("out", t, tb, n, t0)
            transposes("tr2", 6)
            for t in range(3):
                read_out(pe, "tr2", t, 0), read_out(pe, "tr2", t, 1)
            for c in range(8):
                ps, s = take(pe, "xq", c)
                for k in range(KC):
                    if c == 0:
                        pe.wait_ge(slim_in[k], 64)
                    ins = M(ps[:, 0:T], slim[:, k, P * c:P * c + P], ta[:, k, :], start=k == 0, stop=k == KC - 1)
                ins.then_inc(s, 1)

            def cross_scores(b):
                for m in range(2):
                    read_out(pe, "trck", b, m, 0), read_out(pe, "trck", b, m, 1)
                ps, s = take(pe, "sx", b)
                for m in range(2):
                    for h in range(XH):
                        z = 16 * m + 4 * h
                        for c in range(2):
                            ins = M(ps[:, z:z + 4], ktm[b % 2][:, 2 * h + c, P * m:P * m + P],
                                    tb[:, 2 * h + c, SEQ + 4 * b:SEQ + 4 * b + 4], start=c == 0, stop=c == 1)
                ins.then_inc(s, 1)

            for c in range(8):
                read_out(pe, "xq", c)
            for b in range(DEC_B):
                pe.wait_ge(ck_in[b % 4], 16 * (b // 4 + 1))
                for m in range(2):
                    for h in range(2):
                        ps, s = take(pe, "trck", b, m, h)
                        for c in range(4):
                            ins = TR(ps[:, P * c:P * c + P], cmem[b % 4][:, m, 512 * h + P * c:512 * h + P * c + P], ident[:, :])
                        ins.then_inc(s, 1)
                if b:
                    cross_scores(b - 1)
            cross_scores(DEC_B - 1)

            def xscores(u):
                hp, qt = XUNITS[u]
                ps, s = take(pe, "xs", u)
                for h in range(2):
                    for c in range(2):
                        k = 2 * (2 * hp + h) + c
                        ins = M(ps[:, 256 * h:256 * h + 256], tb[:, k, P * qt:P * qt + P], mkT[:, k, :], start=c == 0, stop=c == 1)
                ins.then_inc(s, 1)

            xscores(0)
            for u, (hp, qt) in enumerate(XUNITS):
                if u + 1 < 4:
                    xscores(u + 1)
                pe.wait_ge(scaled, 9 + u)
                ps, s = take(pe, "xpt", u)
                for h in range(2):
                    for c in range(2):
                        z = P * (2 * h + c)
                        ins = TR(ps[:, z:z + P], lg[u % 2][:, h, P * c:P * c + P], ident[:, :])
                ins.then_inc(s, 1)
                read_out(pe, "xpt", u)
                ps, s = take(pe, "xo_", u)
                for h in range(2):
                    for c in range(2):
                        z = P * (2 * h + c)
                        hd = XHD * (2 * hp + h) + P * c
                        for m in range(2):
                            ins = M(ps[:, z:z + P], mv[:, m, hd:hd + P], pT[u % 2][:, 2 * h + m, :], start=m == 0, stop=m == 1)
                ins.then_inc(s, 1)
            pe.wait_ge(xprob, 1)
            ps, s = take(pe, "pvx")
            for b in range(DEC_B):
                pe.wait_ge(cv_in[b], 16)
                v = cmem[4 + b if b < 4 else b - 4]
                for k in range(KC):
                    z = NS * k + DEC_T * b
                    h = k // 2
                    for m in range(2):
                        ins = M(ps[:, z:z + 4], v[:, m, P * k:P * k + P], px[:, b, m, 4 * h:4 * h + 4], start=m == 0, stop=m == 1)
            ins.then_inc(s, 1)
            b_, use = place(("pvx",))
            pe.wait_ge(bank_full[b_], use + 1)
            pe.sem_inc(wide_used, 8)
            read_out(pe, "pvx")
            round_[0] = 5
            for u in range(4):
                read_out(pe, "xo_", u)
            for t, (t0, n) in enumerate(TOK):
                rows_times("xo", t, ta, n, t0)
            b_, use = place(("xo", 2, 1))
            pe.wait_ge(bank_full[b_], use + 1)
            pe.sem_inc(slim_used, 8)
            transposes("tr3", 9)
            pe.wait_ge(loaded["wr"], 16)
            pe.wait_ge(loaded["brow"], 16)
            for t, (t0, n) in enumerate(TOK):
                read_out(pe, "tr3", t, 0), read_out(pe, "tr3", t, 1)
                ps, s = take(pe, "route", t)
                for k in range(KC):
                    M(ps[0:n, 0:EXPERTS], tb[:, k, t0:t0 + n], wr[:, k, :], start=k == 0, stop=False)
                M(ps[0:n, 0:EXPERTS], ones[0:1, 0:n], brow, start=False, stop=True).then_inc(s, 1)
            pe.wait_ge(loaded["before"], 16)
            for t, (t0, n) in enumerate(TOK):
                pe.wait_ge(hots, t + 1)
                ps, s = take(pe, "pos", t)
                for t_ in range(t):
                    M(ps[0:n, 0:EXPERTS], ones[:, 0:n], msk[:, t_, :], start=t_ == 0, stop=False)
                M(ps[0:n, 0:EXPERTS], before[0:n, 0:n], msk[0:n, t, :], start=t == 0, stop=True).then_inc(s, 1)
            ps, s = take(pe, "count")
            for t, (t0, n) in enumerate(TOK):
                ins = M(ps[0:1, 0:EXPERTS], ones[0:n, 0:1], msk[0:n, t, :], start=t == 0, stop=t == 2)
            ins.then_inc(s, 1)
            pe.wait_ge(gmats, 3)
            ps, s = take(pe, "trg")
            for t, (t0, n) in enumerate(TOK):
                ins = TR(ps[0:EXPERTS, t0:t0 + n], gmat[0:n, t, :], ident[0:n, 0:n])
            ins.then_inc(s, 1)
            read_out(pe, "trg")
            pe.wait_ge(loaded["bdn"], 16)
            for t, (t0, n) in enumerate(TOK):
                for h in range(2):
                    ps, s = take(pe, "bd", t, h)
                    M(ps[0:n, :], gT[:, t0:t0 + n], bdn[:, 512 * h:512 * h + 512], start=True, stop=True).then_inc(s, 1)
            pe.wait_ge(most_in, 1)
            crowd = pe.value_load(most[0:1, 0:1], min_val=0, max_val=T)
            for name in jobs[-8:]:
                read_out(pe, *name)

            def gather(count):
                pe.wait_ge(onehot_in, count)
                for k in range(KC):
                    for t, (t0, m) in enumerate(TOK):
                        ins = M(bank_x[:, CAP * k:CAP * k + CAP], hn[0:m, t, P * k:P * k + P], onehot[0:m, t, :], start=t == 0, stop=t == 2)
                ins.then_inc(xg_full, 1)

            gather(1)
            pe.wait_ge(parts_in, 1)

            def step_(n):
                half = [slice(0, CAP), slice(CAP, 2 * CAP)]
                pe.wait_ge(pick_in, n + 1)
                for q, bk in enumerate((bank_g, bank_u)):
                    for h in range(2):
                        c = D * q + 512 * h
                        M(bk[half[h], :], pick, parts[:, c:c + 512], start=True, stop=False)
                pe.wait_ge(xe_in, n + 1)
                for k in range(KC):
                    pe.wait_ge(wide_in[k], 16 * n + 32)
                    for q, bk in enumerate((bank_g, bank_u)):
                        for h in range(2):
                            c = D * q + 512 * h
                            ins = M(bk[half[h], :], xe[:, k, :], wide[:, k, c:c + 512], start=False, stop=k == KC - 1)
                    ins.then_inc(wide_used, 1)
                gather(n + 2)
                pe.wait_ge(a_in, n + 1)
                for j in range(4):
                    ins = TR(bank_t[:, P * j:P * j + P], gu[:, P * j:P * j + P], ident[:, :])
                ins.then_inc(at_full, 1)
                pe.wait_ge(at_in, n + 1)
                pe.wait_ge(y_read, n + 1)
                for f in range(KC):
                    pe.wait_ge(slim_in[f], 16 * n + 96)
                    for h in range(2):
                        ins = M(bank_y[half[h], :], aT[:, f % 4, f // 4, :], slim[:, f, 512 * h:512 * h + 512], start=f == 0, stop=f == KC - 1)
                    ins.then_inc(slim_used, 1)

            with pe.Fori(0, EXPERTS) as n:
                step_(n)
            with pe.If(crowd > CAP):
                with pe.Fori(1, ROUNDS) as j:
                    with pe.Fori(0, EXPERTS) as e:
                        step_(j * EXPERTS + e)


_OUTS = [
    ("y_prompt", (1, SEQ, D)), ("y_sample", (DEC_B, DEC_T, D)),
    ("k_win_prompt", (1, 1, SEQ, HEADS, HD)), ("v_win_prompt", (1, 1, SEQ, HEADS, HD)),
    ("pool_prompt", (1, 1, STATE, AW)),
    ("mem_k_prompt", (1, 1, NMEM, XH, XHD)), ("mem_v_prompt", (1, 1, NMEM, XH, XHD)),
    ("k_win_sample", (1, DEC_B, PAST, HEADS, HD)), ("v_win_sample", (1, DEC_B, PAST, HEADS, HD)),
    ("pool_sample", (1, DEC_B, STATE, AW)),
]
_PLAIN = ["x_prompt", "x_sample", "cache_k_win", "cache_v_win", "state_pool", "cache_mem_k", "cache_mem_v",
          "mem_prompt", "rel_bias", "w_in", "w_pool", "w_out", "w_xq", "w_xk", "w_xv", "w_xo", "w_router",
          "b_router", "w_gate_up", "b_gate_up", "w_down", "b_down"]


def kernel(**inputs):
    import numpy as _np
    import concourse.bacc as _bacc
    from concourse import mybir as _mybir
    from concourse.bass_utils import run_bass_kernel_spmd as _run

    nc = _bacc.Bacc("TRN2", target_bir_lowering=False, num_devices=1)
    arrays = {n: _np.ascontiguousarray(inputs[n]) for n in _PLAIN}
    cols = [_np.asarray(inputs[n])[0].reshape(KC, P).T for n in ("g_mix", "g_mem", "g_x", "g_ff")]
    arrays["g_all"] = _np.ascontiguousarray(_np.stack(cols, 1))
    arrays["pool_scale_col"] = _np.ascontiguousarray(_np.asarray(inputs["pool_scale"])[0].reshape(4, P).T)
    arrays["g_final_rows"] = _np.ascontiguousarray(_np.broadcast_to(_np.asarray(inputs["g_final"]), (P, D)))
    arrays.update(constants())
    ins = {n: nc.dram_tensor(f"in_{n}", a.shape, _mybir.dt.from_np(a.dtype), kind="ExternalInput").ap() for n, a in arrays.items()}
    outs = {n: nc.dram_tensor(f"out_{n}", shape, _mybir.dt.float32, kind="ExternalOutput").ap() for n, shape in _OUTS}
    build(nc, ins, outs)
    r = _run(nc, [{f"in_{n}": a for n, a in arrays.items()}], core_ids=[0])
    return tuple(r.results[0][f"out_{n}"] for n, _ in _OUTS)
```

```python
import math
from contextlib import ExitStack

import concourse.bass as bass
import numpy as np
from concourse import mybir

P = 128
D = 1024
KC = D // P
SEQ, DEC_B, DEC_T = 256, 8, 4
NS = DEC_B * DEC_T
T = SEQ + NS
TOK = [(0, P), (P, P), (SEQ, NS)]
PAST = 2048
HEADS, HD = 8, 64
AW = HEADS * HD
NMEM, XH, XHD = 256, 4, 256
POOLW = (2, 4, 8, 16)
STATE = max(POOLW) - 1
EXPERTS, TOPK = 32, 4
CAP = 64
ROUNDS = -(-T // CAP)
STEPS = EXPERTS * ROUNDS
NTAB = STEPS + 2
FAR = float(2 ** 20)
NEG = -1e30
EPS = 1e-6
BUCKETS = 32
TOEP = 384


def buckets(dist):
    half = BUCKETS // 2
    n = np.maximum(dist, 1).astype(np.float32)
    large = half + (np.log(n / np.float32(half)) / np.float32(math.log(PAST / half))
                    * np.float32(BUCKETS - half)).astype(np.int32)
    return np.where(dist < half, dist, np.minimum(large, BUCKETS - 1))


def bias_rows(dist, add):
    d = np.asarray(dist)
    out = np.zeros((BUCKETS + 1, d.size), np.float32)
    out[buckets(np.clip(d, 0, PAST)), np.arange(d.size)] = 1.0
    out[BUCKETS] = add
    return out


def constants():
    dist = 255 - np.arange(TOEP)
    count = (dist <= 128).astype(int) + (dist % 4 == 0) + (dist % 16 == 0)
    ok = (dist >= 0) & (count > 0)
    toep = bias_rows(dist, np.where(ok, np.log(np.maximum(count, 1)), NEG))
    p = np.arange(P)
    window = [bias_rows(512 - 4 * p, 0.0), bias_rows(2048 - 16 * p, 0.0)]
    window += [bias_rows(128 + t - p, np.where(p >= t, 0.0, NEG)) for t in range(DEC_T)]
    key_t = np.arange(NS) % DEC_T
    fresh = [bias_rows(t - key_t, 0.0) for t in range(DEC_T)]
    kb, kt = np.arange(NS)[:, None] // DEC_T, np.arange(NS)[:, None] % DEC_T
    qb, qt = np.arange(NS)[None, :] // DEC_T, np.arange(NS)[None, :] % DEC_T
    fresh_mask = np.where((kb == qb) & (kt <= qt), np.where(kt == qt, math.log(3.0), 0.0), NEG)
    first = np.array([[1.0 / min(i + 1, w) for i in range(16)] for w in POOLW])
    n = np.arange(NTAB)
    col = np.arange(AW)
    own = ((p[:, None] // 32 == p[:, None] // 8 % 4) & (p[:, None] % 8 == col[None, :] // HD)).astype(np.float32)
    diag = np.concatenate([own, (p[:, None] // 32 == np.arange(DEC_T)[None, :]).astype(np.float32)], 1)
    xcol = np.arange(D)
    r, h_, t_ = p[:, None] // 32, p[:, None] % 32 // 4, p[:, None] % 4
    xown = (h_ == xcol[None, :] // XHD).astype(np.float32)
    c = np.arange(16)[None, :]
    xdiag = np.concatenate([xown, ((r == c // 4) & (t_ == c % 4) & (h_ < XH)).astype(np.float32)], 1)
    return {
        "c_diag": diag,
        "c_xdiag": xdiag,
        "c_bias": np.concatenate([toep] + window + fresh, 1).astype(np.float32),
        "c_fresh": fresh_mask.astype(np.float32),
        "c_first": np.tile(first.reshape(1, 64), (P, 1)).astype(np.float32),
        "c_ident": np.eye(P, dtype=np.float32),
        "c_before": (p[:, None] < p[None, :]).astype(np.float32),
        "c_iota": np.tile(np.arange(CAP, dtype=np.float32), (P, 1)),
        "c_expert": (np.arange(96)[:, None] % 32 == n[None, :] % 32).astype(np.float32),
    }


def build(nc, i, o):
    f32, bf16, u32, i32 = mybir.dt.float32, mybir.dt.bfloat16, mybir.dt.uint32, mybir.dt.int32
    ALU, ACT, AX = mybir.AluOpType, mybir.ActivationFunctionType, mybir.AxisListType
    ds = bass.ds
    ctx = ExitStack()
    with ctx:
        def sb(name, shape, dt=f32):
            return ctx.enter_context(nc.sbuf_tensor(name, shape, dt))

        def sem(name):
            return ctx.enter_context(nc.semaphore(name))

        toep_dram = nc.dram_tensor("toep_dram", (P, HEADS, TOEP), f32, kind="Internal").ap()
        y_dram = nc.dram_tensor("y_dram", (STEPS * CAP, D), f32, kind="Internal").ap()

        wide = sb("wide", [P, KC, 2 * D])
        slim = sb("slim", [P, KC, D])
        x = sb("x", [P, 3, D])
        hn = sb("hn", [P, 3, D])
        ta = sb("ta", [P, KC, T])
        tb = sb("tb", [P, KC, T])
        mkT = sb("mkT", [P, KC, NMEM])
        mv = sb("mv", [P, 2, D])
        att = sb("att", [P, 10112])
        scr = sb("scr", [P, 2048])
        ident = sb("ident", [P, P])
        iota = sb("iota", [P, CAP])
        ones = sb("ones", [P, P])
        gcol = sb("gcol", [P, 4, KC])
        small = sb("small", [P, 456])
        eps = sb("eps", [P, 1])
        meansq = sb("meansq", [P, 41])
        idx = sb("idx", [P, 3, 8], u32)
        rows = sb("rows", [P, 3, TOPK], u32)
        most = sb("most", [1, 1], i32)

        wf = wide[:, :, :].rearrange("p k n -> p (k n)")
        kwin = [wf[:, 4608 * s:4608 * s + 4608].rearrange("p (s n) -> p s n", n=AW) for s in range(2)]
        vwin = wf[:, 9216:13824].rearrange("p (s n) -> p s n", n=AW)
        prod = wf[:, 13824:15360].rearrange("p (s n) -> p s n", n=AW)
        cmem = [wf[:, 2048 * s:2048 * s + 2048].rearrange("p (m n) -> p m n", n=D) for s in range(8)]
        qn = att[:, 0:1536].rearrange("p (t n) -> p t n", n=AW)
        kn = att[:, 1536:3072].rearrange("p (t n) -> p t n", n=AW)
        vn = att[:, 3072:4608].rearrange("p (t n) -> p t n", n=AW)
        qkvn = att[:, 0:4608].rearrange("p (c t n) -> p c t n", c=3, n=AW)
        toep_sb = att[:, 0:3072].rearrange("p (h n) -> p h n", n=TOEP)
        qT = att[:, 4608:5760].rearrange("p (c n) -> p c n", n=T)
        kT = att[:, 5760:6912].rearrange("p (c n) -> p c n", n=T)
        UP = STATE + SEQ
        uP = att[:, 6912:6912 + 4 * UP].rearrange("p (g n) -> p g n", n=UP)
        bias = att[:, 8000:10048].rearrange("p (h n) -> p h n", n=SEQ)
        mvf = mv[:, :, :].rearrange("p t n -> p (t n)")
        dT = mvf[:, 0:1152].rearrange("p (g n) -> p g n", n=T)
        US = STATE + DEC_T
        uS = mvf[:, 1152:1152 + 4 * DEC_B * US].rearrange("p (g b n) -> p g b n", b=DEC_B, n=US)
        unew = mvf[:, 1760:1888].rearrange("p (g n) -> p g n", n=NS)
        mkTf = mkT[:, :, :].rearrange("p k n -> p (k n)")
        cb = mkTf[0:33, 0:TOEP + 10 * P]
        rb = mkTf[0:33, 1300:1308]
        wr = mkTf[:, 0:256].rearrange("p (k n) -> p k n", n=EXPERTS)
        before = mkTf[:, 256:384]
        rbrep = scr[0:33, 0:1024].rearrange("p (h n) -> p h n", n=P)
        state = scr[0:DEC_B * STATE, 1024:1536]
        wpool = scr[:, 1536:2048].rearrange("p (g n) -> p g n", n=P)
        sum_p = [scr[:, 0:UP], scr[:, UP:2 * UP]]
        sum_s = [scr[:, 600 + 152 * s:600 + 152 * s + 152].rearrange("p (b n) -> p b n", n=US) for s in range(2)]
        lg = [scr[:, 512 * s:512 * s + 512].rearrange("p (h n) -> p h n", n=NMEM) for s in range(2)]
        pT = [scr[:, 1024 + 512 * s:1536 + 512 * s].rearrange("p (c n) -> p c n", n=P) for s in range(2)]
        S_ = [small[:, 128 * s:128 * s + 96].rearrange("p (k t h) -> p k t h", k=3, t=DEC_T) for s in range(2)]
        bs = att[:, 10048:10048 + 64]
        bsw = sb("bsw", [P, 3, DEC_T, HEADS])
        bfr = sb("bfr", [NS, DEC_B, DEC_T, HEADS])
        pp = sb("pp", [P, 4, DEC_T, HEADS])
        pr = sb("pr", [P, 4, DEC_T, HEADS])
        fmask = sb("fmask", [NS, NS])
        cfirst = bs.rearrange("p (g n) -> p g n", n=16)
        pscale = sb("pscale", [P, 4])
        mx = small[:, 256:288]
        gm = small[:, 288:320]
        zs = small[:, 320:352]
        zz = small[:, 352:384]
        stat = small[:, 384:456]

        own = hn[:, 2, 0:AW + DEC_T]
        kept = wf[:, 15360:15872]
        ktm = [att[:, 2048 * s:2048 * s + 2048].rearrange("p (k n) -> p k n", n=NMEM) for s in range(2)]
        qm = att[:, 4608:6656]
        xown = scr[:, 0:D + 16]
        px = att[:, 4096:4352]
        pxT = att[:, 4608:5120].rearrange("p (m b n) -> p m b n", m=2, n=32)
        xkept = [wf[:, 12288 + 1024 * s:13312 + 1024 * s] for s in range(2)]
        logit = att[:, 4096:4192].rearrange("p (t n) -> p t n", n=EXPERTS)
        top = att[:, 4192:4216].rearrange("p (t n) -> p t n", n=8)
        idxf = att[:, 4216:4240].rearrange("p (t n) -> p t n", n=8)
        gate = sb("gate", [P, 3, TOPK])
        hot = att[:, 4240:4624].rearrange("p (t k n) -> p t k n", k=TOPK, n=EXPERTS)
        msk = att[:, 4624:4720].rearrange("p (t n) -> p t n", n=EXPERTS)
        gmat = att[:, 4720:4816].rearrange("p (t n) -> p t n", n=EXPERTS)
        posn = att[:, 4816:4912].rearrange("p (t n) -> p t n", n=EXPERTS)
        prodr = att[:, 4912:5296].rearrange("p (t k n) -> p t k n", k=TOPK, n=EXPERTS)
        slot = att[:, 5296:5308].rearrange("p (t n) -> p t n", n=TOPK)
        jump = att[:, 5308:5320].rearrange("p (t n) -> p t n", n=TOPK)
        rowf = att[:, 5320:5332].rearrange("p (t n) -> p t n", n=TOPK)
        gT = att[0:EXPERTS, 5336:5336 + T]
        brow = att[0:1, 5632:5664]
        cntf = att[0:1, 5664:5665]
        table = att[:, 5760:5760 + 3 * NTAB].rearrange("p (t n) -> p t n", n=NTAB)
        expert1 = att[0:96, 6260:6260 + NTAB]
        parts = att[0:96, 6912:7936].bitcast(bf16)
        braw = att[0:96, 8000:10048]
        bdn = scr[0:EXPERTS, 0:D]
        xe = att[:, 0:512].rearrange("p (k n) -> p k n", n=CAP)
        gc, uc, gu, sg = (att[:, 512 * s:512 * s + 512] for s in (1, 2, 3, 4))
        aT = att[:, 2560:3072].rearrange("p (j h n) -> p j h n", j=4, h=2)
        ye = att[:, 3072:3584]
        onehot = att[:, 3584:3776].rearrange("p (t n) -> p t n", n=CAP)
        pick = att[0:96, 3776:3808].bitcast(bf16)
        yk = [wf[:, D * s:D * s + D] for s in range(12)]
        gfin = wf[:, 12 * D:13 * D]
        xout = [wf[:, (13 + t) * D:(14 + t) * D] for t in range(3)]

        TURN = 7
        bank = [ctx.enter_context(nc.psum_tensor(f"bank{b}", [P, 512], f32)) for b in range(8)]
        sx_bank = bank[7]

        jobs = []

        def add(*name):
            jobs.append(name)

        add("bias_w"), add("bias_f")
        for h in range(HEADS):
            add("toep", h)
        for t in range(3):
            for h in range(2):
                add("tr1", t, h)
        for t in range(2):
            for c in range(3):
                add("qkv", t, c)
        add("qkv", 2)
        for c in range(4):
            add("u", c)
        for t in range(3):
            add("trq", t), add("trk", t)
        add("fresh", 0), add("fresh", 1)
        add("state"), add("utp"), add("uts")
        for g in range(4):
            add("pool", g)
        COPIES = [9, 1, 2, 2, 2]
        UNITS = [(hp, qt) for hp in range(4) for qt in range(2)]
        add("s", 0, 0), add("s", 0, 1)
        FILL = {(b, lot): [] for b in range(DEC_B) for lot in range(2)}
        for t in range(2):
            for h in range(2):
                FILL[0, t].append(("trm", t, h))
                FILL[1 + t, h].append(("mk", t, h))
                FILL[3, t].append(("trmk", t, h))
                FILL[4 + t, h].append(("mv", t, h))
        add("qb", 0, 0), add("qb", 0, 1)
        for b in range(DEC_B):
            add("qb", b, 2), add("pt", b)
            if b >= 2:
                add("pvt", b - 2)
            for f in FILL[b, 0]:
                add(*f)
            add("qb", b, 3), add("o", b)
            if b + 1 < DEC_B:
                add("s", b + 1, 0), add("s", b + 1, 1)
            if b + 1 < DEC_B:
                add("qb", b + 1, 0), add("qb", b + 1, 1)
            if b:
                add("pv", b - 1)
            for f in FILL[b, 1]:
                add(*f)
        add("pvt", DEC_B - 2), add("pv", DEC_B - 1), add("pvt", DEC_B - 1)
        add("out", 0, 0), add("out", 0, 1), add("out", 1, 0), add("out", 1, 1), add("out", 2)
        for b in range(2):
            for m in range(2):
                add("trck", b, m, 0), add("trck", b, m, 1)
        for t in range(3):
            add("tr2", t, 0), add("tr2", t, 1)
        for c in range(8):
            add("xq", c)
        for b in range(2, DEC_B):
            for m in range(2):
                add("trck", b, m, 0), add("trck", b, m, 1)
        XUNITS = [(hp, qt) for hp in range(2) for qt in range(2)]
        add("xs", 0)
        for u in range(4):
            if u + 1 < 4:
                add("xs", u + 1)
            add("xpt", u), add("xo_", u)
        add("xpts")
        for g in range(2):
            for h in range(2):
                add("pvx", g, h)
        for g in range(2):
            add("pvxt", g)
        add("xo", 0, 0), add("xo", 0, 1), add("xo", 1, 0), add("xo", 1, 1), add("xo", 2)
        for t in range(3):
            add("tr3", t, 0), add("tr3", t, 1)
        for t in range(3):
            add("route", t)
        for t in range(3):
            add("pos", t)
        add("count"), add("trg")
        for t in range(3):
            add("bd", t, 0), add("bd", t, 1)
        number = {name: n for n, name in enumerate(jobs)}
        assert len(number) == len(jobs)

        bank_full = [sem(f"bank_full{b}") for b in range(TURN)]
        bank_free = [sem(f"bank_free{b}") for b in range(TURN)]

        def place(name):
            n = number[name]
            return n % TURN, n // TURN

        def take(pe, *name):
            b, use = place(name)
            if use:
                pe.wait_ge(bank_free[b], use)
            return bank[b], bank_full[b]

        def product(eng, *name):
            b, use = place(name)
            eng.wait_ge(bank_full[b], use + 1)
            return bank[b], bank_free[b]

        def read_out(eng, *name):
            b, use = place(name)
            eng.wait_ge(bank_free[b], use + 1)

        loaded = {}

        def load(eng, name, out, in_):
            eng.dma_start(out, in_).then_inc(loaded[name], 16)

        for n in ("x0", "x1", "x2", "rel", "cbias", "cfresh", "cfirst", "ident", "before", "iota", "gcol", "wr",
                  "state", "wpool", "pscale", "toep", "mem", "expert", "diag", "xdiag", "braw0", "braw1", "braw2", "brow", "bdn",
                  "gfin"):
            loaded[n] = sem(f"loaded_{n}")
        wide_in = [sem(f"wide_in{k}") for k in range(KC)]
        slim_in = [sem(f"slim_in{k}") for k in range(KC)]
        wide_used = sem("wide_used")
        slim_used = sem("slim_used")
        k_in = [sem("k_in0"), sem("k_in1")]
        v_in = sem("v_in")
        ck_in = [sem(f"ck_in{s}") for s in range(4)]
        cv_in = [sem(f"cv_in{s}") for s in range(8)]
        toep_out = sem("toep_out")
        consts = sem("consts")
        squares = sem("squares")
        normed = sem("normed")
        rb_rep = sem("rb_rep")
        fresh_in = sem("fresh_in")
        pooled = sem("pooled")
        summed = sem("summed")
        expd = sem("expd")
        scaled = sem("scaled")
        pt_in = sem("pt_in")
        scored = sem("scored")
        gmax = sem("gmax")
        shifted = sem("shifted")
        sexp = sem("sexp")
        zpart = sem("zpart")
        zall = sem("zall")
        prob = sem("prob")
        xs_full, xs_part = sem("xs_full"), sem("xs_part")
        qm_in, xmax_in, xexp, xprob = (sem(n) for n in ("qm_in", "xmax_in", "xexp", "xprob"))
        parts_in = sem("parts_in")
        gexp = sem("gexp")
        gz = sem("gz")
        toph = sem("toph")
        hots = sem("hots")
        gmats = sem("gmats")
        tables = sem("tables")
        most_in = sem("most_in")
        stored = {n: sem(f"stored_{n}") for n in ("copies", "kv", "pool", "mk", "mv", "y")}
        dve_done = sem("dve_done")
        act_done = sem("act_done")
        pool_done = sem("pool_done")
        onehot_in, pick_in, xe_in, xg_full, gc_in, uc_in, gu_in, sg_in, a_in, at_full, at_in, y_read, y_stored = (
            sem(n) for n in ("onehot_in", "pick_in", "xe_in", "xg_full", "gc_in", "uc_in", "gu_in", "sg_in", "a_in", "at_full",
                             "at_in", "y_read", "y_stored"))
        gathered = [sem(f"gathered{n}") for n in range(3)]
        xsum = sem("xsum")
        fin = sem("fin")
        bank_g, bank_u, bank_t, bank_x, bank_y = bank[0], bank[1], bank[2], bank[3], bank[4]

        KEEP = PAST - DEC_T
        pieces = []
        for b in range(DEC_B):
            for src, dst in (("cache_k_win", "k_win_sample"), ("cache_v_win", "v_win_sample")):
                for h in range(2):
                    pieces.append(tuple(ap.rearrange("s h d -> (s h d)").rearrange("(c a n) -> c a n", c=2, a=32)[h]
                                        for ap in (o[dst][0, b, 0:KEEP], i[src][0, b, DEC_T:PAST])))

        def swap(ap):
            return ap.rearrange("p a b -> p b a")

        w_in = i["w_in"][0].rearrange("(k p) n -> k p n", p=P)

        def wch(name):
            return i[name][0].rearrange("(k p) n -> k p n", p=P)

        SLIM = ["w_xk", "w_xv", "w_out", "w_xq", "w_xo"]
        SLIM_LAST = [("mk", 1, 1), ("mv", 1, 1), ("out", 2), ("xq", 7), None]

        block = ctx.enter_context(nc.Block())

        @block.sync
        def _(sp):
            load(sp, "ident", ident[:, :], i["c_ident"])
            for t, (t0, n) in enumerate(TOK):
                src = i["x_prompt"][0, t0:t0 + n, :] if t < 2 else i["x_sample"].rearrange("b t d -> (b t) d")
                load(sp, f"x{t}", x[0:n, t, :], src)
            load(sp, "rel", rb[0:BUCKETS, :], i["rel_bias"])
            load(sp, "cbias", cb[:, 0:TOEP + 6 * P + 4 * NS], i["c_bias"])
            load(sp, "cfresh", fmask[:, :], i["c_fresh"])
            load(sp, "gcol", gcol[:, :, :], i["g_all"])
            for k in range(KC):
                sp.dma_start(wide[:, k, :], w_in[k]).then_inc(wide_in[k], 16)
            load(sp, "cfirst", bs, i["c_first"])
            load(sp, "state", state, i["state_pool"][0].rearrange("b s d -> (b s) d"))
            load(sp, "wpool", wpool, i["w_pool"][0].rearrange("g c e -> c g e"))
            load(sp, "pscale", pscale[:, :], i["pool_scale_col"])
            load(sp, "iota", iota[:, :], i["c_iota"])

            def copy(n):
                for _ in range(n):
                    dst, src = pieces.pop(0)
                    sp.dma_start(dst, src).then_inc(stored["copies"], 16)

            def slim_round(r):
                if r:
                    b, use = place(SLIM_LAST[r - 1])
                    sp.wait_ge(bank_full[b], use + 1)
                src = wch(SLIM[r])
                for k in range(KC):
                    sp.dma_start(slim[:, k, :], src[k]).then_inc(slim_in[k], 16)

            sp.wait_ge(toep_out, 16)
            skew = bass.AP(toep_dram.tensor, P - 1, [[HEADS * TOEP - 1, P], [TOEP, HEADS], [1, SEQ]])
            load(sp, "toep", bias, skew)
            slim_round(0)
            b, use = place(("tr1", 2, 1))
            sp.wait_ge(bank_full[b], use + 1)
            load(sp, "mem", hn[:, 0:2, :], i["mem_prompt"][0].rearrange("(t p) d -> p t d", p=P))
            copy(COPIES[0])
            sp.wait_ge(stored["pool"], 48)
            load(sp, "diag", own, i["c_diag"])

            def window(dst, cache, b, s):
                src = cache[0, b]
                sp.dma_start(dst[:, 0:4, :], src[PAST - 512:PAST].rearrange("(p t) h d -> p t (h d)", p=P)).then_inc(s, 16)
                sp.dma_start(dst[:, 4:8, :], src.rearrange("(p t) h d -> p t (h d)", p=P)[:, 0:4, :]).then_inc(s, 16)
                sp.dma_start(dst[:, 8, :], src[PAST - P:PAST].rearrange("p h d -> p (h d)")).then_inc(s, 16)

            b, use = place(("u", 3))
            sp.wait_ge(bank_full[b], use + 1)
            window(kwin[0], i["cache_k_win"], 0, k_in[0])
            window(vwin, i["cache_v_win"], 0, v_in)
            window(kwin[1], i["cache_k_win"], 1, k_in[1])
            for b in range(1, DEC_B):
                if b + 1 < DEC_B:
                    sp.wait_ge(scored, b)
                    window(kwin[(b + 1) % 2], i["cache_k_win"], b + 1, k_in[(b + 1) % 2])
                bb, use = place(("pv", b - 1))
                sp.wait_ge(bank_full[bb], use + 1)
                window(vwin, i["cache_v_win"], b, v_in)
                if b == 2:
                    slim_round(1)
                elif b == 5:
                    slim_round(2)
                else:
                    copy(COPIES[1])
            bb, use = place(("pv", DEC_B - 1))
            sp.wait_ge(bank_full[bb], use + 1)
            sp.wait_ge(scored, DEC_B)

            def cache_mem(dst, name, b, s):
                sp.dma_start(dst, i[name][0, b].rearrange("(m p) h d -> p m (h d)", p=P)).then_inc(s, 16)

            for b in range(4):
                cache_mem(cmem[b], "cache_mem_k", b, ck_in[b])
            bb, use = place(("pvt", DEC_B - 1))
            sp.wait_ge(bank_full[bb], use + 1)
            for b in range(4):
                cache_mem(cmem[4 + b], "cache_mem_v", b, cv_in[b])
            for s in range(3):
                load(sp, f"braw{s}", braw[32 * s:32 * s + 32, :], i["b_gate_up"][0])
            copy(COPIES[2])
            slim_round(3)
            for b in range(4, DEC_B):
                bb, use = place(("trck", b - 4, 1, 1))
                sp.wait_ge(bank_full[bb], use + 1)
                cache_mem(cmem[b - 4], "cache_mem_k", b, ck_in[b - 4])
            for b in range(4, DEC_B):
                bb, use = place(("trck", b, 1, 1))
                sp.wait_ge(bank_full[bb], use + 1)
                cache_mem(cmem[b - 4], "cache_mem_v", b, cv_in[b])
            slim_round(4)
            copy(COPIES[3])
            read_out(sp, "xpt", 3)
            b, use = place(("xo_", 3))
            sp.wait_ge(bank_full[b], use + 1)
            load(sp, "xdiag", xown, i["c_xdiag"])
            load(sp, "before", before, i["c_before"])
            load(sp, "wr", wr, i["w_router"][0].rearrange("(k p) n -> p k n", p=P))
            b, use = place(("pvxt", 1))
            sp.wait_ge(bank_full[b], use + 1)
            load(sp, "bdn", bdn, i["b_down"][0])
            load(sp, "brow", brow, i["b_router"])
            load(sp, "expert", expert1, i["c_expert"])

            def step0():
                sp.wait_ge(wide_used, 8)
                for k in range(KC):
                    sp.dma_start(wide[:, k, :], i["w_gate_up"][0, 0, k * P:(k + 1) * P, :]).then_inc(wide_in[k], 16)
                copy(COPIES[4])
                sp.wait_ge(slim_used, 8)
                for k in range(KC):
                    sp.dma_start(slim[:, k, :], i["w_down"][0, 0, k * P:(k + 1) * P, :]).then_inc(slim_in[k], 16)

            def step(e, n):
                for k in range(KC):
                    sp.wait_ge(wide_used, 8 * n + k + 1)
                    sp.dma_start(wide[:, k, :], i["w_gate_up"][0, ds(e, 1), k * P:(k + 1) * P, :]
                                 .rearrange("e p n -> p (e n)")).then_inc(wide_in[k], 16)
                for k in range(KC):
                    sp.wait_ge(slim_used, 8 * n + k + 1)
                    sp.dma_start(slim[:, k, :], i["w_down"][0, ds(e, 1), k * P:(k + 1) * P, :]
                                 .rearrange("e p n -> p (e n)")).then_inc(slim_in[k], 16)

            step0()
            copy(len(pieces))
            with sp.Fori(1, EXPERTS) as e:
                step(e, e)
            sp.wait_ge(most_in, 1)
            crowd = sp.value_load(most[0:1, 0:1], min_val=0, max_val=T)
            with sp.If(crowd > CAP):
                with sp.Fori(1, ROUNDS) as j:
                    with sp.Fori(0, EXPERTS) as e:
                        step(e, j * EXPERTS + e)
            sp.wait_ge(wide_used, 8 * EXPERTS + 8)
            with sp.If(crowd > CAP):
                sp.wait_ge(wide_used, 8 * STEPS + 8)
            load(sp, "gfin", gfin, i["g_final_rows"])
            for t in range(3):
                n = TOK[t][1]
                sp.wait_ge(fin, t + 1)
                dst = o["y_prompt"][0, TOK[t][0]:TOK[t][0] + n, :] if t < 2 else o["y_sample"].rearrange("b t d -> (b t) d")
                sp.dma_start(dst, xout[t][0:n, :]).then_inc(stored["y"], 16)
            sp.wait_ge(stored["y"], 48)
            sp.wait_ge(stored["copies"], 16 * 4 * DEC_B)

        @block.gpsimd
        def _(pool):
            step = [0]

            def link(ins):
                step[0] += 1
                ins.then_inc(pool_done, 1)
                pool.wait_ge(pool_done, step[0])

            nc.gpsimd.memset(ones[:, :], 1.0).then_inc(consts, 1)
            pool.dma_start(o["pool_sample"][0, :, 0:STATE - DEC_T, :], i["state_pool"][0, :, DEC_T:STATE, :]).then_inc(stored["pool"], 16)
            read_out(pool, "toep", HEADS - 1)
            read_out(pool, "toep", HEADS - 2)
            pool.dma_start(toep_dram, toep_sb).then_inc(toep_out, 16)
            for c, (kp, ks) in ((1, ("k_win_prompt", "k_win_sample")), (2, ("v_win_prompt", "v_win_sample"))):
                read_out(pool, "qkv", 0, c), read_out(pool, "qkv", 1, c), read_out(pool, "qkv", 2)
                pool.dma_start(o[kp][0, 0].rearrange("(t p) h d -> p t (h d)", p=P), qkvn[:, c, 0:2, :]).then_inc(stored["kv"], 16)
                pool.dma_start(o[ks][0, :, KEEP:PAST].rearrange("b t h d -> b t (h d)"),
                               qkvn[0:NS, c, 2, :]).then_inc(stored["kv"], 16)
            read_out(pool, "utp")
            pool.dma_start(o["pool_prompt"][0, 0], hn[0:STATE, 2, 0:512]).then_inc(stored["pool"], 16)
            read_out(pool, "uts")
            pool.dma_start(o["pool_sample"][0, :, STATE - DEC_T:STATE, :], hn[0:NS, 2, 512:1024]).then_inc(stored["pool"], 16)
            for b in range(DEC_B):
                pool.wait_ge(scored, b + 1)
                nc.gpsimd.partition_all_reduce(gm, mx, P, bass.bass_isa.ReduceOp.max).then_inc(gmax, 1)
                pool.wait_ge(zpart, b + 1)
                nc.gpsimd.partition_all_reduce(zz, zs, P, bass.bass_isa.ReduceOp.add).then_inc(zall, 1)
                if b in (3, 4):
                    if b == 3:
                        for t in range(2):
                            for h in range(2):
                                read_out(pool, "mk", t, h)
                        pool.dma_start(o["mem_k_prompt"][0, 0].rearrange("(t p) h d -> p t (h d)", p=P),
                                       hn[:, 0:2, :]).then_inc(stored["mk"], 16)
            for t in range(2):
                for h in range(2):
                    read_out(pool, "mv", t, h)
            pool.dma_start(o["mem_v_prompt"][0, 0].rearrange("(t p) h d -> p t (h d)", p=P), mv[:, :, :]).then_inc(stored["mv"], 16)
            for s in range(3):
                pool.wait_ge(loaded[f"braw{s}"], 16)
            link(nc.gpsimd.tensor_copy(parts, braw))
            for s in (1, 2):
                link(nc.gpsimd.tensor_tensor(braw[32 * s:32 * s + 32, :], braw[32 * s:32 * s + 32, :],
                                             parts[32 * s:32 * s + 32, :], ALU.subtract))
            for s in (1, 2):
                link(nc.gpsimd.tensor_copy(parts[32 * s:32 * s + 32, :], braw[32 * s:32 * s + 32, :]))
            link(nc.gpsimd.tensor_tensor(braw[64:96, :], braw[64:96, :], parts[64:96, :], ALU.subtract))
            nc.gpsimd.tensor_copy(parts[64:96, :], braw[64:96, :]).then_inc(parts_in, 1)
            pool.wait_ge(most_in, 1)
            crowd = pool.value_load(most[0:1, 0:1], min_val=0, max_val=T)
            pool.wait_ge(y_stored, 32 * EXPERTS + 1)
            pool.wait_ge(wide_used, 8 * EXPERTS + 8)

            def gather(given):
                for t in range(3):
                    n = TOK[t][1]
                    for k in range(TOPK):
                        pool.indirect_dma_start(yk[4 * t + k][0:n, :], None, given,
                                                bass.IndirectOffsetOnAxis(ap=rows[0:n, t, k:k + 1], axis=0)).then_inc(gathered[t], 16)

            pool.wait_ge(tables, 1)
            with pool.If(crowd > CAP):
                pool.wait_ge(y_stored, 32 * STEPS + 1)
                pool.wait_ge(wide_used, 8 * STEPS + 8)
                gather(y_dram)
            with pool.Else():
                gather(y_dram[0:EXPERTS * CAP, :])
            pool.wait_ge(stored["kv"], 64)
            pool.wait_ge(stored["pool"], 48)
            pool.wait_ge(stored["mk"], 16)
            pool.wait_ge(stored["mv"], 16)

        @block.scalar
        def _(act):
            A = nc.scalar.activation
            step = [0]

            def link(ins):
                step[0] += 1
                ins.then_inc(act_done, 1)
                act.wait_ge(act_done, step[0])

            def root(col, n, src, junk, wait_eps=False):
                link(A(junk, src, ACT.Square, accum_out=meansq[0:n, col:col + 1]))
                A(stat[0:n, col:col + 1], meansq[0:n, col:col + 1], ACT.Sqrt, bias=eps[0:n, :], scale=1.0 / D).then_inc(squares, 1)

            act.wait_ge(consts, 2)
            for t, (t0, n) in enumerate(TOK):
                act.wait_ge(loaded[f"x{t}"], 16)
                root(t, n, x[0:n, t, :], hn[0:n, t, :])
            for h in range(HEADS):
                ps, s = product(act, "toep", h)
                A(toep_sb[:, h, :], ps[:, 0:TOEP], ACT.Copy).then_inc(s, 1)
            act.wait_ge(toep_out, 16)
            for t in range(2):
                for c in range(3):
                    ps, s = product(act, "qkv", t, c)
                    A(qkvn[:, c, t, :], ps[:, :], ACT.Copy, scale=HD ** -0.5 if c == 0 else 1.0).then_inc(s, 1)
            ps, s = product(act, "qkv", 2)
            for c in range(3):
                ins = A(qkvn[0:NS, c, 2, :], ps[NS * c:NS * c + NS, :], ACT.Copy, scale=HD ** -0.5 if c == 0 else 1.0)
            ins.then_inc(s, 1)
            for c in range(4):
                ps, s = product(act, "u", c)
                A(uP[:, c, STATE:UP], ps[:, 0:SEQ], ACT.Copy)
                link(A(unew[:, c, :], ps[:, SEQ:T], ACT.Copy))
                A(uS[:, c, :, STATE:US], ps[:, SEQ:T].rearrange("p (b t) -> p b t", t=DEC_T), ACT.Copy).then_inc(s, 1)
            for t, (t0, n) in enumerate(TOK):
                for name, dst in (("trq", qT), ("trk", kT)):
                    ps, s = product(act, name, t)
                    A(dst[:, :, t0:t0 + n], ps[:, :].rearrange("p (c n) -> p c n", n=P)[:, :, 0:n], ACT.Copy).then_inc(s, 1)
            ps, s = product(act, "state")
            A(uS[:, :, :, 0:STATE], ps[:, 0:480].rearrange("p (g b n) -> p g b n", g=4, n=STATE), ACT.Copy).then_inc(s, 1)
            ps, s = product(act, "utp")
            A(hn[0:STATE, 2, 0:512], ps[0:STATE, :], ACT.Copy).then_inc(s, 1)
            ps, s = product(act, "uts")
            A(hn[0:NS, 2, 512:1024], ps[0:NS, :], ACT.Copy).then_inc(s, 1)
            act.wait_ge(loaded["pscale"], 16)
            for g in range(4):
                ps, s = product(act, "pool", g)
                A(tb[:, 4 + g, :], ps[:, 0:T], ACT.Copy, scale=pscale[:, g:g + 1]).then_inc(s, 1)
            def unit_exp(u):
                nk = P * (UNITS[u][1] + 1)
                act.wait_ge(summed, 2 * u + 2)
                for h in range(2):
                    A(lg[u % 2][:, h, 0:nk], lg[u % 2][:, h, 0:nk], ACT.Exp, bias=stat[:, 8 + 4 * (u % 2) + h:9 + 4 * (u % 2) + h],
                      accum_out=stat[:, 10 + 4 * (u % 2) + h:11 + 4 * (u % 2) + h]).then_inc(expd, 1)

            def unit_pt(u):
                w = 2 * P * (UNITS[u][1] + 1)
                ps, s = product(act, "pt", u)
                A(pT[u % 2].rearrange("p c n -> p (c n)")[:, 0:w], ps[:, 0:w], ACT.Copy).then_inc(s, 1)

            def unit_out(u):
                hp, qt = UNITS[u]
                ps, s = product(act, "o", u)
                A(tb[:, hp, P * qt:P * qt + P], ps[:, 0:P], ACT.Copy).then_inc(s, 1)

            act.wait_ge(loaded["mem"], 16)
            for t in range(2):
                root(3 + t, P, hn[:, t, :], mkTf[:, 0:D] if t == 0 else mkTf[:, D:2 * D])

            def fill(name):
                kind, t, h = name
                ps, s = product(act, *name)
                if kind == "trm":
                    for c in range(4):
                        ins = A(ta[:, 4 * h + c, P * t:P * t + P], ps[:, P * c:P * c + P], ACT.Copy,
                                scale=gcol[:, 1, 4 * h + c:4 * h + c + 1])
                    ins.then_inc(s, 1)
                elif kind == "mk":
                    A(hn[:, t, 512 * h:512 * h + 512], ps[:, :], ACT.Copy).then_inc(s, 1)
                elif kind == "trmk":
                    A(mkT[:, 4 * h:4 * h + 4, P * t:P * t + P], ps[:, :].rearrange("p (c n) -> p c n", n=P), ACT.Copy).then_inc(s, 1)
                else:
                    A(mv[:, t, 512 * h:512 * h + 512], ps[:, :], ACT.Copy).then_inc(s, 1)

            def sample_exp(b):
                act.wait_ge(shifted, b + 1)
                A(pr[:, :, :, :], pp[:, :, :, :], ACT.Exp).then_inc(sexp, 1)

            def sample_out(b):
                ps, s = product(act, "pvt", b)
                c0 = SEQ + DEC_T * b
                A(tb[:, 0:4, c0:c0 + DEC_T], ps[:, 0:16].rearrange("p (c t) -> p c t", t=DEC_T), ACT.Copy).then_inc(s, 1)

            unit_exp(0)
            for b in range(DEC_B):
                unit_pt(b)
                if b >= 2:
                    sample_out(b - 2)
                if b:
                    sample_exp(b - 1)
                for f in FILL[b, 0]:
                    fill(f)
                unit_out(b)
                if b + 1 < DEC_B:
                    unit_exp(b + 1)
                for f in FILL[b, 1]:
                    fill(f)
            sample_out(DEC_B - 2)
            sample_exp(DEC_B - 1)
            sample_out(DEC_B - 1)
            act.wait_ge(stored["mk"], 16)
            act.wait_ge(stored["pool"], 48)
            for t, (t0, n) in enumerate(TOK):
                for part in ([("out", t, 0), ("out", t, 1)] if t < 2 else [("out", 2)]):
                    read_out(act, *part)
                root(5 + t, n, x[0:n, t, :], hn[0:n, t, :])
            def keys_in(b):
                for m in range(2):
                    ps, s = product(act, "trck", b, m, 0)
                    A(ktm[b % 2][:, 0:4, P * m:P * m + P], ps[:, :].rearrange("p (c n) -> p c n", n=P), ACT.Copy).then_inc(s, 1)

            act.wait_ge(stored["kv"], 64)
            keys_in(0), keys_in(1)
            for c in range(8):
                ps, s = product(act, "xq", c)
                A(tb[:, c, :], ps[:, 0:T], ACT.Copy, scale=XHD ** -0.5).then_inc(s, 1)
            for b in range(2, DEC_B):
                act.wait_ge(xs_part, b - 1)
                keys_in(b)
            act.wait_ge(xmax_in, 1)
            A(px, sx_bank[:, 0:NMEM], ACT.Exp, bias=stat[:, 40:41], accum_out=stat[:, 41:42]).then_inc(xexp, 1)
            for u, (hp, qt) in enumerate(XUNITS):
                act.wait_ge(summed, 17 + u)
                ps, _ = product(act, "xs", u)
                for h in range(2):
                    ins = A(lg[u % 2][:, h, :], ps[:, 256 * h:256 * h + 256], ACT.Exp, bias=stat[:, 8 + 4 * (u % 2) + h:9 + 4 * (u % 2) + h],
                            accum_out=stat[:, 10 + 4 * (u % 2) + h:11 + 4 * (u % 2) + h])
                    if h == 0:
                        ins.then_inc(expd, 1)
                    else:
                        b_, _u = place(("xs", u))
                        ins.then_inc(bank_free[b_], 1)
                ps, s = product(act, "xpt", u)
                A(pT[u % 2].rearrange("p c n -> p (c n)"), ps[:, :], ACT.Copy).then_inc(s, 1)
                ps, s = product(act, "xo_", u)
                A(ta[:, 4 * hp:4 * hp + 4, P * qt:P * qt + P], ps[:, :].rearrange("p (c n) -> p c n", n=P), ACT.Copy).then_inc(s, 1)
            ps, s = product(act, "xpts")
            for m in range(2):
                ins = A(pxT[:, m, :, 0:16].rearrange("p b (h t) -> p b h t", t=DEC_T),
                        ps[:, P * m:P * m + P].rearrange("p (h b t) -> p b h t", b=DEC_B, t=DEC_T), ACT.Copy)
            ins.then_inc(s, 1)
            for g in range(2):
                ps, s = product(act, "pvxt", g)
                A(ta[:, :, SEQ + 16 * g:SEQ + 16 * g + 16], ps[:, 0:128].rearrange("p (c n) -> p c n", n=16), ACT.Copy).then_inc(s, 1)
            for t, (t0, n) in enumerate(TOK):
                for part in ([("xo", t, 0), ("xo", t, 1)] if t < 2 else [("xo", 2)]):
                    read_out(act, *part)
                root(16 + t, n, x[0:n, t, :], hn[0:n, t, :])
            act.wait_ge(toph, 1)
            for t, (t0, n) in enumerate(TOK):
                A(gate[0:n, t, :], top[0:n, t, 0:4], ACT.Exp, bias=stat[0:n, 20 + t:21 + t], accum_out=stat[0:n, 24 + t:25 + t]).then_inc(gexp, 1)
            ps, s = product(act, "trg")
            A(gT, ps[0:EXPERTS, 0:T], ACT.Copy).then_inc(s, 1)
            act.wait_ge(most_in, 1)
            crowd = act.value_load(most[0:1, 0:1], min_val=0, max_val=T)
            for name in [("bd", t, h) for t in range(3) for h in range(2)]:
                read_out(act, *name)
            act.sem_inc(y_read, 1)
            act.sem_inc(y_stored, 1)

            def step_(n):
                act.wait_ge(gc_in, n + 1)
                A(sg, gc, ACT.Sigmoid, scale=1.702).then_inc(sg_in, 1)
                act.wait_ge(at_full, n + 1)
                A(aT.rearrange("p j h n -> p (j h n)"), bank_t[:, :], ACT.Copy).then_inc(at_in, 1)
                act.wait_ge(slim_used, 8 * n + 16)
                act.wait_ge(y_stored, 32 * n + 1)
                A(ye, bank_y[:, :], ACT.Copy).then_inc(y_read, 1)
                act.wait_ge(y_read, n + 2)
                for h in range(2):
                    act.dma_start(y_dram[ds(n * CAP, CAP), 512 * h:512 * h + 512], ye[64 * h:64 * h + 64, :]).then_inc(y_stored, 16)

            with act.Fori(0, EXPERTS) as n:
                step_(n)
            with act.If(crowd > CAP):
                with act.Fori(1, ROUNDS) as j:
                    with act.Fori(0, EXPERTS) as e:
                        step_(j * EXPERTS + e)
            for t, (t0, n) in enumerate(TOK):
                act.wait_ge(xsum, t + 1)
                root(32 + t, n, x[0:n, t, :], hn[0:n, t, :])

        @block.vector
        def _(dve):
            V = nc.vector
            step = [0]

            def link(ins):
                step[0] += 1
                ins.then_inc(dve_done, 1)
                dve.wait_ge(dve_done, step[0])

            def inverse_root(col, n, count):
                dve.wait_ge(squares, count)
                r, v, w = stat[0:n, col:col + 1], meansq[0:n, col:col + 1], meansq[0:n, 40:41]
                V.tensor_scalar(v, v, 1.0 / D, EPS, ALU.mult, ALU.add)
                link(V.reciprocal(r, r))
                link(V.tensor_tensor(w, r, r, ALU.mult))
                link(V.tensor_tensor(w, w, v, ALU.mult))
                link(V.tensor_scalar(w, w, -0.5, 1.5, ALU.mult, ALU.add))
                link(V.tensor_tensor(r, r, w, ALU.mult))

            def norm(col, n, src, dst, count):
                inverse_root(col, n, count)
                V.tensor_scalar(dst, src, stat[0:n, col:col + 1], None, ALU.mult).then_inc(normed, 1)

            def gained(name, dst, g):
                for t, (t0, n) in enumerate(TOK):
                    for h in range(2):
                        ps, s = product(dve, name, t, h)
                        V.tensor_tensor(dst[:, 4 * h:4 * h + 4, t0:t0 + n], ps[:, :].rearrange("p (c n) -> p c n", n=P)[:, :, 0:n],
                                        gcol[:, g, 4 * h:4 * h + 4].unsqueeze(2).broadcast_to([P, 4, n]), ALU.mult).then_inc(s, 1)

            V.memset(eps[:, :], EPS).then_inc(consts, 1)
            V.memset(uP[:, :, 0:STATE], 0.0)
            V.memset(pp[:, 3, :, :], NEG)
            link(V.memset(rb[32:33, :], 1.0))
            dve.wait_ge(loaded["rel"], 16)
            V.tensor_copy(rbrep, rb.unsqueeze(2).broadcast_to([33, HEADS, P])).then_inc(rb_rep, 1)
            for t, (t0, n) in enumerate(TOK):
                norm(t, n, x[0:n, t, :], hn[0:n, t, :], t + 1)
            ps, s = product(dve, "bias_w")
            V.tensor_copy(bsw[:, :, :, :].rearrange("p k t h -> p (k t h)"), ps[:, 0:96]).then_inc(s, 1)
            ps, s = product(dve, "bias_f")
            dve.wait_ge(loaded["cfresh"], 16)
            for b in range(DEC_B):
                ins = V.tensor_tensor(bfr[:, b, :, :], ps[0:NS, 0:32].rearrange("p (t h) -> p t h", h=HEADS),
                                      fmask[:, 4 * b:4 * b + 4].unsqueeze(2).broadcast_to([NS, DEC_T, HEADS]), ALU.add)
            ins.then_inc(s, 1)
            dve.wait_ge(loaded["gcol"], 16)
            gained("tr1", ta, 0)
            for h in range(2):
                ps, s = product(dve, "fresh", h)
                dst = bfr[:, :, :, :].rearrange("p b t (c h) -> p h c (b t)", h=2)[:, h]
                V.tensor_tensor(dst, dst, ps[0:NS, 0:128].rearrange("p (c q) -> p c q", q=NS), ALU.add).then_inc(s, 1)
            dve.wait_ge(loaded["cfirst"], 16)
            for c in range(4):
                read_out(dve, "u", c)
            read_out(dve, "state")
            for g, w in enumerate(POOLW):
                sp_, ss_ = uP[:, g, :], uS[:, g]
                m, turn = 1, 0
                while m < w:
                    dp, dss = sum_p[turn], sum_s[turn]
                    V.tensor_tensor(dp[:, 2 * m - 1:UP], sp_[:, 2 * m - 1:UP], sp_[:, m - 1:UP - m], ALU.add)
                    link(V.tensor_tensor(dss[:, :, 2 * m - 1:US], ss_[:, :, 2 * m - 1:US], ss_[:, :, m - 1:US - m], ALU.add))
                    sp_, ss_ = dp, dss
                    m, turn = 2 * m, 1 - turn
                V.scalar_tensor_tensor(out=dT[:, g, 0:SEQ], in0=sp_[:, STATE:UP], scalar=1.0 / w, in1=uP[:, g, STATE:UP],
                                       op0=ALU.mult, op1=ALU.subtract)
                V.scalar_tensor_tensor(out=dT[:, g, SEQ:T].rearrange("p (b t) -> p b t", t=DEC_T), in0=ss_[:, :, STATE:US], scalar=1.0 / w,
                                       in1=uS[:, g, :, STATE:US], op0=ALU.mult, op1=ALU.subtract)
                link(V.tensor_tensor(stat[:, 48:64], sp_[:, STATE:STATE + 16], cfirst[:, g, :], ALU.mult))
                link(V.tensor_tensor(dT[:, g, 0:16], stat[:, 48:64], uP[:, g, STATE:STATE + 16], ALU.subtract))
                dve.sem_inc(pooled, 1)
            dve.wait_ge(loaded["toep"], 16)

            def logits(u):
                hp, qt = UNITS[u]
                nk = P * (qt + 1)
                if u >= 2:
                    b_, use = place(("pt", u - 2))
                    dve.wait_ge(bank_full[b_], use + 1)
                for h in range(2):
                    ps, s = product(dve, "s", u, h)
                    V.tensor_tensor(lg[u % 2][:, h, 0:nk], ps[:, 0:nk], bias[:, 2 * hp + h, SEQ - nk:SEQ], ALU.add).then_inc(s, 1)
                for h in range(2):
                    read_out(dve, "s", u, h)
                    c = 8 + 4 * (u % 2) + h
                    V.tensor_reduce(stat[:, c:c + 1], lg[u % 2][:, h, 0:nk], AX.X, ALU.max, negate=True).then_inc(summed, 1)

            def share(u, n, nk):
                c = 10 + 4 * (u % 2)
                link(V.reciprocal(stat[:, c:c + 2], stat[:, c:c + 2]))
                V.tensor_tensor(lg[u % 2][:, :, 0:nk], lg[u % 2][:, :, 0:nk],
                                stat[:, c:c + 2].unsqueeze(2).broadcast_to([P, 2, nk]), ALU.mult).then_inc(scaled, 1)

            for g in range(4):
                b_, use = place(("pool", g))
                dve.wait_ge(bank_full[b_], use + 1)
            logits(0)
            for t in range(2):
                norm(3 + t, P, hn[:, t, :], hn[:, t, :], 4 + t)

            def shift(b):
                dve.wait_ge(gmax, b + 1)
                s = S_[b % 2]
                V.tensor_tensor(pp[:, 0:3, :, :].rearrange("p k t h -> p k (t h)"), s.rearrange("p k t h -> p k (t h)"),
                                gm.unsqueeze(1).broadcast_to([P, 3, 32]), ALU.subtract)
                link(V.tensor_tensor(pp[0:NS, 3, :, :].rearrange("p t h -> p (t h)"), bfr[:, b, :, :].rearrange("p t h -> p (t h)"),
                                     gm[0:NS, :], ALU.subtract))
                dve.sem_inc(shifted, 1)

            def sums(b):
                dve.wait_ge(sexp, b + 1)
                V.tensor_reduce(zs, pr[:, :, :, :].rearrange("p k t h -> p (t h) k"), AX.X, ALU.add).then_inc(zpart, 1)

            def shares(b):
                dve.wait_ge(zall, b + 1)
                link(V.reciprocal(zz, zz))
                V.tensor_tensor(pr[:, :, :, :].rearrange("p k t h -> p k (t h)"), pr[:, :, :, :].rearrange("p k t h -> p k (t h)"),
                                zz.unsqueeze(1).broadcast_to([P, 4, 32]), ALU.mult).then_inc(prob, 1)

            def keep(b):
                if b:
                    b_, use = place(("pvt", b - 1))
                    dve.wait_ge(bank_full[b_], use + 1)
                else:
                    dve.wait_ge(loaded["diag"], 16)
                ps, s = product(dve, "pv", b)
                V.tensor_tensor(kept, ps[:, :], own[:, 0:AW], ALU.mult).then_inc(s, 1)

            for b in range(DEC_B):
                dve.wait_ge(expd, 2 * b + 2)
                share(b, b + 1, P * (UNITS[b][1] + 1))
                dve.wait_ge(k_in[b % 2], 48 * (b // 2 + 1))
                kw = kwin[b % 2]
                for t in range(DEC_T):
                    ps, s = product(dve, "qb", b, t)
                    pair = kw[:, 0:8, :].rearrange("p (k s) n -> p k s n", k=2)[:, :, t, :]
                    V.tensor_tensor(prod[:, 0:2, :], pair, ps[:, :].unsqueeze(1).broadcast_to([P, 2, AW]), ALU.mult)
                    V.tensor_tensor(prod[:, 2, :], kw[:, 8, :], ps[:, :], ALU.mult).then_inc(s, 1)
                    read_out(dve, "qb", b, t)
                    link(V.tensor_reduce(S_[b % 2][:, :, t, :], prod.rearrange("p k (h d) -> p k h d", d=HD), AX.X, ALU.add))
                    if b and t < 3:
                        (shift, sums, shares)[t](b - 1)
                    if b >= 2 and t == 0:
                        keep(b - 2)
                    if t == 2 and b + 1 < DEC_B:
                        logits(b + 1)
                s = S_[b % 2]
                link(V.tensor_tensor(s, s, bsw[:, :, :, :], ALU.add))
                link(V.tensor_reduce(mx, s.rearrange("p k t h -> p (t h) k"), AX.X, ALU.max))
                V.tensor_tensor(mx[0:NS, :], mx[0:NS, :], bfr[:, b, :, :].rearrange("p t h -> p (t h)"), ALU.max).then_inc(scored, 1)
            shift(DEC_B - 1), keep(DEC_B - 2), sums(DEC_B - 1), shares(DEC_B - 1), keep(DEC_B - 1)

            def residual(name):
                for t in range(2):
                    for h in range(2):
                        ps, s = product(dve, name, t, h)
                        dst = x[:, t, 512 * h:512 * h + 512]
                        V.tensor_tensor(dst, dst, ps[:, :], ALU.add).then_inc(s, 1)
                if name == "bd":
                    for h in range(2):
                        ps, s = product(dve, name, 2, h)
                        dst = x[0:NS, 2, 512 * h:512 * h + 512]
                        V.tensor_tensor(dst, dst, ps[0:NS, :], ALU.add).then_inc(s, 1)
                    return
                ps, s = product(dve, name, 2)
                for h in range(2):
                    dst = x[0:NS, 2, 512 * h:512 * h + 512]
                    ins = V.tensor_tensor(dst, dst, ps[NS * h:NS * h + NS, :], ALU.add)
                ins.then_inc(s, 1)

            residual("out")
            for t, (t0, n) in enumerate(TOK):
                norm(5 + t, n, x[0:n, t, :], hn[0:n, t, :], 6 + t)
            dve.wait_ge(stored["kv"], 64)

            def keys_in(b):
                for m in range(2):
                    ps, s = product(dve, "trck", b, m, 1)
                    V.tensor_copy(ktm[b % 2][:, 4:8, P * m:P * m + P], ps[:, :].rearrange("p (c n) -> p c n", n=P)).then_inc(s, 1)

            keys_in(0), keys_in(1)
            gained("tr2", ta, 2)
            link(V.memset(qm, 0.0))
            for c in range(8):
                read_out(dve, "xq", c)
            for b in range(DEC_B):
                ins = V.tensor_copy(qm.rearrange("p (c b n) -> p c b n", c=KC, b=DEC_B)[:, :, b, DEC_T * b:DEC_T * b + DEC_T],
                                    tb[:, :, SEQ + DEC_T * b:SEQ + DEC_T * b + DEC_T])
            ins.then_inc(qm_in, 1)
            for b in range(2, DEC_B):
                dve.wait_ge(xs_part, b - 1)
                keys_in(b)
            dve.wait_ge(xs_full, 1)
            V.tensor_reduce(stat[:, 40:41], sx_bank[:, 0:NMEM], AX.X, ALU.max, negate=True).then_inc(xmax_in, 1)
            dve.wait_ge(xexp, 1)
            link(V.reciprocal(stat[:, 41:42], stat[:, 41:42]))
            V.tensor_scalar(px, px, stat[:, 41:42], None, ALU.mult).then_inc(xprob, 1)
            V.memset(pxT.rearrange("p m b n -> p (m b n)"), 0.0).then_inc(xprob, 1)
            def xmax(u):
                if u >= 2:
                    b_, use = place(("xpt", u - 2))
                    dve.wait_ge(bank_full[b_], use + 1)
                ps, _ = product(dve, "xs", u)
                c = 8 + 4 * (u % 2)
                V.tensor_reduce(stat[:, c:c + 2], ps[:, :].rearrange("p (h n) -> p h n", n=NMEM), AX.X, ALU.max, negate=True).then_inc(summed, 1)

            xmax(0)
            for u in range(4):
                if u + 1 < 4:
                    xmax(u + 1)
                read_out(dve, "xs", u)
                dve.wait_ge(expd, 17 + u)
                share(u, 9 + u, NMEM)
            dve.wait_ge(loaded["xdiag"], 16)
            for g in range(2):
                for h in range(2):
                    ps, s = product(dve, "pvx", g, h)
                    V.tensor_tensor(xkept[g][:, 512 * h:512 * h + 512], ps[:, :], xown[:, 512 * h:512 * h + 512], ALU.mult).then_inc(s, 1)
            residual("xo")
            for t, (t0, n) in enumerate(TOK):
                norm(16 + t, n, x[0:n, t, :], hn[0:n, t, :], 9 + t)
            gained("tr3", tb, 3)
            for t, (t0, n) in enumerate(TOK):
                ps, s = product(dve, "route", t)
                V.tensor_copy(logit[0:n, t, :], ps[0:n, 0:EXPERTS]).then_inc(s, 1)
                read_out(dve, "route", t)
                link(V.max(top[0:n, t, :], logit[0:n, t, :]))
                V.max_index(idx[0:n, t, :], top[0:n, t, :], logit[0:n, t, :])
                link(V.tensor_scalar(stat[0:n, 20 + t:21 + t], top[0:n, t, 0:1], -1.0, None, ALU.mult))
            dve.sem_inc(toph, 1)
            dve.wait_ge(loaded["iota"], 16)
            for t, (t0, n) in enumerate(TOK):
                link(V.tensor_copy(idxf[0:n, t, :], idx[0:n, t, :]))
                for k in range(TOPK):
                    ins = V.tensor_scalar(hot[0:n, t, k, :], iota[0:n, 0:EXPERTS], idxf[0:n, t, k:k + 1], None, ALU.is_equal)
                link(ins)
                V.tensor_reduce(msk[0:n, t, :], hot[0:n, t].rearrange("p k e -> p e k"), AX.X, ALU.add).then_inc(hots, 1)
            dve.wait_ge(gexp, 3)
            for t, (t0, n) in enumerate(TOK):
                link(V.reciprocal(stat[0:n, 24 + t:25 + t], stat[0:n, 24 + t:25 + t]))
                link(V.tensor_scalar(gate[0:n, t, :], gate[0:n, t, :], stat[0:n, 24 + t:25 + t], None, ALU.mult))
                link(V.tensor_tensor(prodr[0:n, t], hot[0:n, t], gate[0:n, t, :].unsqueeze(2).broadcast_to([n, TOPK, EXPERTS]), ALU.mult))
                V.tensor_reduce(gmat[0:n, t, :], prodr[0:n, t].rearrange("p k e -> p e k"), AX.X, ALU.add).then_inc(gmats, 1)
            for t, (t0, n) in enumerate(TOK):
                ps, s = product(dve, "pos", t)
                V.tensor_copy(posn[0:n, t, :], ps[0:n, 0:EXPERTS]).then_inc(s, 1)
                read_out(dve, "pos", t)
                link(V.scalar_tensor_tensor(out=table[0:n, t, 0:EXPERTS], in0=posn[0:n, t, :], scalar=FAR, in1=msk[0:n, t, :],
                                            op0=ALU.add, op1=ALU.mult))
                link(V.tensor_scalar(table[0:n, t, 0:EXPERTS], table[0:n, t, 0:EXPERTS], -FAR, None, ALU.add))
                for j in range(1, ROUNDS):
                    V.tensor_scalar(table[0:n, t, EXPERTS * j:EXPERTS * j + EXPERTS], table[0:n, t, 0:EXPERTS], -float(CAP * j), None, ALU.add)
                ins = V.memset(table[0:n, t, STEPS:NTAB], -FAR)
                link(ins)
            for t, (t0, n) in enumerate(TOK):
                ins = V.tensor_scalar(onehot[0:n, t, :], iota[0:n, 0:CAP], table[0:n, t, 0:1], None, ALU.is_equal)
            link(ins)
            dve.sem_inc(onehot_in, 1)
            ps, s = product(dve, "count")
            link(V.tensor_reduce(cntf, ps[0:1, 0:EXPERTS], AX.X, ALU.max))
            link(V.tensor_copy(most[:, :], cntf))
            dve.sem_inc(s, 1)
            dve.sem_inc(most_in, 1)
            crowd = dve.value_load(most[0:1, 0:1], min_val=0, max_val=T)
            residual("bd")
            dve.wait_ge(loaded["expert"], 16)
            V.tensor_scalar(pick, ones[0:96, 0:CAP], expert1[:, 0:1], None, ALU.mult).then_inc(pick_in, 1)

            def evac_xe():
                V.tensor_tensor(xe, bank_x[:, :].rearrange("p (k n) -> p k n", n=CAP),
                                gcol[:, 3, :].unsqueeze(2).broadcast_to([P, KC, CAP]), ALU.mult).then_inc(xe_in, 1)

            dve.wait_ge(xg_full, 1)
            evac_xe()
            for t, (t0, n) in enumerate(TOK):
                ins = V.tensor_scalar(onehot[0:n, t, :], iota[0:n, 0:CAP], table[0:n, t, 1:2], None, ALU.is_equal)
            ins.then_inc(onehot_in, 1)
            for t, (t0, n) in enumerate(TOK):
                link(V.tensor_tensor(prodr[0:n, t], hot[0:n, t], posn[0:n, t, :].unsqueeze(1).broadcast_to([n, TOPK, EXPERTS]), ALU.mult))
                link(V.tensor_reduce(slot[0:n, t, :], prodr[0:n, t], AX.X, ALU.add))
                link(V.scalar_tensor_tensor(out=rowf[0:n, t, :], in0=idxf[0:n, t, 0:TOPK], scalar=float(CAP), in1=slot[0:n, t, :],
                                            op0=ALU.mult, op1=ALU.add))
                for j in range(1, ROUNDS):
                    link(V.tensor_scalar(jump[0:n, t, :], slot[0:n, t, :], float(CAP * j), float((EXPERTS - 1) * CAP), ALU.is_ge, ALU.mult))
                    link(V.tensor_tensor(rowf[0:n, t, :], rowf[0:n, t, :], jump[0:n, t, :], ALU.add))
                link(V.tensor_copy(rows[0:n, t, :], rowf[0:n, t, :]))
            dve.sem_inc(tables, 1)

            def step_(n):
                dve.wait_ge(wide_used, 8 * n + 16)
                V.tensor_scalar(gc, bank_g[:, :], 7.0, None, ALU.min).then_inc(gc_in, 1)
                V.tensor_scalar(uc, bank_u[:, :], 7.0, -7.0, ALU.min, ALU.max).then_inc(uc_in, 1)
                dve.wait_ge(gc_in, n + 1)
                dve.wait_ge(uc_in, n + 1)
                V.scalar_tensor_tensor(out=gu, in0=uc, scalar=1.0, in1=gc, op0=ALU.add, op1=ALU.mult).then_inc(gu_in, 1)
                dve.wait_ge(gu_in, n + 1)
                dve.wait_ge(sg_in, n + 1)
                V.tensor_tensor(gu, gu, sg, ALU.mult).then_inc(a_in, 1)
                V.tensor_scalar(pick, ones[0:96, 0:CAP], expert1[:, ds(n + 1, 1)], None, ALU.mult).then_inc(pick_in, 1)
                dve.wait_ge(xg_full, n + 2)
                evac_xe()
                for t, (t0, m) in enumerate(TOK):
                    ins = V.tensor_scalar(onehot[0:m, t, :], iota[0:m, 0:CAP], table[0:m, t, ds(n + 2, 1)], None, ALU.is_equal)
                ins.then_inc(onehot_in, 1)

            with dve.Fori(0, EXPERTS) as n:
                step_(n)
            with dve.If(crowd > CAP):
                with dve.Fori(1, ROUNDS) as j:
                    with dve.Fori(0, EXPERTS) as e:
                        step_(j * EXPERTS + e)
            def last_norm(t):
                n = TOK[t][1]
                inverse_root(32 + t, n, 12 + t)
                V.scalar_tensor_tensor(out=xout[t][0:n, :], in0=x[0:n, t, :], scalar=stat[0:n, 32 + t:33 + t], in1=gfin[0:n, :],
                                       op0=ALU.mult, op1=ALU.mult).then_inc(fin, 1)

            for t, (t0, n) in enumerate(TOK):
                dve.wait_ge(gathered[t], 64)
                for k in range(TOPK):
                    ins = V.scalar_tensor_tensor(out=x[0:n, t, :], in0=yk[4 * t + k][0:n, :], scalar=gate[0:n, t, k:k + 1],
                                                 in1=x[0:n, t, :], op0=ALU.mult, op1=ALU.add)
                    if k < TOPK - 1:
                        link(ins)
                ins.then_inc(xsum, 1)
                if t == 0:
                    dve.wait_ge(loaded["gfin"], 16)
                else:
                    last_norm(t - 1)
            last_norm(2)

        @block.tensor
        def _(pe):
            M = nc.tensor.matmul
            TR = nc.tensor.transpose

            pe.wait_ge(loaded["cbias"], 16)
            pe.wait_ge(rb_rep, 1)
            cw = [cb[:, TOEP + P * s:TOEP + P * s + P] for s in range(6)]
            ps, s = take(pe, "bias_w")
            for kind in range(3):
                for t in range(DEC_T):
                    c = 32 * kind + 8 * t
                    ins = M(ps[:, c:c + 8], cw[kind if kind < 2 else 2 + t], rb, start=True, stop=True)
            ins.then_inc(s, 1)
            ps, s = take(pe, "bias_f")
            for t in range(DEC_T):
                c = TOEP + 6 * P + NS * t
                ins = M(ps[0:NS, 8 * t:8 * t + 8], cb[:, c:c + NS], rb, start=True, stop=True)
            ins.then_inc(s, 1)
            for h in range(HEADS):
                ps, s = take(pe, "toep", h)
                M(ps[:, 0:TOEP], rbrep[:, h, :], cb[:, 0:TOEP], start=True, stop=True).then_inc(s, 1)

            def transposes(name, count):
                for t, (t0, n) in enumerate(TOK):
                    pe.wait_ge(normed, count + t)
                    for h in range(2):
                        ps, s = take(pe, name, t, h)
                        for c in range(4):
                            ins = TR(ps[:, P * c:P * c + n], hn[0:n, t, 512 * h + P * c:512 * h + P * c + P], ident[0:n, 0:n])
                        ins.then_inc(s, 1)

            pe.wait_ge(loaded["ident"], 16)
            transposes("tr1", 1)
            for t in range(2):
                read_out(pe, "tr1", t, 0), read_out(pe, "tr1", t, 1)
                tk = [take(pe, "qkv", t, c) for c in range(3)]
                for k in range(KC):
                    if t == 0:
                        pe.wait_ge(wide_in[k], 16)
                    for c in range(3):
                        ins = M(tk[c][0][:, :], ta[:, k, P * t:P * t + P], wide[:, k, 512 * c:512 * c + 512], start=k == 0, stop=k == KC - 1)
                        if k == KC - 1:
                            ins.then_inc(tk[c][1], 1)
            read_out(pe, "tr1", 2, 0), read_out(pe, "tr1", 2, 1)
            ps, s = take(pe, "qkv", 2)
            for k in range(KC):
                for c in range(3):
                    ins = M(ps[NS * c:NS * c + NS, :], ta[:, k, SEQ:T], wide[:, k, 512 * c:512 * c + 512], start=k == 0, stop=k == KC - 1)
            ins.then_inc(s, 1)
            for c in range(4):
                ps, s = take(pe, "u", c)
                for k in range(KC):
                    ins = M(ps[:, 0:T], wide[:, k, 1536 + P * c:1536 + P * c + P], ta[:, k, :], start=k == 0, stop=k == KC - 1)
                ins.then_inc(s, 1)
            for t, (t0, n) in enumerate(TOK):
                for ci, name, src in ((0, "trq", qn), (1, "trk", kn)):
                    read_out(pe, *(("qkv", t, ci) if t < 2 else ("qkv", 2)))
                    ps, s = take(pe, name, t)
                    for c in range(4):
                        ins = TR(ps[:, P * c:P * c + n], src[0:n, t, P * c:P * c + P], ident[0:n, 0:n])
                    ins.then_inc(s, 1)
            for h in range(2):
                read_out(pe, "trq", 2), read_out(pe, "trk", 2)
                ps, s = take(pe, "fresh", h)
                for c in range(4):
                    ins = M(ps[0:NS, NS * c:NS * c + NS], kT[64 * h:64 * h + 64, c, SEQ:T], qT[64 * h:64 * h + 64, c, SEQ:T], start=True, stop=True)
                ins.then_inc(s, 1)
            pe.wait_ge(loaded["state"], 16)
            ps, s = take(pe, "state")
            ns = DEC_B * STATE
            for c in range(4):
                ins = TR(ps[:, ns * c:ns * c + ns], state[:, P * c:P * c + P], ident[0:ns, 0:ns])
            ins.then_inc(s, 1)
            for c in range(4):
                read_out(pe, "u", c)
            ps, s = take(pe, "utp")
            for c in range(4):
                ins = TR(ps[0:STATE, P * c:P * c + P], uP[:, c, UP - STATE:UP], ident[:, :])
            ins.then_inc(s, 1)
            ps, s = take(pe, "uts")
            for c in range(4):
                ins = TR(ps[0:NS, P * c:P * c + P], unew[:, c, :], ident[:, :])
            ins.then_inc(s, 1)
            pe.wait_ge(loaded["wpool"], 16)
            for g in range(4):
                pe.wait_ge(pooled, g + 1)
                ps, s = take(pe, "pool", g)
                M(ps[:, 0:T], wpool[:, g, :], dT[:, g, :], start=True, stop=True).then_inc(s, 1)

            def scores(u):
                hp, qt = UNITS[u]
                nk = P * (qt + 1)
                for h in range(2):
                    ps, s = take(pe, "s", u, h)
                    r = slice(64 * h, 64 * h + 64)
                    M(ps[:, 0:nk], qT[r, hp, P * qt:P * qt + P], kT[r, hp, 0:nk], start=True, stop=True).then_inc(s, 1)

            for t in range(2):
                read_out(pe, "trq", t), read_out(pe, "trk", t)
            scores(0)

            def turned(u):
                hp, qt = UNITS[u]
                pe.wait_ge(scaled, u + 1)
                ps, s = take(pe, "pt", u)
                for h in range(2):
                    for c in range(qt + 1):
                        z = P * ((qt + 1) * h + c)
                        ins = TR(ps[:, z:z + P], lg[u % 2][:, h, P * c:P * c + P], ident[:, :])
                ins.then_inc(s, 1)

            def unit_values(u):
                hp, qt = UNITS[u]
                read_out(pe, "pt", u)
                ps, s = take(pe, "o", u)
                for h in range(2):
                    for c in range(qt + 1):
                        hd = 64 * (2 * hp + h)
                        ins = M(ps[64 * h:64 * h + 64, 0:P], vn[:, c, hd:hd + 64], pT[u % 2][:, (qt + 1) * h + c, :], start=c == 0, stop=c == qt)
                ins.then_inc(s, 1)

            def rows_times(name, t, left, n, t0, halves=2):
                if name in ("out", "xo") and t == 2:
                    ps, s = take(pe, name, 2)
                    for k in range(KC):
                        for h in range(2):
                            ins = M(ps[NS * h:NS * h + NS, :], left[:, k, SEQ:T], slim[:, k, 512 * h:512 * h + 512], start=k == 0, stop=k == KC - 1)
                    ins.then_inc(s, 1)
                    return
                tk = [take(pe, name, t, h) for h in range(2)]
                for k in range(KC):
                    if t == 0:
                        pe.wait_ge(slim_in[k], 16 * round_[0])
                    for h in range(2):
                        ins = M(tk[h][0][0:n, :], left[:, k, t0:t0 + n], slim[:, k, 512 * h:512 * h + 512], start=k == 0, stop=k == KC - 1)
                        if k == KC - 1:
                            ins.then_inc(tk[h][1], 1)

            round_ = [1]

            def fill(name):
                kind, t, h = name
                if kind == "trm":
                    pe.wait_ge(normed, 4 + t)
                    ps, s = take(pe, *name)
                    for c in range(4):
                        ins = TR(ps[:, P * c:P * c + P], hn[:, t, 512 * h + P * c:512 * h + P * c + P], ident[:, :])
                    ins.then_inc(s, 1)
                elif kind in ("mk", "mv"):
                    if h == 0:
                        read_out(pe, "trm", t, 0), read_out(pe, "trm", t, 1)
                    ps, s = take(pe, *name)
                    for k in range(KC):
                        if t == 0 and h == 0:
                            pe.wait_ge(slim_in[k], 16 if kind == "mk" else 32)
                        ins = M(ps[:, :], ta[:, k, P * t:P * t + P], slim[:, k, 512 * h:512 * h + 512], start=k == 0, stop=k == KC - 1)
                    ins.then_inc(s, 1)
                else:
                    read_out(pe, "mk", t, h)
                    ps, s = take(pe, *name)
                    for c in range(4):
                        ins = TR(ps[:, P * c:P * c + P], hn[:, t, 512 * h + P * c:512 * h + P * c + P], ident[:, :])
                    ins.then_inc(s, 1)

            def values(b):
                pe.wait_ge(prob, b + 1)
                pe.wait_ge(v_in, 48 * (b + 1))
                ps, s = take(pe, "pv", b)
                flat = pr[:, :, :, :].rearrange("p k t h -> p k (t h)")
                for k, kind in enumerate((2, 0, 1, 3)):
                    for t in range(DEC_T):
                        g = slice(32 * t, 32 * t + 32)
                        if kind == 3:
                            ins = M(ps[g, :], flat[0:NS, 3, :], vn[0:NS, 2, :], start=False, stop=True, tile_position=(0, 32 * t))
                        else:
                            ins = M(ps[g, :], flat[:, kind, :], vwin[:, 8 if kind == 2 else 4 * kind + t, :], start=k == 0, stop=False)
                ins.then_inc(s, 1)

            def turn_values(b):
                read_out(pe, "pv", b)
                ps, s = take(pe, "pvt", b)
                for c in range(4):
                    ins = M(ps[:, 4 * c:4 * c + 4], kept[:, P * c:P * c + P], own[:, AW:AW + DEC_T], start=True, stop=True)
                ins.then_inc(s, 1)

            def row(b, t):
                ps, s = take(pe, "qb", b, t)
                r = DEC_T * b + t
                M(ps[:, :], ident[0:NS, r:r + 1].broadcast_to([NS, P]), qn[0:NS, 2, :], start=True, stop=True).then_inc(s, 1)

            row(0, 0), row(0, 1)
            for b in range(DEC_B):
                row(b, 2)
                turned(b)
                if b >= 2:
                    turn_values(b - 2)
                for f in FILL[b, 0]:
                    fill(f)
                row(b, 3)
                unit_values(b)
                if b + 1 < DEC_B:
                    scores(b + 1)
                if b + 1 < DEC_B:
                    row(b + 1, 0), row(b + 1, 1)
                if b:
                    values(b - 1)
                for f in FILL[b, 1]:
                    fill(f)
            turn_values(DEC_B - 2)
            values(DEC_B - 1)
            turn_values(DEC_B - 1)
            read_out(pe, "pvt", DEC_B - 1)
            round_[0] = 3
            for t, (t0, n) in enumerate(TOK):
                rows_times("out", t, tb, n, t0)

            def turn_keys(b):
                pe.wait_ge(ck_in[b % 4], 16 * (b // 4 + 1))
                for m in range(2):
                    for h in range(2):
                        ps, s = take(pe, "trck", b, m, h)
                        for c in range(4):
                            ins = TR(ps[:, P * c:P * c + P], cmem[b % 4][:, m, 512 * h + P * c:512 * h + P * c + P], ident[:, :])
                        ins.then_inc(s, 1)

            turn_keys(0), turn_keys(1)
            transposes("tr2", 6)
            for t in range(3):
                read_out(pe, "tr2", t, 0), read_out(pe, "tr2", t, 1)
            for c in range(8):
                ps, s = take(pe, "xq", c)
                for k in range(KC):
                    if c == 0:
                        pe.wait_ge(slim_in[k], 64)
                    ins = M(ps[:, 0:T], slim[:, k, P * c:P * c + P], ta[:, k, :], start=k == 0, stop=k == KC - 1)
                ins.then_inc(s, 1)

            def cross_scores(b):
                for m in range(2):
                    read_out(pe, "trck", b, m, 0), read_out(pe, "trck", b, m, 1)
                for c in range(2):
                    for h in range(XH):
                        q0 = 256 * (2 * h + c) + 32 * b
                        ins = M(sx_bank[32 * h:32 * h + 32, 0:NMEM], qm[:, q0:q0 + 32], ktm[b % 2][:, 2 * h + c, :],
                                start=b == 0 and c == 0, stop=b == DEC_B - 1 and c == 1)
                ins.then_inc(xs_full if b == DEC_B - 1 else xs_part, 1)

            pe.wait_ge(qm_in, 1)
            cross_scores(0)
            for b in range(2, DEC_B):
                turn_keys(b)
                cross_scores(b - 1)
            cross_scores(DEC_B - 1)

            def xscores(u):
                hp, qt = XUNITS[u]
                ps, s = take(pe, "xs", u)
                for h in range(2):
                    for c in range(2):
                        k = 2 * (2 * hp + h) + c
                        ins = M(ps[:, 256 * h:256 * h + 256], tb[:, k, P * qt:P * qt + P], mkT[:, k, :], start=c == 0, stop=c == 1)
                ins.then_inc(s, 1)

            xscores(0)
            for u, (hp, qt) in enumerate(XUNITS):
                if u + 1 < 4:
                    xscores(u + 1)
                pe.wait_ge(scaled, 9 + u)
                ps, s = take(pe, "xpt", u)
                for h in range(2):
                    for c in range(2):
                        z = P * (2 * h + c)
                        ins = TR(ps[:, z:z + P], lg[u % 2][:, h, P * c:P * c + P], ident[:, :])
                ins.then_inc(s, 1)
                read_out(pe, "xpt", u)
                ps, s = take(pe, "xo_", u)
                for h in range(2):
                    for c in range(2):
                        z = P * (2 * h + c)
                        hd = XHD * (2 * hp + h) + P * c
                        for m in range(2):
                            ins = M(ps[:, z:z + P], mv[:, m, hd:hd + P], pT[u % 2][:, 2 * h + m, :], start=m == 0, stop=m == 1)
                ins.then_inc(s, 1)
            pe.wait_ge(xprob, 2)
            ps, s = take(pe, "xpts")
            for m in range(2):
                ins = TR(ps[:, P * m:P * m + P], px[:, P * m:P * m + P], ident[:, :])
            ins.then_inc(s, 1)
            read_out(pe, "xpts")
            for g in range(2):
                tk = [take(pe, "pvx", g, h) for h in range(2)]
                for h in range(2):
                    for m in range(2):
                        for r in range(4):
                            b = 4 * g + r
                            if h == 0 and m == 0:
                                pe.wait_ge(cv_in[b], 16)
                            v = cmem[4 + b if b < 4 else b - 4]
                            ins = M(tk[h][0][32 * r:32 * r + 32, :], pxT[:, m, b, :], v[:, m, 512 * h:512 * h + 512], start=m == 0, stop=m == 1)
                    ins.then_inc(tk[h][1], 1)
            pe.wait_ge(loaded["xdiag"], 16)
            for g in range(2):
                read_out(pe, "pvx", g, 0), read_out(pe, "pvx", g, 1)
                ps, s = take(pe, "pvxt", g)
                for c in range(KC):
                    ins = M(ps[:, 16 * c:16 * c + 16], xkept[g][:, P * c:P * c + P], xown[:, D:D + 16], start=True, stop=True)
                ins.then_inc(s, 1)
            b_, use = place(("pvxt", 1))
            pe.wait_ge(bank_full[b_], use + 1)
            pe.sem_inc(wide_used, 8)
            read_out(pe, "pvxt", 1)
            round_[0] = 5
            for u in range(4):
                read_out(pe, "xo_", u)
            for t, (t0, n) in enumerate(TOK):
                rows_times("xo", t, ta, n, t0)
            b_, use = place(("xo", 2))
            pe.wait_ge(bank_full[b_], use + 1)
            pe.sem_inc(slim_used, 8)
            transposes("tr3", 9)
            pe.wait_ge(loaded["wr"], 16)
            pe.wait_ge(loaded["brow"], 16)
            for t, (t0, n) in enumerate(TOK):
                read_out(pe, "tr3", t, 0), read_out(pe, "tr3", t, 1)
                ps, s = take(pe, "route", t)
                for k in range(KC):
                    M(ps[0:n, 0:EXPERTS], tb[:, k, t0:t0 + n], wr[:, k, :], start=k == 0, stop=False)
                M(ps[0:n, 0:EXPERTS], ones[0:1, 0:n], brow, start=False, stop=True).then_inc(s, 1)
            pe.wait_ge(loaded["before"], 16)
            for t, (t0, n) in enumerate(TOK):
                pe.wait_ge(hots, t + 1)
                ps, s = take(pe, "pos", t)
                for t_ in range(t):
                    M(ps[0:n, 0:EXPERTS], ones[:, 0:n], msk[:, t_, :], start=t_ == 0, stop=False)
                M(ps[0:n, 0:EXPERTS], before[0:n, 0:n], msk[0:n, t, :], start=t == 0, stop=True).then_inc(s, 1)
            ps, s = take(pe, "count")
            for t, (t0, n) in enumerate(TOK):
                ins = M(ps[0:1, 0:EXPERTS], ones[0:n, 0:1], msk[0:n, t, :], start=t == 0, stop=t == 2)
            ins.then_inc(s, 1)
            pe.wait_ge(gmats, 3)
            ps, s = take(pe, "trg")
            for t, (t0, n) in enumerate(TOK):
                ins = TR(ps[0:EXPERTS, t0:t0 + n], gmat[0:n, t, :], ident[0:n, 0:n])
            ins.then_inc(s, 1)
            read_out(pe, "trg")
            pe.wait_ge(loaded["bdn"], 16)
            for t, (t0, n) in enumerate(TOK):
                for h in range(2):
                    ps, s = take(pe, "bd", t, h)
                    M(ps[0:n, :], gT[:, t0:t0 + n], bdn[:, 512 * h:512 * h + 512], start=True, stop=True).then_inc(s, 1)
            pe.wait_ge(most_in, 1)
            crowd = pe.value_load(most[0:1, 0:1], min_val=0, max_val=T)
            for name in jobs[-TURN:]:
                read_out(pe, *name)

            def gather(count):
                pe.wait_ge(onehot_in, count)
                for k in range(KC):
                    for t, (t0, m) in enumerate(TOK):
                        ins = M(bank_x[:, CAP * k:CAP * k + CAP], hn[0:m, t, P * k:P * k + P], onehot[0:m, t, :], start=t == 0, stop=t == 2)
                ins.then_inc(xg_full, 1)

            gather(1)
            pe.wait_ge(parts_in, 1)

            def step_(n):
                half = [slice(0, CAP), slice(CAP, 2 * CAP)]
                pe.wait_ge(pick_in, n + 1)
                for q, bk in enumerate((bank_g, bank_u)):
                    for h in range(2):
                        c = D * q + 512 * h
                        M(bk[half[h], :], pick, parts[:, c:c + 512], start=True, stop=False)
                pe.wait_ge(xe_in, n + 1)
                for k in range(KC):
                    pe.wait_ge(wide_in[k], 16 * n + 32)
                    for q, bk in enumerate((bank_g, bank_u)):
                        for h in range(2):
                            c = D * q + 512 * h
                            ins = M(bk[half[h], :], xe[:, k, :], wide[:, k, c:c + 512], start=False, stop=k == KC - 1)
                    ins.then_inc(wide_used, 1)
                gather(n + 2)
                pe.wait_ge(a_in, n + 1)
                for j in range(4):
                    ins = TR(bank_t[:, P * j:P * j + P], gu[:, P * j:P * j + P], ident[:, :])
                ins.then_inc(at_full, 1)
                pe.wait_ge(at_in, n + 1)
                pe.wait_ge(y_read, n + 1)
                for f in range(KC):
                    pe.wait_ge(slim_in[f], 16 * n + 96)
                    for h in range(2):
                        ins = M(bank_y[half[h], :], aT[:, f % 4, f // 4, :], slim[:, f, 512 * h:512 * h + 512], start=f == 0, stop=f == KC - 1)
                    ins.then_inc(slim_used, 1)

            with pe.Fori(0, EXPERTS) as n:
                step_(n)
            with pe.If(crowd > CAP):
                with pe.Fori(1, ROUNDS) as j:
                    with pe.Fori(0, EXPERTS) as e:
                        step_(j * EXPERTS + e)


_OUTS = [
    ("y_prompt", (1, SEQ, D)), ("y_sample", (DEC_B, DEC_T, D)),
    ("k_win_prompt", (1, 1, SEQ, HEADS, HD)), ("v_win_prompt", (1, 1, SEQ, HEADS, HD)),
    ("pool_prompt", (1, 1, STATE, AW)),
    ("mem_k_prompt", (1, 1, NMEM, XH, XHD)), ("mem_v_prompt", (1, 1, NMEM, XH, XHD)),
    ("k_win_sample", (1, DEC_B, PAST, HEADS, HD)), ("v_win_sample", (1, DEC_B, PAST, HEADS, HD)),
    ("pool_sample", (1, DEC_B, STATE, AW)),
]
_PLAIN = ["x_prompt", "x_sample", "cache_k_win", "cache_v_win", "state_pool", "cache_mem_k", "cache_mem_v",
          "mem_prompt", "rel_bias", "w_in", "w_pool", "w_out", "w_xq", "w_xk", "w_xv", "w_xo", "w_router",
          "b_router", "w_gate_up", "b_gate_up", "w_down", "b_down"]


def kernel(**inputs):
    import numpy as _np
    import concourse.bacc as _bacc
    from concourse import mybir as _mybir
    from concourse.bass_utils import run_bass_kernel_spmd as _run

    nc = _bacc.Bacc("TRN2", target_bir_lowering=False, num_devices=1)
    arrays = {n: _np.ascontiguousarray(inputs[n]) for n in _PLAIN}
    cols = [_np.asarray(inputs[n])[0].reshape(KC, P).T for n in ("g_mix", "g_mem", "g_x", "g_ff")]
    arrays["g_all"] = _np.ascontiguousarray(_np.stack(cols, 1))
    arrays["pool_scale_col"] = _np.ascontiguousarray(_np.asarray(inputs["pool_scale"])[0].reshape(4, P).T)
    arrays["g_final_rows"] = _np.ascontiguousarray(_np.broadcast_to(_np.asarray(inputs["g_final"]), (P, D)))
    arrays.update(constants())
    ins = {n: nc.dram_tensor(f"in_{n}", a.shape, _mybir.dt.from_np(a.dtype), kind="ExternalInput").ap() for n, a in arrays.items()}
    outs = {n: nc.dram_tensor(f"out_{n}", shape, _mybir.dt.float32, kind="ExternalOutput").ap() for n, shape in _OUTS}
    build(nc, ins, outs)
    r = _run(nc, [{f"in_{n}": a for n, a in arrays.items()}], core_ids=[0])
    return tuple(r.results[0][f"out_{n}"] for n, _ in _OUTS)
```

```python
import math
from contextlib import ExitStack

import concourse.bass as bass
import numpy as np
from concourse import mybir

P = 128
D = 1024
KC = D // P
SEQ, DEC_B, DEC_T = 256, 8, 4
NS = DEC_B * DEC_T
T = SEQ + NS
TOK = [(0, P), (P, P), (SEQ, NS)]
PAST = 2048
HEADS, HD = 8, 64
AW = HEADS * HD
NMEM, XH, XHD = 256, 4, 256
POOLW = (2, 4, 8, 16)
STATE = max(POOLW) - 1
EXPERTS, TOPK = 32, 4
CAP = 64
ROUNDS = -(-T // CAP)
STEPS = EXPERTS * ROUNDS
LOT = 4
NTAB = STEPS + 4
FAR = float(2 ** 20)
NEG = -1e30
EPS = 1e-6
BUCKETS = 32
TOEP = 384


def buckets(dist):
    half = BUCKETS // 2
    n = np.maximum(dist, 1).astype(np.float32)
    large = half + (np.log(n / np.float32(half)) / np.float32(math.log(PAST / half))
                    * np.float32(BUCKETS - half)).astype(np.int32)
    return np.where(dist < half, dist, np.minimum(large, BUCKETS - 1))


def bias_rows(dist, add):
    d = np.asarray(dist)
    out = np.zeros((BUCKETS + 1, d.size), np.float32)
    out[buckets(np.clip(d, 0, PAST)), np.arange(d.size)] = 1.0
    out[BUCKETS] = add
    return out


def constants():
    dist = 255 - np.arange(TOEP)
    count = (dist <= 128).astype(int) + (dist % 4 == 0) + (dist % 16 == 0)
    ok = (dist >= 0) & (count > 0)
    toep = bias_rows(dist, np.where(ok, np.log(np.maximum(count, 1)), NEG))
    p = np.arange(P)
    window = [bias_rows(512 - 4 * p, 0.0), bias_rows(2048 - 16 * p, 0.0)]
    r = 4 * (p % 32) + p // 32
    window += [bias_rows(128 + t - r, np.where(r >= t, 0.0, NEG)) for t in range(DEC_T)]
    key_t = np.arange(NS) % DEC_T
    fresh = [bias_rows(t - key_t, 0.0) for t in range(DEC_T)]
    kb, kt = np.arange(NS)[:, None] // DEC_T, np.arange(NS)[:, None] % DEC_T
    qb, qt = np.arange(NS)[None, :] // DEC_T, np.arange(NS)[None, :] % DEC_T
    fresh_mask = np.where((kb == qb) & (kt <= qt), np.where(kt == qt, math.log(3.0), 0.0), NEG)
    first = np.array([[1.0 / min(i + 1, w) for i in range(16)] for w in POOLW])
    n = np.arange(NTAB)
    col = np.arange(AW)
    own = ((p[:, None] // 32 == p[:, None] // 8 % 4) & (p[:, None] % 8 == col[None, :] // HD)).astype(np.float32)
    diag = np.concatenate([own, (p[:, None] // 32 == np.arange(DEC_T)[None, :]).astype(np.float32)], 1)
    xcol = np.arange(D)
    r, h_, t_ = p[:, None] // 32, p[:, None] % 32 // 4, p[:, None] % 4
    xown = (h_ == xcol[None, :] // XHD).astype(np.float32)
    c = np.arange(16)[None, :]
    xdiag = np.concatenate([xown, ((r == c // 4) & (t_ == c % 4) & (h_ < XH)).astype(np.float32)], 1)
    return {
        "c_diag": diag,
        "c_xdiag": xdiag,
        "c_bias": np.concatenate([toep] + window + fresh, 1).astype(np.float32),
        "c_fresh": fresh_mask.astype(np.float32),
        "c_first": np.tile(first.reshape(1, 64), (P, 1)).astype(np.float32),
        "c_ident": np.eye(P, dtype=np.float32),
        "c_before": (p[:, None] < p[None, :]).astype(np.float32),
        "c_iota": np.tile(np.arange(CAP, dtype=np.float32), (P, 2)),
        "c_expert": (np.arange(96)[:, None] % 32 == n[None, :] % 32).astype(np.float32),
    }


def build(nc, i, o):
    f32, bf16, u32, i32 = mybir.dt.float32, mybir.dt.bfloat16, mybir.dt.uint32, mybir.dt.int32
    ALU, ACT, AX = mybir.AluOpType, mybir.ActivationFunctionType, mybir.AxisListType
    ds = bass.ds
    ctx = ExitStack()
    with ctx:
        def sb(name, shape, dt=f32):
            return ctx.enter_context(nc.sbuf_tensor(name, shape, dt))

        def sem(name):
            return ctx.enter_context(nc.semaphore(name))

        toep_dram = nc.dram_tensor("toep_dram", (P, HEADS, TOEP), f32, kind="Internal").ap()

        wide = sb("wide", [P, KC, 2 * D])
        slim = sb("slim", [P, KC, D])
        x = sb("x", [P, 3, D])
        hn = sb("hn", [P, 3, D])
        ta = sb("ta", [P, KC, T])
        tb = sb("tb", [P, KC, T])
        mkT = sb("mkT", [P, KC, NMEM])
        mv = sb("mv", [P, 2, D])
        att = sb("att", [P, 10112])
        scr = sb("scr", [P, 2048])
        ident = sb("ident", [P, P])
        iota = sb("iota", [P, 2 * CAP])
        ones = sb("ones", [P, P])
        gcol = sb("gcol", [P, 4, KC])
        small = sb("small", [P, 456])
        eps = sb("eps", [P, 1])
        meansq = sb("meansq", [P, 41])
        idx = sb("idx", [P, 3, 8], u32)
        most = sb("most", [1, 1], i32)

        wf = wide[:, :, :].rearrange("p k n -> p (k n)")
        kwin = [wf[:, 4608 * s:4608 * s + 4608].rearrange("p (s n) -> p s n", n=AW) for s in range(2)]
        vwin = wf[:, 9216:13824].rearrange("p (s n) -> p s n", n=AW)
        prod = wf[:, 13824:15360].rearrange("p (s n) -> p s n", n=AW)
        cmem = [wf[:, 2048 * s:2048 * s + 2048].rearrange("p (m n) -> p m n", n=D) for s in range(8)]
        qn = att[:, 0:1536].rearrange("p (t n) -> p t n", n=AW)
        kn = att[:, 1536:3072].rearrange("p (t n) -> p t n", n=AW)
        vn = att[:, 3072:4608].rearrange("p (t n) -> p t n", n=AW)
        qkvn = att[:, 0:4608].rearrange("p (c t n) -> p c t n", c=3, n=AW)
        qT = att[:, 4608:5760].rearrange("p (c n) -> p c n", n=T)
        kT = att[:, 5760:6912].rearrange("p (c n) -> p c n", n=T)
        UP = STATE + SEQ
        uP = att[:, 6912:6912 + 4 * UP].rearrange("p (g n) -> p g n", n=UP)
        bias = att[:, 8000:10048].rearrange("p (h n) -> p h n", n=SEQ)
        mvf = mv[:, :, :].rearrange("p t n -> p (t n)")
        dT = mvf[:, 0:1152].rearrange("p (g n) -> p g n", n=T)
        US = STATE + DEC_T
        uS = mvf[:, 1152:1152 + 4 * DEC_B * US].rearrange("p (g b n) -> p g b n", b=DEC_B, n=US)
        unew = mvf[:, 1760:1888].rearrange("p (g n) -> p g n", n=NS)
        mkTf = mkT[:, :, :].rearrange("p k n -> p (k n)")
        cb = mkTf[0:33, 0:TOEP + 10 * P]
        rb = mkTf[0:33, 1300:1308]
        wr = mkTf[:, 0:256].rearrange("p (k n) -> p k n", n=EXPERTS)
        before = mkTf[:, 256:384]
        rbrep = scr[0:33, 0:1024].rearrange("p (h n) -> p h n", n=P)
        state = scr[0:DEC_B * STATE, 1024:1536]
        wpool = scr[:, 1536:2048].rearrange("p (g n) -> p g n", n=P)
        sum_p = [scr[:, 0:UP], scr[:, UP:2 * UP]]
        sum_s = [scr[:, 600 + 152 * s:600 + 152 * s + 152].rearrange("p (b n) -> p b n", n=US) for s in range(2)]
        lg = [scr[:, 512 * s:512 * s + 512].rearrange("p (h n) -> p h n", n=NMEM) for s in range(2)]
        pT = [scr[:, 1024 + 512 * s:1536 + 512 * s].rearrange("p (c n) -> p c n", n=P) for s in range(2)]
        toep_sb = [att[:, 8000:9920].rearrange("p (h n) -> p h n", n=TOEP),
                   tb[:, :, :].rearrange("p k n -> p (k n)")[:, 0:1152].rearrange("p (h n) -> p h n", n=TOEP)]
        S_ = [small[:, 128 * s:128 * s + 96].rearrange("p (k t h) -> p k t h", k=3, t=DEC_T) for s in range(2)]
        bs = att[:, 10048:10048 + 64]
        bsw = sb("bsw", [P, 3, DEC_T, HEADS])
        bfr = sb("bfr", [NS, DEC_B, DEC_T, HEADS])
        pp = sb("pp", [P, 4, DEC_T, HEADS])
        pr = sb("pr", [P, 4, DEC_T, HEADS])
        fmask = sb("fmask", [NS, NS])
        cfirst = bs.rearrange("p (g n) -> p g n", n=16)
        pscale = sb("pscale", [P, 4])
        mx = small[:, 256:288]
        gm = small[:, 288:320]
        zs = small[:, 320:352]
        zz = small[:, 352:384]
        stat = small[:, 384:456]

        own = hn[:, 2, 0:AW + DEC_T]
        kept = wf[:, 15360:15872]
        qrows = wf[0:96, 13824:14336]
        qparts = wf[0:96, 15872:16128].bitcast(bf16)
        rowsel = wf[0:96, 16128:16144].bitcast(bf16)
        ktm = [att[:, 2048 * s:2048 * s + 2048].rearrange("p (k n) -> p k n", n=NMEM) for s in range(2)]
        qm = att[:, 4608:6656]
        xown = scr[:, 0:D + 16]
        px = att[:, 4096:4352]
        pxT = att[:, 4608:5120].rearrange("p (m b n) -> p m b n", m=2, n=32)
        xkept = [wf[:, 12288 + 1024 * s:13312 + 1024 * s] for s in range(2)]
        logit = att[:, 4096:4192].rearrange("p (t n) -> p t n", n=EXPERTS)
        top = att[:, 4192:4216].rearrange("p (t n) -> p t n", n=8)
        idxf = att[:, 4216:4240].rearrange("p (t n) -> p t n", n=8)
        gate = sb("gate", [P, 3, TOPK])
        hot = att[:, 4240:4624].rearrange("p (t k n) -> p t k n", k=TOPK, n=EXPERTS)
        msk = att[:, 4624:4720].rearrange("p (t n) -> p t n", n=EXPERTS)
        gmat = att[:, 4720:4816].rearrange("p (t n) -> p t n", n=EXPERTS)
        posn = att[:, 4816:4912].rearrange("p (t n) -> p t n", n=EXPERTS)
        prodr = att[:, 4912:5296].rearrange("p (t k n) -> p t k n", k=TOPK, n=EXPERTS)
        gT = att[0:EXPERTS, 5336:5336 + T]
        brow = att[0:1, 5632:5664]
        cntf = att[0:1, 5664:5665]
        table = att[:, 5760:5760 + 3 * NTAB].rearrange("p (t n) -> p t n", n=NTAB)
        expert1 = att[0:96, 6260:6260 + NTAB]
        parts = att[0:96, 6912:7936].bitcast(bf16)
        braw = att[0:96, 8000:10048]
        bdn = scr[0:EXPERTS, 0:D]
        onehot = att[:, 0:384].rearrange("p (t n) -> p t n", n=2 * CAP)
        xe = [att[:, 8000 + 1024 * s:9024 + 1024 * s].rearrange("p (k n) -> p k n", n=2 * CAP) for s in range(2)]
        gc, uc, gu, sg = (att[:, 512 * s:512 * s + 512] for s in (1, 2, 3, 4))
        aT = att[:, 2560:3072].rearrange("p (j h n) -> p j h n", j=4, h=2)
        ye = att[:, 3072:3584]
        pick = att[0:96, 3776:3808].bitcast(bf16)
        gated = att[:, 3808:4192].rearrange("p (t n) -> p t n", n=2 * CAP)
        back = att[:, 4240:4240 + T]
        gfin = mvf[:, 0:D]
        taf, tbf = (a[:, :, :].rearrange("p k n -> p (k n)") for a in (ta, tb))
        xout = [taf[:, 0:D], taf[:, D:2 * D], tbf[:, 0:D]]

        TURN = 7
        bank = [ctx.enter_context(nc.psum_tensor(f"bank{b}", [P, 512], f32)) for b in range(8)]
        sx_bank = bank[7]

        jobs = []

        def add(*name):
            jobs.append(name)

        add("bias_w"), add("bias_f")
        for t in range(3):
            for h in range(2):
                add("tr1", t, h)
        for t in range(2):
            for c in range(3):
                add("qkv", t, c)
            for h in range(4):
                add("toep", 4 * t + h)
        add("qkv", 2)
        for c in range(4):
            add("u", c)
        for t in range(3):
            add("trq", t), add("trk", t)
        add("fresh", 0), add("fresh", 1)
        add("state"), add("utp"), add("uts")
        for g in range(4):
            add("pool", g)
        COPIES = [7, 2, 1, 1, 1, 1, 1, 1, 2, 5, 2, 2, 6]
        ROUND_AT = {3: 1, 7: 2}
        UNITS = [(hp, qt) for hp in range(4) for qt in range(2)]
        add("s", 0, 0), add("s", 0, 1)
        FILL = {(b, lot): [] for b in range(DEC_B) for lot in range(2)}
        for t in range(2):
            for h in range(2):
                FILL[0, t].append(("trm", t, h))
        for n, (t, h) in enumerate([(0, 0), (0, 1), (1, 0), (1, 1)]):
            FILL[1 + n // 2, n % 2].append(("mk", t, h))
            FILL[3, n // 2].append(("trmk", t, h))
            FILL[3 + n, 1].append(("mv", t, h))
        add("qb", 0, 0), add("qb", 0, 1)
        for b in range(DEC_B):
            add("qb", b, 2), add("pt", b)
            if b >= 2:
                add("pvt", b - 2)
            for f in FILL[b, 0]:
                add(*f)
            add("qb", b, 3), add("o", b)
            if b + 1 < DEC_B:
                add("s", b + 1, 0), add("s", b + 1, 1)
            if b + 1 < DEC_B:
                add("qb", b + 1, 0), add("qb", b + 1, 1)
            if b:
                add("pv", b - 1)
            for f in FILL[b, 1]:
                add(*f)
        add("pvt", DEC_B - 2), add("out", 0, 0), add("out", 0, 1), add("pv", DEC_B - 1)
        add("out", 1, 0), add("out", 1, 1), add("pvt", DEC_B - 1), add("out", 2)
        for b in range(2):
            for m in range(2):
                add("trck", b, m, 0), add("trck", b, m, 1)
        for t in range(3):
            add("tr2", t, 0), add("tr2", t, 1)
        for c in range(8):
            add("xq", c)
        for b in range(2, DEC_B):
            for m in range(2):
                add("trck", b, m, 0), add("trck", b, m, 1)
        XUNITS = [(hp, qt) for hp in range(2) for qt in range(2)]
        add("xs", 0)
        for u in range(4):
            if u + 1 < 4:
                add("xs", u + 1)
            add("xpt", u), add("xo_", u)
        add("xpts")
        for g in range(2):
            for h in range(2):
                add("pvx", g, h)
        for g in range(2):
            add("pvxt", g)
        add("xo", 0, 0), add("xo", 0, 1), add("xo", 1, 0), add("xo", 1, 1)
        add("tr3", 0, 0), add("tr3", 0, 1), add("xo", 2), add("tr3", 1, 0), add("tr3", 1, 1), add("route", 0)
        add("tr3", 2, 0), add("tr3", 2, 1), add("route", 1), add("route", 2)
        for t in range(3):
            add("pos", t)
        add("count"), add("trg")
        number = {name: n for n, name in enumerate(jobs)}
        assert len(number) == len(jobs)

        bank_full = [sem(f"bank_full{b}") for b in range(TURN)]
        bank_free = [sem(f"bank_free{b}") for b in range(TURN)]

        def place(name):
            n = number[name]
            return n % TURN, n // TURN

        def take(pe, *name):
            b, use = place(name)
            if use:
                pe.wait_ge(bank_free[b], use)
            return bank[b], bank_full[b]

        def product(eng, *name):
            b, use = place(name)
            eng.wait_ge(bank_full[b], use + 1)
            return bank[b], bank_free[b]

        def read_out(eng, *name):
            b, use = place(name)
            eng.wait_ge(bank_free[b], use + 1)

        loaded = {}

        def load(eng, name, out, in_):
            eng.dma_start(out, in_).then_inc(loaded[name], 16)

        for n in ("x0", "x1", "x2", "rel", "cbias", "cfresh", "cfirst", "ident", "before", "iota", "gcol", "wr",
                  "state", "wpool", "pscale", "toep", "mem", "expert", "diag", "xdiag", "braw0", "braw1", "braw2", "brow", "bdn",
                  "gfin"):
            loaded[n] = sem(f"loaded_{n}")
        wide_in = [sem(f"wide_in{k}") for k in range(KC)]
        slim_in = [sem(f"slim_in{k}") for k in range(KC)]
        wide_used = sem("wide_used")
        slim_used = sem("slim_used")
        out_used = sem("out_used")
        k_in = [sem("k_in0"), sem("k_in1")]
        v_in = sem("v_in")
        late_k, late_v = sem("late_k"), sem("late_v")
        ck_in = [sem(f"ck_in{s}") for s in range(4)]
        cv_in = [sem(f"cv_in{s}") for s in range(8)]
        toep_out = sem("toep_out")
        consts = sem("consts")
        squares = sem("squares")
        normed = sem("normed")
        rb_rep = sem("rb_rep")
        pooled = sem("pooled")
        summed = sem("summed")
        expd = sem("expd")
        scaled = sem("scaled")
        scored = sem("scored")
        gmax = sem("gmax")
        shifted = sem("shifted")
        sexp = sem("sexp")
        zpart = sem("zpart")
        zall = sem("zall")
        prob = sem("prob")
        xs_part = sem("xs_part")
        xs_full = sem("xs_full")
        qm_in = sem("qm_in")
        xmax_in = sem("xmax_in")
        xexp = sem("xexp")
        xprob = sem("xprob")
        parts_in = sem("parts_in")
        qrows_in = sem("qrows_in")
        qparts_in = sem("qparts_in")
        toph = sem("toph")
        hots = sem("hots")
        gexp = sem("gexp")
        gmats = sem("gmats")
        most_in = sem("most_in")
        stored = {n: sem(f"stored_{n}") for n in ("copies", "kv", "pool", "mk", "mv", "y")}
        dve_done = sem("dve_done")
        act_done = sem("act_done")
        pool_done = sem("pool_done")
        onehot_in, pick_in, xe_in, xg_full, gc_in, uc_in, gu_in, sg_in, a_in, at_full, at_in, y_read = (
            sem(n) for n in ("onehot_in", "pick_in", "xe_in", "xg_full", "gc_in", "uc_in", "gu_in", "sg_in", "a_in", "at_full",
                             "at_in", "y_read"))
        gated_in, back_full, back_in, z_full, z_read = (sem(n) for n in ("gated_in", "back_full", "back_in", "z_full", "z_read"))
        xsum = sem("xsum")
        fin = sem("fin")
        bank_g, bank_u, bank_t, bank_b, bank_y = bank[0:5]
        bank_z, bank_x = bank[5:7], bank[7]
        BACK = [(0, 0), (2, None), (0, 1), (1, 0), (1, 1)]
        LAST = (2, 0, 1)

        KEEP = PAST - DEC_T
        pieces = []
        for b in range(DEC_B):
            for src, dst in (("cache_k_win", "k_win_sample"), ("cache_v_win", "v_win_sample")):
                for h in range(2):
                    pieces.append(tuple(ap.rearrange("s h d -> (s h d)").rearrange("(c a n) -> c a n", c=2, a=32)[h]
                                        for ap in (o[dst][0, b, 0:KEEP], i[src][0, b, DEC_T:PAST])))

        w_in = i["w_in"][0].rearrange("(k p) n -> k p n", p=P)

        def wch(name):
            return i[name][0].rearrange("(k p) n -> k p n", p=P)

        SLIM = ["w_xk", "w_xv", "w_out", "w_xq", "w_xo"]
        SLIM_LAST = [("mk", 1, 1), ("mv", 1, 1), None, ("xq", 7)]

        block = ctx.enter_context(nc.Block())

        @block.sync
        def _(sp):
            load(sp, "ident", ident[:, :], i["c_ident"])
            for t, (t0, n) in enumerate(TOK):
                src = i["x_prompt"][0, t0:t0 + n, :] if t < 2 else i["x_sample"].rearrange("b t d -> (b t) d")
                load(sp, f"x{t}", x[0:n, t, :], src)
            load(sp, "rel", rb[0:BUCKETS, :], i["rel_bias"])
            load(sp, "cbias", cb[:, 0:TOEP + 6 * P + 4 * NS], i["c_bias"])
            load(sp, "cfresh", fmask[:, :], i["c_fresh"])
            load(sp, "gcol", gcol[:, :, :], i["g_all"])
            for k in range(KC):
                sp.dma_start(wide[:, k, :], w_in[k]).then_inc(wide_in[k], 16)
            load(sp, "cfirst", bs, i["c_first"])
            load(sp, "state", state, i["state_pool"][0].rearrange("b s d -> (b s) d"))
            load(sp, "wpool", wpool, i["w_pool"][0].rearrange("g c e -> c g e"))
            load(sp, "pscale", pscale[:, :], i["pool_scale_col"])
            load(sp, "iota", iota[:, :], i["c_iota"])

            def copy(n):
                for _ in range(n):
                    dst, src = pieces.pop(0)
                    sp.dma_start(dst, src).then_inc(stored["copies"], 16)

            def slim_round(r):
                if r and r != 3:
                    b, use = place(SLIM_LAST[r - 1])
                    sp.wait_ge(bank_full[b], use + 1)
                src = wch(SLIM[r])
                for k in range(KC):
                    if r == 3:
                        sp.wait_ge(out_used, k + 1)
                    sp.dma_start(slim[:, k, :], src[k]).then_inc(slim_in[k], 16)

            slim_round(0)
            b, use = place(("tr1", 2, 1))
            sp.wait_ge(bank_full[b], use + 1)
            load(sp, "mem", hn[:, 0:2, :], i["mem_prompt"][0].rearrange("(t p) d -> p t d", p=P))
            copy(3)
            sp.wait_ge(toep_out, 32)
            skew = bass.AP(toep_dram.tensor, P - 1, [[HEADS * TOEP - 1, P], [TOEP, HEADS], [1, SEQ]])
            load(sp, "toep", bias, skew)
            copy(COPIES.pop(0) - 3)
            sp.wait_ge(stored["pool"], 48)
            load(sp, "diag", own, i["c_diag"])

            def window(dst, cache, b, s):
                src = cache[0, b]
                sp.dma_start(dst[:, 0:4, :], src[PAST - 512:PAST].rearrange("(p t) h d -> p t (h d)", p=P)).then_inc(s, 16)
                sp.dma_start(dst[:, 4:8, :], src.rearrange("(p t) h d -> p t (h d)", p=P)[:, 0:4, :]).then_inc(s, 16)

            b, use = place(("u", 3))
            sp.wait_ge(bank_full[b], use + 1)
            window(kwin[0], i["cache_k_win"], 0, k_in[0])
            window(vwin, i["cache_v_win"], 0, v_in)
            window(kwin[1], i["cache_k_win"], 1, k_in[1])
            copy(COPIES.pop(0))
            for b in range(1, DEC_B):
                if b + 1 < DEC_B:
                    sp.wait_ge(scored, b)
                    window(kwin[(b + 1) % 2], i["cache_k_win"], b + 1, k_in[(b + 1) % 2])
                if b in ROUND_AT:
                    slim_round(ROUND_AT[b])
                else:
                    copy(COPIES.pop(0))
                bb, use = place(("pv", b - 1))
                sp.wait_ge(bank_full[bb], use + 1)
                window(vwin, i["cache_v_win"], b, v_in)
            copy(COPIES.pop(0))
            sp.wait_ge(scored, DEC_B)

            def cache_mem(dst, name, b, s):
                sp.dma_start(dst, i[name][0, b].rearrange("(m p) h d -> p m (h d)", p=P)).then_inc(s, 16)

            for b in range(4):
                cache_mem(cmem[b], "cache_mem_k", b, ck_in[b])
            copy(COPIES.pop(0))
            slim_round(3)
            bb, use = place(("pvt", DEC_B - 1))
            sp.wait_ge(bank_full[bb], use + 1)
            for b in range(4):
                cache_mem(cmem[4 + b], "cache_mem_v", b, cv_in[b])
            for s in range(3):
                load(sp, f"braw{s}", braw[32 * s:32 * s + 32, :], i["b_gate_up"][0])
            for b in range(4, DEC_B):
                bb, use = place(("trck", b - 4, 1, 1))
                sp.wait_ge(bank_full[bb], use + 1)
                cache_mem(cmem[b - 4], "cache_mem_k", b, ck_in[b - 4])
                if b == 5:
                    copy(COPIES.pop(0))
            for b in range(4, DEC_B):
                bb, use = place(("trck", b, 1, 1))
                sp.wait_ge(bank_full[bb], use + 1)
                cache_mem(cmem[b - 4], "cache_mem_v", b, cv_in[b])
            slim_round(4)
            copy(COPIES.pop(0))
            read_out(sp, "xpt", 3)
            b, use = place(("xo_", 3))
            sp.wait_ge(bank_full[b], use + 1)
            load(sp, "xdiag", xown, i["c_xdiag"])
            load(sp, "before", before, i["c_before"])
            load(sp, "wr", wr, i["w_router"][0].rearrange("(k p) n -> p k n", p=P))
            copy(COPIES.pop(0))
            b, use = place(("pvxt", 1))
            sp.wait_ge(bank_full[b], use + 1)
            load(sp, "bdn", bdn, i["b_down"][0])
            load(sp, "brow", brow, i["b_router"])
            load(sp, "expert", expert1, i["c_expert"])

            sp.wait_ge(stored["mv"], 16)
            load(sp, "gfin", gfin, i["g_final_rows"])

            def step0():
                sp.wait_ge(wide_used, 8)
                for k in range(KC):
                    sp.dma_start(wide[:, k, :], i["w_gate_up"][0, 0, k * P:(k + 1) * P, :]).then_inc(wide_in[k], 16)
                copy(COPIES.pop(0))
                for k in range(KC):
                    sp.wait_ge(slim_used, k + 1)
                    sp.dma_start(slim[:, k, :], i["w_down"][0, 0, k * P:(k + 1) * P, :]).then_inc(slim_in[k], 16)

            def step(e, n):
                for k in range(KC):
                    sp.wait_ge(wide_used, 8 * n + k + 1)
                    sp.dma_start(wide[:, k, :], i["w_gate_up"][0, ds(e, 1), k * P:(k + 1) * P, :]
                                 .rearrange("e p n -> p (e n)")).then_inc(wide_in[k], 16)
                for k in range(KC):
                    sp.wait_ge(slim_used, 8 * n + k + 1)
                    sp.dma_start(slim[:, k, :], i["w_down"][0, ds(e, 1), k * P:(k + 1) * P, :]
                                 .rearrange("e p n -> p (e n)")).then_inc(slim_in[k], 16)

            step0()
            copy(len(pieces))
            with sp.Fori(1, EXPERTS) as e:
                step(e, e)
            sp.wait_ge(most_in, 1)
            crowd = sp.value_load(most[0:1, 0:1], min_val=0, max_val=T)
            with sp.If(crowd > CAP):
                with sp.Fori(1, ROUNDS) as j:
                    with sp.Fori(0, EXPERTS) as e:
                        step(e, j * EXPERTS + e)
            for c, t in enumerate(LAST):
                n = TOK[t][1]
                sp.wait_ge(fin, c + 1)
                dst = o["y_prompt"][0, TOK[t][0]:TOK[t][0] + n, :] if t < 2 else o["y_sample"].rearrange("b t d -> (b t) d")
                sp.dma_start(dst, xout[t][0:n, :]).then_inc(stored["y"], 16)
            sp.wait_ge(stored["y"], 48)
            sp.wait_ge(stored["copies"], 16 * 4 * DEC_B)

        @block.gpsimd
        def _(pool):
            step = [0]

            def link(ins):
                step[0] += 1
                ins.then_inc(pool_done, 1)
                pool.wait_ge(pool_done, step[0])

            nc.gpsimd.memset(ones[:, :], 1.0).then_inc(consts, 1)
            pool.dma_start(o["pool_sample"][0, :, 0:STATE - DEC_T, :], i["state_pool"][0, :, DEC_T:STATE, :]).then_inc(stored["pool"], 16)
            for h in range(HEADS):
                read_out(pool, "toep", h)
            pool.dma_start(toep_dram[:, 0:5, :], toep_sb[0]).then_inc(toep_out, 16)
            pool.dma_start(toep_dram[:, 5:8, :], toep_sb[1]).then_inc(toep_out, 16)
            for c, (kp, ks) in ((1, ("k_win_prompt", "k_win_sample")), (2, ("v_win_prompt", "v_win_sample"))):
                read_out(pool, "qkv", 0, c), read_out(pool, "qkv", 1, c), read_out(pool, "qkv", 2)
                pool.dma_start(o[kp][0, 0].rearrange("(t p) h d -> p t (h d)", p=P), qkvn[:, c, 0:2, :]).then_inc(stored["kv"], 16)
                pool.dma_start(o[ks][0, :, KEEP:PAST].rearrange("b t h d -> b t (h d)"),
                               qkvn[0:NS, c, 2, :]).then_inc(stored["kv"], 16)
            read_out(pool, "utp")
            pool.dma_start(o["pool_prompt"][0, 0], hn[0:STATE, 2, 0:512]).then_inc(stored["pool"], 16)
            read_out(pool, "uts")
            pool.dma_start(o["pool_sample"][0, :, STATE - DEC_T:STATE, :], hn[0:NS, 2, 512:1024]).then_inc(stored["pool"], 16)
            for b in range(DEC_B):
                pool.wait_ge(scored, b + 1)
                nc.gpsimd.partition_all_reduce(gm, mx, P, bass.bass_isa.ReduceOp.max).then_inc(gmax, 1)
                pool.wait_ge(zpart, b + 1)
                nc.gpsimd.partition_all_reduce(zz, zs, P, bass.bass_isa.ReduceOp.add).then_inc(zall, 1)
                if b in (3, 4):
                    if b == 3:
                        for t in range(2):
                            for h in range(2):
                                read_out(pool, "mk", t, h)
                        pool.dma_start(o["mem_k_prompt"][0, 0].rearrange("(t p) h d -> p t (h d)", p=P),
                                       hn[:, 0:2, :]).then_inc(stored["mk"], 16)
            for t in range(2):
                for h in range(2):
                    read_out(pool, "mv", t, h)
            pool.dma_start(o["mem_v_prompt"][0, 0].rearrange("(t p) h d -> p t (h d)", p=P), mv[:, :, :]).then_inc(stored["mv"], 16)
            for s in range(3):
                pool.wait_ge(loaded[f"braw{s}"], 16)
            link(nc.gpsimd.tensor_copy(parts, braw))
            for s in (1, 2):
                link(nc.gpsimd.tensor_tensor(braw[32 * s:32 * s + 32, :], braw[32 * s:32 * s + 32, :],
                                             parts[32 * s:32 * s + 32, :], ALU.subtract))
            for s in (1, 2):
                link(nc.gpsimd.tensor_copy(parts[32 * s:32 * s + 32, :], braw[32 * s:32 * s + 32, :]))
            link(nc.gpsimd.tensor_tensor(braw[64:96, :], braw[64:96, :], parts[64:96, :], ALU.subtract))
            nc.gpsimd.tensor_copy(parts[64:96, :], braw[64:96, :]).then_inc(parts_in, 1)
            pool.wait_ge(stored["kv"], 64)
            pool.wait_ge(stored["pool"], 48)
            pool.wait_ge(stored["mk"], 16)
            pool.wait_ge(stored["mv"], 16)

        @block.scalar
        def _(act):
            A = nc.scalar.activation
            step = [0]

            def link(ins):
                step[0] += 1
                ins.then_inc(act_done, 1)
                act.wait_ge(act_done, step[0])

            def root(col, n, src, junk, wait_eps=False):
                link(A(junk, src, ACT.Square, accum_out=meansq[0:n, col:col + 1]))
                A(stat[0:n, col:col + 1], meansq[0:n, col:col + 1], ACT.Sqrt, bias=eps[0:n, :], scale=1.0 / D).then_inc(squares, 1)

            act.wait_ge(consts, 2)
            for t, (t0, n) in enumerate(TOK):
                act.wait_ge(loaded[f"x{t}"], 16)
                root(t, n, x[0:n, t, :], hn[0:n, t, :])
            for t in range(2):
                for h in range(4 * t, 4 * t + 4):
                    ps, s = product(act, "toep", h)
                    A(toep_sb[h // 5][:, h % 5, :], ps[:, 0:TOEP], ACT.Copy).then_inc(s, 1)
                for c in range(3):
                    ps, s = product(act, "qkv", t, c)
                    A(qkvn[:, c, t, :], ps[:, :], ACT.Copy, scale=HD ** -0.5 if c == 0 else 1.0).then_inc(s, 1)
            ps, s = product(act, "qkv", 2)
            for c in range(3):
                ins = A(qkvn[0:NS, c, 2, :], ps[NS * c:NS * c + NS, :], ACT.Copy, scale=HD ** -0.5 if c == 0 else 1.0)
            ins.then_inc(s, 1)
            for c in range(4):
                ps, s = product(act, "u", c)
                A(uP[:, c, STATE:UP], ps[:, 0:SEQ], ACT.Copy)
                link(A(unew[:, c, :], ps[:, SEQ:T], ACT.Copy))
                A(uS[:, c, :, STATE:US], ps[:, SEQ:T].rearrange("p (b t) -> p b t", t=DEC_T), ACT.Copy).then_inc(s, 1)
            for c in range(3):
                ins = A(qrows[NS * c:NS * c + NS, :], qn[0:NS, 2, :], ACT.Copy)
            ins.then_inc(qrows_in, 1)
            for t, (t0, n) in enumerate(TOK):
                for name, dst in (("trq", qT), ("trk", kT)):
                    ps, s = product(act, name, t)
                    A(dst[:, :, t0:t0 + n], ps[:, :].rearrange("p (c n) -> p c n", n=P)[:, :, 0:n], ACT.Copy).then_inc(s, 1)
            ps, s = product(act, "state")
            A(uS[:, :, :, 0:STATE], ps[:, 0:480].rearrange("p (g b n) -> p g b n", g=4, n=STATE), ACT.Copy).then_inc(s, 1)
            ps, s = product(act, "utp")
            A(hn[0:STATE, 2, 0:512], ps[0:STATE, :], ACT.Copy).then_inc(s, 1)
            ps, s = product(act, "uts")
            A(hn[0:NS, 2, 512:1024], ps[0:NS, :], ACT.Copy).then_inc(s, 1)
            act.wait_ge(loaded["pscale"], 16)
            act.wait_ge(toep_out, 32)
            for g in range(4):
                ps, s = product(act, "pool", g)
                A(tb[:, 4 + g, :], ps[:, 0:T], ACT.Copy, scale=pscale[:, g:g + 1]).then_inc(s, 1)
            def unit_exp(u):
                nk = P * (UNITS[u][1] + 1)
                act.wait_ge(summed, 2 * u + 2)
                for h in range(2):
                    A(lg[u % 2][:, h, 0:nk], lg[u % 2][:, h, 0:nk], ACT.Exp, bias=stat[:, 8 + 4 * (u % 2) + h:9 + 4 * (u % 2) + h],
                      accum_out=stat[:, 10 + 4 * (u % 2) + h:11 + 4 * (u % 2) + h]).then_inc(expd, 1)

            def unit_pt(u):
                w = 2 * P * (UNITS[u][1] + 1)
                ps, s = product(act, "pt", u)
                A(pT[u % 2].rearrange("p c n -> p (c n)")[:, 0:w], ps[:, 0:w], ACT.Copy).then_inc(s, 1)

            def unit_out(u):
                hp, qt = UNITS[u]
                ps, s = product(act, "o", u)
                A(tb[:, hp, P * qt:P * qt + P], ps[:, 0:P], ACT.Copy).then_inc(s, 1)

            act.wait_ge(loaded["mem"], 16)
            for t in range(2):
                root(3 + t, P, hn[:, t, :], mkTf[:, 0:D] if t == 0 else mkTf[:, D:2 * D])

            def fill(name):
                kind, t, h = name
                ps, s = product(act, *name)
                if kind == "trm":
                    for c in range(4):
                        ins = A(ta[:, 4 * h + c, P * t:P * t + P], ps[:, P * c:P * c + P], ACT.Copy,
                                scale=gcol[:, 1, 4 * h + c:4 * h + c + 1])
                    ins.then_inc(s, 1)
                elif kind == "mk":
                    A(hn[:, t, 512 * h:512 * h + 512], ps[:, :], ACT.Copy).then_inc(s, 1)
                elif kind == "trmk":
                    A(mkT[:, 4 * h:4 * h + 4, P * t:P * t + P], ps[:, :].rearrange("p (c n) -> p c n", n=P), ACT.Copy).then_inc(s, 1)
                else:
                    A(mv[:, t, 512 * h:512 * h + 512], ps[:, :], ACT.Copy).then_inc(s, 1)

            def sample_exp(b):
                act.wait_ge(shifted, b + 1)
                A(pr[:, :, :, :], pp[:, :, :, :], ACT.Exp).then_inc(sexp, 1)

            def sample_out(b):
                ps, s = product(act, "pvt", b)
                c0 = SEQ + DEC_T * b
                A(tb[:, 0:4, c0:c0 + DEC_T], ps[:, 0:16].rearrange("p (c t) -> p c t", t=DEC_T), ACT.Copy).then_inc(s, 1)

            def late_rows(win, done):
                for s in range(4):
                    ins = A(win[32 * s:32 * s + 32, 8, :], win[96:128, s, :], ACT.Copy)
                ins.then_inc(done, 1)

            def late_keys(b):
                act.wait_ge(k_in[b % 2], 32 * (b // 2 + 1))
                late_rows(kwin[b % 2], late_k)

            def late_values(b):
                act.wait_ge(v_in, 32 * (b + 1))
                late_rows(vwin, late_v)

            unit_exp(0)
            late_keys(0)
            for b in range(DEC_B):
                unit_pt(b)
                if b >= 2:
                    sample_out(b - 2)
                if b:
                    sample_exp(b - 1)
                    late_values(b - 1)
                for f in FILL[b, 0]:
                    fill(f)
                unit_out(b)
                if b + 1 < DEC_B:
                    unit_exp(b + 1)
                    late_keys(b + 1)
                for f in FILL[b, 1]:
                    fill(f)
            sample_out(DEC_B - 2)
            late_values(DEC_B - 1)
            sample_exp(DEC_B - 1)
            act.wait_ge(stored["mk"], 16)
            act.wait_ge(stored["pool"], 48)
            for t, (t0, n) in enumerate(TOK):
                if t == 1:
                    sample_out(DEC_B - 1)
                for part in ([("out", t, 0), ("out", t, 1)] if t < 2 else [("out", 2)]):
                    read_out(act, *part)
                root(5 + t, n, x[0:n, t, :], hn[0:n, t, :])
            def keys_in(b):
                for m in range(2):
                    ps, s = product(act, "trck", b, m, 0)
                    A(ktm[b % 2][:, 0:4, P * m:P * m + P], ps[:, :].rearrange("p (c n) -> p c n", n=P), ACT.Copy).then_inc(s, 1)

            act.wait_ge(stored["kv"], 64)
            keys_in(0), keys_in(1)
            for c in range(8):
                ps, s = product(act, "xq", c)
                A(tb[:, c, :], ps[:, 0:T], ACT.Copy, scale=XHD ** -0.5).then_inc(s, 1)
            for b in range(2, DEC_B):
                act.wait_ge(xs_part, b - 1)
                keys_in(b)
            act.wait_ge(xmax_in, 1)
            A(px, sx_bank[:, 0:NMEM], ACT.Exp, bias=stat[:, 40:41], accum_out=stat[:, 41:42]).then_inc(xexp, 1)
            for u, (hp, qt) in enumerate(XUNITS):
                act.wait_ge(summed, 17 + u)
                ps, _ = product(act, "xs", u)
                for h in range(2):
                    ins = A(lg[u % 2][:, h, :], ps[:, 256 * h:256 * h + 256], ACT.Exp, bias=stat[:, 8 + 4 * (u % 2) + h:9 + 4 * (u % 2) + h],
                            accum_out=stat[:, 10 + 4 * (u % 2) + h:11 + 4 * (u % 2) + h])
                    if h == 0:
                        ins.then_inc(expd, 1)
                    else:
                        b_, _ = place(("xs", u))
                        ins.then_inc(bank_free[b_], 1)
                ps, s = product(act, "xpt", u)
                A(pT[u % 2].rearrange("p c n -> p (c n)"), ps[:, :], ACT.Copy).then_inc(s, 1)
                ps, s = product(act, "xo_", u)
                A(ta[:, 4 * hp:4 * hp + 4, P * qt:P * qt + P], ps[:, :].rearrange("p (c n) -> p c n", n=P), ACT.Copy).then_inc(s, 1)
            ps, s = product(act, "xpts")
            for m in range(2):
                ins = A(pxT[:, m, :, 0:16].rearrange("p b (h t) -> p b h t", t=DEC_T),
                        ps[:, P * m:P * m + P].rearrange("p (h b t) -> p b h t", b=DEC_B, t=DEC_T), ACT.Copy)
            ins.then_inc(s, 1)
            for g in range(2):
                ps, s = product(act, "pvxt", g)
                A(ta[:, :, SEQ + 16 * g:SEQ + 16 * g + 16], ps[:, 0:128].rearrange("p (c n) -> p c n", n=16), ACT.Copy).then_inc(s, 1)
            for t, (t0, n) in enumerate(TOK):
                for part in ([("xo", t, 0), ("xo", t, 1)] if t < 2 else [("xo", 2)]):
                    read_out(act, *part)
                root(16 + t, n, x[0:n, t, :], hn[0:n, t, :])
            act.wait_ge(toph, 1)
            for t, (t0, n) in enumerate(TOK):
                A(gate[0:n, t, :], top[0:n, t, 0:4], ACT.Exp, bias=stat[0:n, 20 + t:21 + t], accum_out=stat[0:n, 24 + t:25 + t]).then_inc(gexp, 1)
            ps, s = product(act, "trg")
            A(gT, ps[0:EXPERTS, 0:T], ACT.Copy).then_inc(s, 1)
            act.wait_ge(most_in, 1)
            crowd = act.value_load(most[0:1, 0:1], min_val=0, max_val=T)
            act.sem_inc(y_read, 1)

            def step_(n):
                act.wait_ge(gc_in, n + 1)
                A(sg, gc, ACT.Sigmoid, scale=1.702).then_inc(sg_in, 1)
                act.wait_ge(at_full, n + 1)
                A(aT.rearrange("p j h n -> p (j h n)"), bank_t[:, :], ACT.Copy).then_inc(at_in, 1)
                act.wait_ge(back_full, n + 1)
                A(back, bank_b[:, 0:T], ACT.Copy).then_inc(back_in, 1)
                act.wait_ge(slim_used, 8 * n + 16)
                A(ye, bank_y[:, :], ACT.Copy).then_inc(y_read, 1)

            with act.Fori(0, EXPERTS) as n:
                step_(n)
            with act.If(crowd > CAP):
                with act.Fori(1, ROUNDS) as j:
                    with act.Fori(0, EXPERTS) as e:
                        step_(j * EXPERTS + e)
            A(stat[:, 35:36], eps[:, :], ACT.Sqrt)
            for c, t in enumerate(LAST):
                n = TOK[t][1]
                act.wait_ge(xsum, c + 1)
                root(32 + t, n, x[0:n, t, :], wf[0:n, D * t:D * t + D])

        @block.vector
        def _(dve):
            V = nc.vector
            step = [0]

            def link(ins):
                step[0] += 1
                ins.then_inc(dve_done, 1)
                dve.wait_ge(dve_done, step[0])

            def inverse_root(col, n, count):
                dve.wait_ge(squares, count)
                r, v, w = stat[0:n, col:col + 1], meansq[0:n, col:col + 1], meansq[0:n, 40:41]
                V.tensor_scalar(v, v, 1.0 / D, EPS, ALU.mult, ALU.add)
                link(V.reciprocal(r, r))
                link(V.tensor_tensor(w, r, r, ALU.mult))
                link(V.tensor_tensor(w, w, v, ALU.mult))
                link(V.tensor_scalar(w, w, -0.5, 1.5, ALU.mult, ALU.add))
                link(V.tensor_tensor(r, r, w, ALU.mult))

            def norm(col, n, src, dst, count):
                inverse_root(col, n, count)
                V.tensor_scalar(dst, src, stat[0:n, col:col + 1], None, ALU.mult).then_inc(normed, 1)

            def gained(name, dst, g, tiles=(0, 1, 2)):
                for t in tiles:
                    t0, n = TOK[t]
                    for h in range(2):
                        ps, s = product(dve, name, t, h)
                        V.tensor_tensor(dst[:, 4 * h:4 * h + 4, t0:t0 + n], ps[:, :].rearrange("p (c n) -> p c n", n=P)[:, :, 0:n],
                                        gcol[:, g, 4 * h:4 * h + 4].unsqueeze(2).broadcast_to([P, 4, n]), ALU.mult).then_inc(s, 1)

            V.memset(eps[:, :], EPS).then_inc(consts, 1)
            V.memset(uP[:, :, 0:STATE], 0.0)
            V.memset(pp[:, 3, :, :], NEG)
            link(V.memset(rb[32:33, :], 1.0))
            dve.wait_ge(loaded["rel"], 16)
            V.tensor_copy(rbrep, rb.unsqueeze(2).broadcast_to([33, HEADS, P])).then_inc(rb_rep, 1)
            for t, (t0, n) in enumerate(TOK):
                norm(t, n, x[0:n, t, :], hn[0:n, t, :], t + 1)
            ps, s = product(dve, "bias_w")
            V.tensor_copy(bsw[:, :, :, :].rearrange("p k t h -> p (k t h)"), ps[:, 0:96]).then_inc(s, 1)
            ps, s = product(dve, "bias_f")
            dve.wait_ge(loaded["cfresh"], 16)
            for b in range(DEC_B):
                ins = V.tensor_tensor(bfr[:, b, :, :], ps[0:NS, 0:32].rearrange("p (t h) -> p t h", h=HEADS),
                                      fmask[:, 4 * b:4 * b + 4].unsqueeze(2).broadcast_to([NS, DEC_T, HEADS]), ALU.add)
            ins.then_inc(s, 1)
            dve.wait_ge(loaded["gcol"], 16)
            gained("tr1", ta, 0)
            dve.wait_ge(qrows_in, 1)
            for c in range(3):
                V.tensor_copy(rowsel[NS * c:NS * c + NS, :], ident[NS * c:NS * c + NS, NS * c:NS * c + NS])
            link(V.tensor_copy(qparts, qrows))
            for c in (1, 2):
                r = slice(NS * c, NS * c + NS)
                link(V.tensor_tensor(qrows[r, :], qrows[r, :], qparts[r, :], ALU.subtract))
                link(V.tensor_copy(qparts[r, :], qrows[r, :]))
            link(V.tensor_tensor(qrows[64:96, :], qrows[64:96, :], qparts[64:96, :], ALU.subtract))
            V.tensor_copy(qparts[64:96, :], qrows[64:96, :]).then_inc(qparts_in, 1)
            for h in range(2):
                ps, s = product(dve, "fresh", h)
                dst = bfr[:, :, :, :].rearrange("p b t (c h) -> p h c (b t)", h=2)[:, h]
                V.tensor_tensor(dst, dst, ps[0:NS, 0:128].rearrange("p (c q) -> p c q", q=NS), ALU.add).then_inc(s, 1)
            dve.wait_ge(loaded["cfirst"], 16)
            for c in range(4):
                read_out(dve, "u", c)
            read_out(dve, "state")
            for g, w in enumerate(POOLW):
                sp_, ss_ = uP[:, g, :], uS[:, g]
                m, turn = 1, 0
                while m < w:
                    dp, dss = sum_p[turn], sum_s[turn]
                    V.tensor_tensor(dp[:, 2 * m - 1:UP], sp_[:, 2 * m - 1:UP], sp_[:, m - 1:UP - m], ALU.add)
                    link(V.tensor_tensor(dss[:, :, 2 * m - 1:US], ss_[:, :, 2 * m - 1:US], ss_[:, :, m - 1:US - m], ALU.add))
                    sp_, ss_ = dp, dss
                    m, turn = 2 * m, 1 - turn
                V.scalar_tensor_tensor(out=dT[:, g, 0:SEQ], in0=sp_[:, STATE:UP], scalar=1.0 / w, in1=uP[:, g, STATE:UP],
                                       op0=ALU.mult, op1=ALU.subtract)
                V.scalar_tensor_tensor(out=dT[:, g, SEQ:T].rearrange("p (b t) -> p b t", t=DEC_T), in0=ss_[:, :, STATE:US], scalar=1.0 / w,
                                       in1=uS[:, g, :, STATE:US], op0=ALU.mult, op1=ALU.subtract)
                link(V.tensor_tensor(stat[:, 48:64], sp_[:, STATE:STATE + 16], cfirst[:, g, :], ALU.mult))
                link(V.tensor_tensor(dT[:, g, 0:16], stat[:, 48:64], uP[:, g, STATE:STATE + 16], ALU.subtract))
                dve.sem_inc(pooled, 1)
            dve.wait_ge(loaded["toep"], 16)

            def logits(u):
                hp, qt = UNITS[u]
                nk = P * (qt + 1)
                if u >= 2:
                    b_, use = place(("pt", u - 2))
                    dve.wait_ge(bank_full[b_], use + 1)
                for h in range(2):
                    ps, s = product(dve, "s", u, h)
                    V.tensor_tensor(lg[u % 2][:, h, 0:nk], ps[:, 0:nk], bias[:, 2 * hp + h, SEQ - nk:SEQ], ALU.add).then_inc(s, 1)
                for h in range(2):
                    read_out(dve, "s", u, h)
                    c = 8 + 4 * (u % 2) + h
                    V.tensor_reduce(stat[:, c:c + 1], lg[u % 2][:, h, 0:nk], AX.X, ALU.max, negate=True).then_inc(summed, 1)

            def share(u, n, nk):
                c = 10 + 4 * (u % 2)
                link(V.reciprocal(stat[:, c:c + 2], stat[:, c:c + 2]))
                V.tensor_tensor(lg[u % 2][:, :, 0:nk], lg[u % 2][:, :, 0:nk],
                                stat[:, c:c + 2].unsqueeze(2).broadcast_to([P, 2, nk]), ALU.mult).then_inc(scaled, 1)

            for g in range(4):
                b_, use = place(("pool", g))
                dve.wait_ge(bank_full[b_], use + 1)
            logits(0)
            for t in range(2):
                norm(3 + t, P, hn[:, t, :], hn[:, t, :], 4 + t)

            def shift(b):
                dve.wait_ge(gmax, b + 1)
                s = S_[b % 2]
                V.tensor_tensor(pp[:, 0:3, :, :].rearrange("p k t h -> p k (t h)"), s.rearrange("p k t h -> p k (t h)"),
                                gm.unsqueeze(1).broadcast_to([P, 3, 32]), ALU.subtract)
                link(V.tensor_tensor(pp[0:NS, 3, :, :].rearrange("p t h -> p (t h)"), bfr[:, b, :, :].rearrange("p t h -> p (t h)"),
                                     gm[0:NS, :], ALU.subtract))
                dve.sem_inc(shifted, 1)

            def sums(b):
                dve.wait_ge(sexp, b + 1)
                V.tensor_reduce(zs, pr[:, :, :, :].rearrange("p k t h -> p (t h) k"), AX.X, ALU.add).then_inc(zpart, 1)

            def shares(b):
                dve.wait_ge(zall, b + 1)
                link(V.reciprocal(zz, zz))
                V.tensor_tensor(pr[:, :, :, :].rearrange("p k t h -> p k (t h)"), pr[:, :, :, :].rearrange("p k t h -> p k (t h)"),
                                zz.unsqueeze(1).broadcast_to([P, 4, 32]), ALU.mult).then_inc(prob, 1)

            def keep(b):
                if b:
                    b_, use = place(("pvt", b - 1))
                    dve.wait_ge(bank_full[b_], use + 1)
                else:
                    dve.wait_ge(loaded["diag"], 16)
                ps, s = product(dve, "pv", b)
                V.tensor_tensor(kept, ps[:, :], own[:, 0:AW], ALU.mult).then_inc(s, 1)

            for b in range(DEC_B):
                dve.wait_ge(expd, 2 * b + 2)
                share(b, b + 1, P * (UNITS[b][1] + 1))
                dve.wait_ge(k_in[b % 2], 32 * (b // 2 + 1))
                dve.wait_ge(late_k, b + 1)
                kw = kwin[b % 2]
                for t in range(DEC_T):
                    ps, s = product(dve, "qb", b, t)
                    pair = kw[:, 0:8, :].rearrange("p (k s) n -> p k s n", k=2)[:, :, t, :]
                    V.tensor_tensor(prod[:, 0:2, :], pair, ps[:, :].unsqueeze(1).broadcast_to([P, 2, AW]), ALU.mult)
                    V.tensor_tensor(prod[:, 2, :], kw[:, 8, :], ps[:, :], ALU.mult).then_inc(s, 1)
                    read_out(dve, "qb", b, t)
                    link(V.tensor_reduce(S_[b % 2][:, :, t, :], prod.rearrange("p k (h d) -> p k h d", d=HD), AX.X, ALU.add))
                    if b and t < 3:
                        (shift, sums, shares)[t](b - 1)
                    if b >= 2 and t == 0:
                        keep(b - 2)
                    if t == 2 and b + 1 < DEC_B:
                        logits(b + 1)
                s = S_[b % 2]
                link(V.tensor_tensor(s, s, bsw[:, :, :, :], ALU.add))
                link(V.tensor_reduce(mx, s.rearrange("p k t h -> p (t h) k"), AX.X, ALU.max))
                V.tensor_tensor(mx[0:NS, :], mx[0:NS, :], bfr[:, b, :, :].rearrange("p t h -> p (t h)"), ALU.max).then_inc(scored, 1)
            shift(DEC_B - 1), keep(DEC_B - 2), sums(DEC_B - 1), shares(DEC_B - 1)

            def residual(name, t):
                if t < 2:
                    n = P
                    for h in range(2):
                        ps, s = product(dve, name, t, h)
                        dst = x[0:n, t, 512 * h:512 * h + 512]
                        V.tensor_tensor(dst, dst, ps[0:n, :], ALU.add).then_inc(s, 1)
                    return
                ps, s = product(dve, name, 2)
                for h in range(2):
                    dst = x[0:NS, 2, 512 * h:512 * h + 512]
                    ins = V.tensor_tensor(dst, dst, ps[NS * h:NS * h + NS, :], ALU.add)
                ins.then_inc(s, 1)

            for t, (t0, n) in enumerate(TOK):
                residual("out", t)
                if t == 0:
                    keep(DEC_B - 1)
                norm(5 + t, n, x[0:n, t, :], hn[0:n, t, :], 6 + t)
            dve.wait_ge(stored["kv"], 64)

            def keys_in(b):
                for m in range(2):
                    ps, s = product(dve, "trck", b, m, 1)
                    V.tensor_copy(ktm[b % 2][:, 4:8, P * m:P * m + P], ps[:, :].rearrange("p (c n) -> p c n", n=P)).then_inc(s, 1)

            keys_in(0), keys_in(1)
            gained("tr2", ta, 2)
            link(V.memset(qm, 0.0))
            for c in range(8):
                read_out(dve, "xq", c)
            for b in range(DEC_B):
                ins = V.tensor_copy(qm.rearrange("p (c b n) -> p c b n", c=KC, b=DEC_B)[:, :, b, DEC_T * b:DEC_T * b + DEC_T],
                                    tb[:, :, SEQ + DEC_T * b:SEQ + DEC_T * b + DEC_T])
            ins.then_inc(qm_in, 1)
            for b in range(2, DEC_B):
                dve.wait_ge(xs_part, b - 1)
                keys_in(b)
            dve.wait_ge(xs_full, 1)
            V.tensor_reduce(stat[:, 40:41], sx_bank[:, 0:NMEM], AX.X, ALU.max, negate=True).then_inc(xmax_in, 1)
            dve.wait_ge(xexp, 1)
            link(V.reciprocal(stat[:, 41:42], stat[:, 41:42]))
            V.tensor_scalar(px, px, stat[:, 41:42], None, ALU.mult).then_inc(xprob, 1)
            V.memset(pxT.rearrange("p m b n -> p (m b n)"), 0.0).then_inc(xprob, 1)
            def xmax(u):
                if u >= 2:
                    b_, use = place(("xpt", u - 2))
                    dve.wait_ge(bank_full[b_], use + 1)
                ps, _ = product(dve, "xs", u)
                c = 8 + 4 * (u % 2)
                V.tensor_reduce(stat[:, c:c + 2], ps[:, :].rearrange("p (h n) -> p h n", n=NMEM), AX.X, ALU.max, negate=True).then_inc(summed, 1)

            xmax(0)
            for u in range(4):
                if u + 1 < 4:
                    xmax(u + 1)
                read_out(dve, "xs", u)
                dve.wait_ge(expd, 17 + u)
                share(u, 9 + u, NMEM)
            dve.wait_ge(loaded["xdiag"], 16)
            for g in range(2):
                for h in range(2):
                    ps, s = product(dve, "pvx", g, h)
                    V.tensor_tensor(xkept[g][:, 512 * h:512 * h + 512], ps[:, :], xown[:, 512 * h:512 * h + 512], ALU.mult).then_inc(s, 1)

            def largest(t):
                n = TOK[t][1]
                ps, s = product(dve, "route", t)
                V.tensor_copy(logit[0:n, t, :], ps[0:n, 0:EXPERTS]).then_inc(s, 1)
                read_out(dve, "route", t)
                link(V.max(top[0:n, t, :], logit[0:n, t, :]))
                V.max_index(idx[0:n, t, :], top[0:n, t, :], logit[0:n, t, :])
                link(V.tensor_scalar(stat[0:n, 20 + t:21 + t], top[0:n, t, 0:1], -1.0, None, ALU.mult))

            for t in range(2):
                residual("xo", t)
                norm(16 + t, P, x[:, t, :], hn[:, t, :], 9 + t)
            gained("tr3", tb, 3, (0,))
            residual("xo", 2)
            gained("tr3", tb, 3, (1,))
            largest(0)
            norm(18, NS, x[0:NS, 2, :], hn[0:NS, 2, :], 11)
            gained("tr3", tb, 3, (2,))
            largest(1), largest(2)
            dve.sem_inc(toph, 1)
            dve.wait_ge(loaded["iota"], 16)
            for t, (t0, n) in enumerate(TOK):
                link(V.tensor_copy(idxf[0:n, t, :], idx[0:n, t, :]))
                for k in range(TOPK):
                    ins = V.tensor_scalar(hot[0:n, t, k, :], iota[0:n, 0:EXPERTS], idxf[0:n, t, k:k + 1], None, ALU.is_equal)
                link(ins)
                V.tensor_reduce(msk[0:n, t, :], hot[0:n, t].rearrange("p k e -> p e k"), AX.X, ALU.add).then_inc(hots, 1)
            for t, (t0, n) in enumerate(TOK):
                ps, s = product(dve, "pos", t)
                V.tensor_copy(posn[0:n, t, :], ps[0:n, 0:EXPERTS]).then_inc(s, 1)
                read_out(dve, "pos", t)
                link(V.scalar_tensor_tensor(out=table[0:n, t, 0:EXPERTS], in0=posn[0:n, t, :], scalar=FAR, in1=msk[0:n, t, :],
                                            op0=ALU.add, op1=ALU.mult))
                link(V.tensor_scalar(table[0:n, t, 0:EXPERTS], table[0:n, t, 0:EXPERTS], -FAR, None, ALU.add))
            def pair_onehot(n):
                for t, (t0, m) in enumerate(TOK):
                    for a in range(2):
                        ins = V.tensor_scalar(onehot[0:m, t, CAP * a:CAP * a + CAP], iota[0:m, 0:CAP], table[0:m, t, ds(n + a, 1)],
                                              None, ALU.is_equal)
                ins.then_inc(onehot_in, 2)

            pair_onehot(0)
            for t, (t0, n) in enumerate(TOK):
                for j in range(1, ROUNDS):
                    V.tensor_scalar(table[0:n, t, EXPERTS * j:EXPERTS * j + EXPERTS], table[0:n, t, 0:EXPERTS], -float(CAP * j), None, ALU.add)
                V.memset(table[0:n, t, STEPS:NTAB], -FAR)
            dve.wait_ge(gexp, 3)
            for t, (t0, n) in enumerate(TOK):
                link(V.reciprocal(stat[0:n, 24 + t:25 + t], stat[0:n, 24 + t:25 + t]))
                link(V.tensor_scalar(gate[0:n, t, :], gate[0:n, t, :], stat[0:n, 24 + t:25 + t], None, ALU.mult))
                link(V.tensor_tensor(prodr[0:n, t], hot[0:n, t], gate[0:n, t, :].unsqueeze(2).broadcast_to([n, TOPK, EXPERTS]), ALU.mult))
                V.tensor_reduce(gmat[0:n, t, :], prodr[0:n, t].rearrange("p k e -> p e k"), AX.X, ALU.add).then_inc(gmats, 1)
            ps, s = product(dve, "count")
            link(V.tensor_reduce(cntf, ps[0:1, 0:EXPERTS], AX.X, ALU.max))
            link(V.tensor_copy(most[:, :], cntf))
            dve.sem_inc(s, 1)
            dve.sem_inc(most_in, 1)
            crowd = dve.value_load(most[0:1, 0:1], min_val=0, max_val=T)

            def evac_xe(half, buf):
                V.tensor_tensor(xe[buf][:, 4 * half:4 * half + 4, :], bank_x[:, :].rearrange("p (k n) -> p k n", n=2 * CAP),
                                gcol[:, 3, 4 * half:4 * half + 4].unsqueeze(2).broadcast_to([P, 4, 2 * CAP]), ALU.mult).then_inc(xe_in, 1)

            dve.wait_ge(parts_in, 1)
            for half in range(2):
                dve.wait_ge(xg_full, half + 1)
                evac_xe(half, 0)
            pair_onehot(2)
            dve.sem_inc(z_read, 1)
            dve.wait_ge(loaded["expert"], 16)
            V.tensor_scalar(pick, ones[0:96, 0:CAP], expert1[:, 0:1], None, ALU.mult).then_inc(pick_in, 1)

            def add_back(n, last=False):
                dve.wait_ge(z_read, 5 * (n + 1) + 1)
                for q, (t, h) in enumerate(BACK):
                    dve.wait_ge(z_full, 5 * (n + 1) + q + 1)
                    bk = bank_z[q % 2]
                    if t < 2:
                        dst = x[:, t, 512 * h:512 * h + 512]
                        ins = V.tensor_tensor(dst, dst, bk[:, :], ALU.add)
                    else:
                        for h in range(2):
                            dst = x[0:NS, 2, 512 * h:512 * h + 512]
                            ins = V.tensor_tensor(dst, dst, bk[NS * h:NS * h + NS, :], ALU.add)
                    ins.then_inc(z_read, 1)
                    if last and q in (1, 2, 4):
                        dve.wait_ge(z_read, 5 * (n + 1) + q + 2)
                        dve.sem_inc(xsum, 1)

            def step_(n, e, i):
                for t, (t0, m) in enumerate(TOK):
                    ins = V.tensor_scalar(gated[0:m, t, :], iota[0:m, :], table[0:m, t, ds(n, 1)], gmat[0:m, t, ds(e, 1)],
                                          ALU.is_equal, ALU.mult)
                ins.then_inc(gated_in, 1)
                add_back(n - 1)
                dve.wait_ge(wide_used, 8 * n + 16)
                V.tensor_scalar(gc, bank_g[:, :], 7.0, None, ALU.min).then_inc(gc_in, 1)
                V.tensor_scalar(uc, bank_u[:, :], 7.0, -7.0, ALU.min, ALU.max).then_inc(uc_in, 1)
                dve.wait_ge(gc_in, n + 1)
                dve.wait_ge(uc_in, n + 1)
                V.scalar_tensor_tensor(out=gu, in0=uc, scalar=1.0, in1=gc, op0=ALU.add, op1=ALU.mult).then_inc(gu_in, 1)
                dve.wait_ge(gu_in, n + 1)
                dve.wait_ge(sg_in, n + 1)
                V.tensor_tensor(gu, gu, sg, ALU.mult).then_inc(a_in, 1)
                V.tensor_scalar(pick, ones[0:96, 0:CAP], expert1[:, ds(n + 1, 1)], None, ALU.mult).then_inc(pick_in, 1)
                dve.wait_ge(xg_full, n + 3)
                evac_xe(i % 2, 1 - i // 2)
                if i % 2:
                    pair_onehot(n + 3)

            with dve.Fori(0, EXPERTS // LOT) as m:
                for i in range(LOT):
                    step_(m * LOT + i, m * LOT + i, i)
            with dve.If(crowd > CAP):
                with dve.Fori(1, ROUNDS) as j:
                    with dve.Fori(0, EXPERTS // LOT) as m:
                        for i in range(LOT):
                            step_(j * EXPERTS + m * LOT + i, m * LOT + i, i)
                add_back(STEPS - 1, last=True)
            with dve.Else():
                add_back(EXPERTS - 1, last=True)
            dve.wait_ge(loaded["gfin"], 16)
            for c, t in enumerate(LAST):
                n = TOK[t][1]
                inverse_root(32 + t, n, 12 + c)
                V.scalar_tensor_tensor(out=xout[t][0:n, :], in0=x[0:n, t, :], scalar=stat[0:n, 32 + t:33 + t], in1=gfin[0:n, :],
                                       op0=ALU.mult, op1=ALU.mult).then_inc(fin, 1)

        @block.tensor
        def _(pe):
            M = nc.tensor.matmul
            TR = nc.tensor.transpose

            pe.wait_ge(loaded["cbias"], 16)
            pe.wait_ge(rb_rep, 1)
            cw = [cb[:, TOEP + P * s:TOEP + P * s + P] for s in range(6)]
            ps, s = take(pe, "bias_w")
            for kind in range(3):
                for t in range(DEC_T):
                    c = 32 * kind + 8 * t
                    ins = M(ps[:, c:c + 8], cw[kind if kind < 2 else 2 + t], rb, start=True, stop=True)
            ins.then_inc(s, 1)
            ps, s = take(pe, "bias_f")
            for t in range(DEC_T):
                c = TOEP + 6 * P + NS * t
                ins = M(ps[0:NS, 8 * t:8 * t + 8], cb[:, c:c + NS], rb, start=True, stop=True)
            ins.then_inc(s, 1)
            def transposes(name, count, tiles=(0, 1, 2)):
                for t in tiles:
                    t0, n = TOK[t]
                    pe.wait_ge(normed, count + t)
                    for h in range(2):
                        ps, s = take(pe, name, t, h)
                        for c in range(4):
                            ins = TR(ps[:, P * c:P * c + n], hn[0:n, t, 512 * h + P * c:512 * h + P * c + P], ident[0:n, 0:n])
                        ins.then_inc(s, 1)

            pe.wait_ge(loaded["ident"], 16)
            transposes("tr1", 1)
            for t in range(2):
                read_out(pe, "tr1", t, 0), read_out(pe, "tr1", t, 1)
                tk = [take(pe, "qkv", t, c) for c in range(3)]
                for k in range(KC):
                    if t == 0:
                        pe.wait_ge(wide_in[k], 16)
                    for c in range(3):
                        ins = M(tk[c][0][:, :], ta[:, k, P * t:P * t + P], wide[:, k, 512 * c:512 * c + 512], start=k == 0, stop=k == KC - 1)
                        if k == KC - 1:
                            ins.then_inc(tk[c][1], 1)
                    if k < 4:
                        ps, s = take(pe, "toep", 4 * t + k)
                        M(ps[:, 0:TOEP], rbrep[:, 4 * t + k, :], cb[:, 0:TOEP], start=True, stop=True).then_inc(s, 1)
            read_out(pe, "tr1", 2, 0), read_out(pe, "tr1", 2, 1)
            ps, s = take(pe, "qkv", 2)
            for k in range(KC):
                for c in range(3):
                    ins = M(ps[NS * c:NS * c + NS, :], ta[:, k, SEQ:T], wide[:, k, 512 * c:512 * c + 512], start=k == 0, stop=k == KC - 1)
            ins.then_inc(s, 1)
            for c in range(4):
                ps, s = take(pe, "u", c)
                for k in range(KC):
                    ins = M(ps[:, 0:T], wide[:, k, 1536 + P * c:1536 + P * c + P], ta[:, k, :], start=k == 0, stop=k == KC - 1)
                ins.then_inc(s, 1)
            for t, (t0, n) in enumerate(TOK):
                for ci, name, src in ((0, "trq", qn), (1, "trk", kn)):
                    read_out(pe, *(("qkv", t, ci) if t < 2 else ("qkv", 2)))
                    ps, s = take(pe, name, t)
                    for c in range(4):
                        ins = TR(ps[:, P * c:P * c + n], src[0:n, t, P * c:P * c + P], ident[0:n, 0:n])
                    ins.then_inc(s, 1)
            for h in range(2):
                read_out(pe, "trq", 2), read_out(pe, "trk", 2)
                ps, s = take(pe, "fresh", h)
                for c in range(4):
                    ins = M(ps[0:NS, NS * c:NS * c + NS], kT[64 * h:64 * h + 64, c, SEQ:T], qT[64 * h:64 * h + 64, c, SEQ:T], start=True, stop=True)
                ins.then_inc(s, 1)
            pe.wait_ge(loaded["state"], 16)
            ps, s = take(pe, "state")
            ns = DEC_B * STATE
            for c in range(4):
                ins = TR(ps[:, ns * c:ns * c + ns], state[:, P * c:P * c + P], ident[0:ns, 0:ns])
            ins.then_inc(s, 1)
            for c in range(4):
                read_out(pe, "u", c)
            ps, s = take(pe, "utp")
            for c in range(4):
                ins = TR(ps[0:STATE, P * c:P * c + P], uP[:, c, UP - STATE:UP], ident[:, :])
            ins.then_inc(s, 1)
            ps, s = take(pe, "uts")
            for c in range(4):
                ins = TR(ps[0:NS, P * c:P * c + P], unew[:, c, :], ident[:, :])
            ins.then_inc(s, 1)
            pe.wait_ge(loaded["wpool"], 16)
            for g in range(4):
                pe.wait_ge(pooled, g + 1)
                ps, s = take(pe, "pool", g)
                M(ps[:, 0:T], wpool[:, g, :], dT[:, g, :], start=True, stop=True).then_inc(s, 1)

            def scores(u):
                hp, qt = UNITS[u]
                nk = P * (qt + 1)
                for h in range(2):
                    ps, s = take(pe, "s", u, h)
                    r = slice(64 * h, 64 * h + 64)
                    M(ps[:, 0:nk], qT[r, hp, P * qt:P * qt + P], kT[r, hp, 0:nk], start=True, stop=True).then_inc(s, 1)

            for t in range(2):
                read_out(pe, "trq", t), read_out(pe, "trk", t)
            scores(0)

            def turned(u):
                hp, qt = UNITS[u]
                pe.wait_ge(scaled, u + 1)
                ps, s = take(pe, "pt", u)
                for h in range(2):
                    for c in range(qt + 1):
                        z = P * ((qt + 1) * h + c)
                        ins = TR(ps[:, z:z + P], lg[u % 2][:, h, P * c:P * c + P], ident[:, :])
                ins.then_inc(s, 1)

            def unit_values(u):
                hp, qt = UNITS[u]
                read_out(pe, "pt", u)
                ps, s = take(pe, "o", u)
                for h in range(2):
                    for c in range(qt + 1):
                        hd = 64 * (2 * hp + h)
                        ins = M(ps[64 * h:64 * h + 64, 0:P], vn[:, c, hd:hd + 64], pT[u % 2][:, (qt + 1) * h + c, :], start=c == 0, stop=c == qt)
                ins.then_inc(s, 1)

            def rows_times(name, t, left, n, t0):
                if name in ("out", "xo") and t == 2:
                    ps, s = take(pe, name, 2)
                    for k in range(KC):
                        for h in range(2):
                            ins = M(ps[NS * h:NS * h + NS, :], left[:, k, SEQ:T], slim[:, k, 512 * h:512 * h + 512], start=k == 0, stop=k == KC - 1)
                        if k < KC - 1:
                            ins.then_inc(out_used if name == "out" else slim_used, 1)
                    ins.then_inc(s, 1)
                    b_, use = place((name, 2))
                    pe.wait_ge(bank_full[b_], use + 1)
                    pe.sem_inc(out_used if name == "out" else slim_used, 1)
                    return
                tk = [take(pe, name, t, h) for h in range(2)]
                for k in range(KC):
                    if t == 0:
                        pe.wait_ge(slim_in[k], 16 * (SLIM.index({"out": "w_out", "xo": "w_xo"}[name]) + 1))
                    for h in range(2):
                        ins = M(tk[h][0][0:n, :], left[:, k, t0:t0 + n], slim[:, k, 512 * h:512 * h + 512], start=k == 0, stop=k == KC - 1)
                        if k == KC - 1:
                            ins.then_inc(tk[h][1], 1)


            def fill(name):
                kind, t, h = name
                if kind == "trm":
                    pe.wait_ge(normed, 4 + t)
                    ps, s = take(pe, *name)
                    for c in range(4):
                        ins = TR(ps[:, P * c:P * c + P], hn[:, t, 512 * h + P * c:512 * h + P * c + P], ident[:, :])
                    ins.then_inc(s, 1)
                elif kind in ("mk", "mv"):
                    if h == 0:
                        read_out(pe, "trm", t, 0), read_out(pe, "trm", t, 1)
                    ps, s = take(pe, *name)
                    for k in range(KC):
                        if t == 0 and h == 0:
                            pe.wait_ge(slim_in[k], 16 if kind == "mk" else 32)
                        ins = M(ps[:, :], ta[:, k, P * t:P * t + P], slim[:, k, 512 * h:512 * h + 512], start=k == 0, stop=k == KC - 1)
                    ins.then_inc(s, 1)
                else:
                    read_out(pe, "mk", t, h)
                    ps, s = take(pe, *name)
                    for c in range(4):
                        ins = TR(ps[:, P * c:P * c + P], hn[:, t, 512 * h + P * c:512 * h + P * c + P], ident[:, :])
                    ins.then_inc(s, 1)

            def values(b):
                pe.wait_ge(prob, b + 1)
                pe.wait_ge(v_in, 32 * (b + 1))
                pe.wait_ge(late_v, b + 1)
                ps, s = take(pe, "pv", b)
                flat = pr[:, :, :, :].rearrange("p k t h -> p k (t h)")
                for k, kind in enumerate((2, 0, 1, 3)):
                    for t in range(DEC_T):
                        g = slice(32 * t, 32 * t + 32)
                        if kind == 3:
                            ins = M(ps[g, :], flat[0:NS, 3, :], vn[0:NS, 2, :], start=False, stop=True, tile_position=(0, 32 * t))
                        else:
                            ins = M(ps[g, :], flat[:, kind, :], vwin[:, 8 if kind == 2 else 4 * kind + t, :], start=k == 0, stop=False)
                ins.then_inc(s, 1)

            def turn_values(b):
                read_out(pe, "pv", b)
                ps, s = take(pe, "pvt", b)
                for c in range(4):
                    ins = M(ps[:, 4 * c:4 * c + 4], kept[:, P * c:P * c + P], own[:, AW:AW + DEC_T], start=True, stop=True)
                ins.then_inc(s, 1)

            def row(b, t):
                ps, s = take(pe, "qb", b, t)
                r = DEC_T * b + t
                M(ps[:, :], rowsel[:, r:r + 1].broadcast_to([96, P]), qparts, start=True, stop=True).then_inc(s, 1)

            pe.wait_ge(qparts_in, 1)
            row(0, 0), row(0, 1)
            for b in range(DEC_B):
                row(b, 2)
                turned(b)
                if b >= 2:
                    turn_values(b - 2)
                for f in FILL[b, 0]:
                    fill(f)
                row(b, 3)
                unit_values(b)
                if b + 1 < DEC_B:
                    scores(b + 1)
                if b + 1 < DEC_B:
                    row(b + 1, 0), row(b + 1, 1)
                if b:
                    values(b - 1)
                for f in FILL[b, 1]:
                    fill(f)
            turn_values(DEC_B - 2)
            read_out(pe, "o", DEC_B - 1)
            rows_times("out", 0, tb, P, 0)
            values(DEC_B - 1)
            rows_times("out", 1, tb, P, P)
            turn_values(DEC_B - 1)
            read_out(pe, "pvt", DEC_B - 1)
            rows_times("out", 2, tb, NS, SEQ)

            def turn_keys(b):
                pe.wait_ge(ck_in[b % 4], 16 * (b // 4 + 1))
                for m in range(2):
                    for h in range(2):
                        ps, s = take(pe, "trck", b, m, h)
                        for c in range(4):
                            ins = TR(ps[:, P * c:P * c + P], cmem[b % 4][:, m, 512 * h + P * c:512 * h + P * c + P], ident[:, :])
                        ins.then_inc(s, 1)

            turn_keys(0), turn_keys(1)
            transposes("tr2", 6)
            for t in range(3):
                read_out(pe, "tr2", t, 0), read_out(pe, "tr2", t, 1)
            for c in range(8):
                ps, s = take(pe, "xq", c)
                for k in range(KC):
                    if c == 0:
                        pe.wait_ge(slim_in[k], 64)
                    ins = M(ps[:, 0:T], slim[:, k, P * c:P * c + P], ta[:, k, :], start=k == 0, stop=k == KC - 1)
                ins.then_inc(s, 1)

            def cross_scores(b):
                for m in range(2):
                    read_out(pe, "trck", b, m, 0), read_out(pe, "trck", b, m, 1)
                for c in range(2):
                    for h in range(XH):
                        q0 = 256 * (2 * h + c) + 32 * b
                        ins = M(sx_bank[32 * h:32 * h + 32, 0:NMEM], qm[:, q0:q0 + 32], ktm[b % 2][:, 2 * h + c, :],
                                start=b == 0 and c == 0, stop=b == DEC_B - 1 and c == 1)
                ins.then_inc(xs_full if b == DEC_B - 1 else xs_part, 1)

            pe.wait_ge(qm_in, 1)
            cross_scores(0)
            for b in range(2, DEC_B):
                turn_keys(b)
                cross_scores(b - 1)
            cross_scores(DEC_B - 1)

            def xscores(u):
                hp, qt = XUNITS[u]
                ps, s = take(pe, "xs", u)
                for h in range(2):
                    for c in range(2):
                        k = 2 * (2 * hp + h) + c
                        ins = M(ps[:, 256 * h:256 * h + 256], tb[:, k, P * qt:P * qt + P], mkT[:, k, :], start=c == 0, stop=c == 1)
                ins.then_inc(s, 1)

            xscores(0)
            for u, (hp, qt) in enumerate(XUNITS):
                if u + 1 < 4:
                    xscores(u + 1)
                pe.wait_ge(scaled, 9 + u)
                ps, s = take(pe, "xpt", u)
                for h in range(2):
                    for c in range(2):
                        z = P * (2 * h + c)
                        ins = TR(ps[:, z:z + P], lg[u % 2][:, h, P * c:P * c + P], ident[:, :])
                ins.then_inc(s, 1)
                read_out(pe, "xpt", u)
                ps, s = take(pe, "xo_", u)
                for h in range(2):
                    for c in range(2):
                        z = P * (2 * h + c)
                        hd = XHD * (2 * hp + h) + P * c
                        for m in range(2):
                            ins = M(ps[:, z:z + P], mv[:, m, hd:hd + P], pT[u % 2][:, 2 * h + m, :], start=m == 0, stop=m == 1)
                ins.then_inc(s, 1)
            pe.wait_ge(xprob, 2)
            ps, s = take(pe, "xpts")
            for m in range(2):
                ins = TR(ps[:, P * m:P * m + P], px[:, P * m:P * m + P], ident[:, :])
            ins.then_inc(s, 1)
            read_out(pe, "xpts")
            for g in range(2):
                tk = [take(pe, "pvx", g, h) for h in range(2)]
                for h in range(2):
                    for m in range(2):
                        for r in range(4):
                            b = 4 * g + r
                            if h == 0 and m == 0:
                                pe.wait_ge(cv_in[b], 16)
                            v = cmem[4 + b if b < 4 else b - 4]
                            ins = M(tk[h][0][32 * r:32 * r + 32, :], pxT[:, m, b, :], v[:, m, 512 * h:512 * h + 512], start=m == 0, stop=m == 1)
                    ins.then_inc(tk[h][1], 1)
            pe.wait_ge(loaded["xdiag"], 16)
            for g in range(2):
                read_out(pe, "pvx", g, 0), read_out(pe, "pvx", g, 1)
                ps, s = take(pe, "pvxt", g)
                for c in range(KC):
                    ins = M(ps[:, 16 * c:16 * c + 16], xkept[g][:, P * c:P * c + P], xown[:, D:D + 16], start=True, stop=True)
                ins.then_inc(s, 1)
            b_, use = place(("pvxt", 1))
            pe.wait_ge(bank_full[b_], use + 1)
            pe.sem_inc(wide_used, 8)
            read_out(pe, "pvxt", 1)
            for u in range(4):
                read_out(pe, "xo_", u)

            def route(t):
                t0, n = TOK[t]
                read_out(pe, "tr3", t, 0), read_out(pe, "tr3", t, 1)
                ps, s = take(pe, "route", t)
                for k in range(KC):
                    M(ps[0:n, 0:EXPERTS], tb[:, k, t0:t0 + n], wr[:, k, :], start=k == 0, stop=False)
                M(ps[0:n, 0:EXPERTS], ones[0:1, 0:n], brow, start=False, stop=True).then_inc(s, 1)

            rows_times("xo", 0, ta, P, 0), rows_times("xo", 1, ta, P, P)
            transposes("tr3", 9, (0,))
            rows_times("xo", 2, ta, NS, SEQ)
            transposes("tr3", 9, (1,))
            pe.wait_ge(loaded["wr"], 16)
            pe.wait_ge(loaded["brow"], 16)
            route(0)
            transposes("tr3", 9, (2,))
            route(1), route(2)
            pe.wait_ge(loaded["before"], 16)
            for t, (t0, n) in enumerate(TOK):
                pe.wait_ge(hots, t + 1)
                ps, s = take(pe, "pos", t)
                for t_ in range(t):
                    M(ps[0:n, 0:EXPERTS], ones[:, 0:n], msk[:, t_, :], start=t_ == 0, stop=False)
                M(ps[0:n, 0:EXPERTS], before[0:n, 0:n], msk[0:n, t, :], start=t == 0, stop=True).then_inc(s, 1)
            ps, s = take(pe, "count")
            for t, (t0, n) in enumerate(TOK):
                ins = M(ps[0:1, 0:EXPERTS], ones[0:n, 0:1], msk[0:n, t, :], start=t == 0, stop=t == 2)
            ins.then_inc(s, 1)
            def gather(n, half):
                for k in range(4 * half, 4 * half + 4):
                    c = 2 * CAP * (k % 4)
                    for t, (t0, m) in enumerate(TOK):
                        ins = M(bank_x[:, c:c + 2 * CAP], hn[0:m, t, P * k:P * k + P], onehot[0:m, t, :], start=t == 0, stop=t == 2)
                ins.then_inc(xg_full, 1)

            pe.wait_ge(onehot_in, 2)
            gather(0, 0)
            pe.wait_ge(gmats, 3)
            ps, s = take(pe, "trg")
            for t, (t0, n) in enumerate(TOK):
                ins = TR(ps[0:EXPERTS, t0:t0 + n], gmat[0:n, t, :], ident[0:n, 0:n])
            ins.then_inc(s, 1)
            pe.wait_ge(xe_in, 1)
            gather(0, 1)
            pe.wait_ge(most_in, 1)
            crowd = pe.value_load(most[0:1, 0:1], min_val=0, max_val=T)
            for name in jobs[-TURN:]:
                read_out(pe, *name)

            pe.wait_ge(parts_in, 1)
            half = [slice(0, CAP), slice(CAP, 2 * CAP)]

            def give_back(n, q, first=False):
                t, h = BACK[q]
                t0, m = TOK[t]
                if q == 0 and first:
                    read_out(pe, "trg")
                    pe.wait_ge(loaded["bdn"], 16)
                elif q == 0:
                    pe.wait_ge(back_in, n + 1)
                    pe.wait_ge(y_read, n + 2)
                if q != 1:
                    pe.wait_ge(z_read, 5 * (n + 1) + max(q, 1))
                for h in ([h] if t < 2 else range(2)):
                    out = bank_z[q % 2][:, :] if t < 2 else bank_z[q % 2][NS * h:NS * h + NS, :]
                    if first:
                        ins = M(out, gT[:, t0:t0 + m], bdn[:, 512 * h:512 * h + 512], start=True, stop=True)
                    else:
                        ins = M(out, back[half[h], t0:t0 + m], ye[half[h], :], start=True, stop=True)
                ins.then_inc(z_full, 1)

            def step_(n, i, first=False):
                pe.wait_ge(pick_in, n + 1)
                for q, bk in enumerate((bank_g, bank_u)):
                    for h in range(2):
                        c = D * q + 512 * h
                        M(bk[half[h], :], pick, parts[:, c:c + 512], start=True, stop=False)
                pe.wait_ge(xe_in, n + 2)
                rows = xe[i // 2][:, :, CAP * (i % 2):CAP * (i % 2) + CAP]
                for k in range(KC):
                    pe.wait_ge(wide_in[k], 16 * n + 32)
                    for q, bk in enumerate((bank_g, bank_u)):
                        for h in range(2):
                            c = D * q + 512 * h
                            ins = M(bk[half[h], :], rows[:, k, :], wide[:, k, c:c + 512], start=False, stop=k == KC - 1)
                    ins.then_inc(wide_used, 1)
                    if k in range(1, 6):
                        give_back(n - 1, k - 1, first)
                pe.wait_ge(gated_in, n + 1)
                for t, (t0, m) in enumerate(TOK):
                    ins = TR(bank_b[:, t0:t0 + m], gated[0:m, t, :], ident[0:m, 0:m])
                ins.then_inc(back_full, 1)
                if i % 2 == 0:
                    pe.wait_ge(onehot_in, n + 4)
                gather(n + 2, i % 2)
                pe.wait_ge(a_in, n + 1)
                for j in range(4):
                    ins = TR(bank_t[:, P * j:P * j + P], gu[:, P * j:P * j + P], ident[:, :])
                ins.then_inc(at_full, 1)
                pe.wait_ge(at_in, n + 1)
                pe.wait_ge(y_read, n + 1)
                for f in range(KC):
                    pe.wait_ge(slim_in[f], 16 * n + 96)
                    for h in range(2):
                        ins = M(bank_y[half[h], :], aT[:, f % 4, f // 4, :], slim[:, f, 512 * h:512 * h + 512], start=f == 0, stop=f == KC - 1)
                    ins.then_inc(slim_used, 1)

            for i in range(LOT):
                step_(i, i, first=i == 0)
            with pe.Fori(1, EXPERTS // LOT) as m:
                for i in range(LOT):
                    step_(m * LOT + i, i)
            with pe.If(crowd > CAP):
                with pe.Fori(1, ROUNDS) as j:
                    with pe.Fori(0, EXPERTS // LOT) as m:
                        for i in range(LOT):
                            step_(j * EXPERTS + m * LOT + i, i)
                for q in range(5):
                    give_back(STEPS - 1, q)
            with pe.Else():
                for q in range(5):
                    give_back(EXPERTS - 1, q)


_OUTS = [
    ("y_prompt", (1, SEQ, D)), ("y_sample", (DEC_B, DEC_T, D)),
    ("k_win_prompt", (1, 1, SEQ, HEADS, HD)), ("v_win_prompt", (1, 1, SEQ, HEADS, HD)),
    ("pool_prompt", (1, 1, STATE, AW)),
    ("mem_k_prompt", (1, 1, NMEM, XH, XHD)), ("mem_v_prompt", (1, 1, NMEM, XH, XHD)),
    ("k_win_sample", (1, DEC_B, PAST, HEADS, HD)), ("v_win_sample", (1, DEC_B, PAST, HEADS, HD)),
    ("pool_sample", (1, DEC_B, STATE, AW)),
]
_PLAIN = ["x_prompt", "x_sample", "cache_k_win", "cache_v_win", "state_pool", "cache_mem_k", "cache_mem_v",
          "mem_prompt", "rel_bias", "w_in", "w_pool", "w_out", "w_xq", "w_xk", "w_xv", "w_xo", "w_router",
          "b_router", "w_gate_up", "b_gate_up", "w_down", "b_down"]


def kernel(**inputs):
    import numpy as _np
    import concourse.bacc as _bacc
    from concourse import mybir as _mybir
    from concourse.bass_utils import run_bass_kernel_spmd as _run

    nc = _bacc.Bacc("TRN2", target_bir_lowering=False, num_devices=1)
    arrays = {n: _np.ascontiguousarray(inputs[n]) for n in _PLAIN}
    cols = [_np.asarray(inputs[n])[0].reshape(KC, P).T for n in ("g_mix", "g_mem", "g_x", "g_ff")]
    arrays["g_all"] = _np.ascontiguousarray(_np.stack(cols, 1))
    arrays["pool_scale_col"] = _np.ascontiguousarray(_np.asarray(inputs["pool_scale"])[0].reshape(4, P).T)
    arrays["g_final_rows"] = _np.ascontiguousarray(_np.broadcast_to(_np.asarray(inputs["g_final"]), (P, D)))
    arrays.update(constants())
    ins = {n: nc.dram_tensor(f"in_{n}", a.shape, _mybir.dt.from_np(a.dtype), kind="ExternalInput").ap() for n, a in arrays.items()}
    outs = {n: nc.dram_tensor(f"out_{n}", shape, _mybir.dt.float32, kind="ExternalOutput").ap() for n, shape in _OUTS}
    build(nc, ins, outs)
    r = _run(nc, [{f"in_{n}": a for n, a in arrays.items()}], core_ids=[0])
    return tuple(r.results[0][f"out_{n}"] for n, _ in _OUTS)
```
